# Optimizing a Trainium2 kernel written in Bass

```python
import math
import jax
import jax.numpy as jnp
from jax import lax
import numpy as np

D_MODEL = 1024
BATCH = 1
SEQ = 1024
DEPTH = 1

N_BRANCHES = 4
BRANCH_WIDTH = D_MODEL // 4
RMS_EPS = 1e-6
CONV_WIDTH = 4

GLA_HEADS = 4
GLA_DV = BRANCH_WIDTH // GLA_HEADS
GLA_DK = GLA_DV // 2
GLA_RANK = 16
GLA_GATE_NORM = 16.0
GLA_CHUNK = 64
GLA_QK_W = GLA_HEADS * GLA_DK
GLA_V_W = GLA_HEADS * GLA_DV

LRU_WIDTH = BRANCH_WIDTH
LRU_BLOCKS = 4
LRU_C = 8.0

DIFF_HEADS = 4
DIFF_DV = BRANCH_WIDTH // DIFF_HEADS
DIFF_DH = DIFF_DV // 2
DIFF_QK_W = DIFF_HEADS * 2 * DIFF_DH
DIFF_V_W = DIFF_HEADS * DIFF_DV
Q_BLOCK = 128

GDN_HEADS = 4
GDN_DK = BRANCH_WIDTH // GDN_HEADS
GDN_DV = BRANCH_WIDTH // GDN_HEADS
GDN_CHUNK = 64
GDN_QK_W = GDN_HEADS * GDN_DK
GDN_V_W = GDN_HEADS * GDN_DV

IN_SPLITS = (GLA_QK_W, GLA_QK_W, GLA_V_W, GLA_V_W, 2 * GLA_RANK,
             LRU_WIDTH, LRU_WIDTH,
             DIFF_QK_W, DIFF_QK_W, DIFF_V_W,
             2 * GDN_QK_W + GDN_V_W, GDN_V_W, 4 * GDN_HEADS)
D_IN = sum(IN_SPLITS)

MEM_LEN = 256
XATTN_HEADS = 4
XATTN_DH = D_MODEL // XATTN_HEADS

N_GROUPS = 4
EXPERTS_PER_GROUP = 8
N_EXPERTS = N_GROUPS * EXPERTS_PER_GROUP
TOP_K = 2
D_EXPERT = D_MODEL // 2
MOE_BLOCK = 128

kernel_name = 'hybrid_bidir_gla_rglru_diffattn_gdn_hmoe'

def rmsnorm(x, g):
    xf = x.astype(jnp.float32)
    y = xf * lax.rsqrt(jnp.mean(xf * xf, axis=-1, keepdims=True) + RMS_EPS)
    return (y * g.astype(jnp.float32)).astype(x.dtype)

def l2norm(t):
    return t * lax.rsqrt(jnp.sum(t * t, axis=-1, keepdims=True) + 1e-6)

def _flip(t):
    return jnp.flip(t, axis=1)

def alibi_slopes(n):
    return jnp.exp2(-8.0 * jnp.arange(1, n + 1, dtype=jnp.float32) / n)

def dwconv_centred(x, w):
    k = w.shape[0]
    return lax.conv_general_dilated(
        x, w[:, None, :].astype(x.dtype), window_strides=(1,),
        padding=[(k // 2, k - 1 - k // 2)],
        dimension_numbers=('NWC', 'WIO', 'NWC'),
        feature_group_count=x.shape[-1])

def _to_chunks(t, chunk):
    b, s, h = t.shape[:3]
    t = t.reshape((b, s // chunk, chunk, h) + t.shape[3:])
    return jnp.moveaxis(t, 3, 1)

def _from_chunks(o):
    nc, b, h, c, d = o.shape
    return o.transpose(1, 0, 3, 2, 4).reshape(b, nc * c, h, d)

def _linrec_combine(c1, c2):
    a1, b1 = c1
    a2, b2 = c2
    return a1 * a2, a2 * b1 + b2

def gla_scan(q, k, v, log_f):
    b_, s_, h_, dk = q.shape
    dv = v.shape[-1]
    c = GLA_CHUNK
    incl = jnp.tril(jnp.ones((c, c), dtype=bool))[:, :, None]

    def step(state, inp):
        q_i, k_i, v_i, g_i = inp
        bcum = jnp.cumsum(g_i, axis=2)
        decay = jnp.exp(jnp.where(incl, bcum[:, :, :, None, :] - bcum[:, :, None, :, :], -jnp.inf))
        scores = jnp.einsum('bhtd,bhsd,bhtsd->bhts', q_i, k_i, decay)
        o = (jnp.einsum('bhts,bhse->bhte', scores, v_i)
             + jnp.einsum('bhtd,bhde->bhte', q_i * jnp.exp(bcum), state))
        b_end = bcum[:, :, -1:, :]
        state = (jnp.exp(b_end)[:, :, 0, :, None] * state
                 + jnp.einsum('bhsd,bhse->bhde', k_i * jnp.exp(b_end - bcum), v_i))
        return state, o

    xs = tuple(jnp.moveaxis(_to_chunks(t, c), 2, 0) for t in (q, k, v, log_f))
    _, o = lax.scan(step, jnp.zeros((b_, h_, dk, dv), jnp.float32), xs)
    return _from_chunks(o)

def gla_mixer(q, k, v, og, lr, lr_up, lr_bias, norm_g):
    B, S, _ = q.shape
    f32 = jnp.float32
    qh = q.astype(f32).reshape(B, S, GLA_HEADS, GLA_DK) * GLA_DK ** -0.5
    kh = k.astype(f32).reshape(B, S, GLA_HEADS, GLA_DK)
    vh = v.astype(f32).reshape(B, S, GLA_HEADS, GLA_DV)
    lr = lr.astype(f32).reshape(B, S, 2, GLA_RANK)
    z = jnp.einsum('bsdr,drk->bsdk', lr, lr_up.astype(f32)) + lr_bias.astype(f32)
    log_f = (jax.nn.log_sigmoid(z) / GLA_GATE_NORM).reshape(B, S, 2, GLA_HEADS, GLA_DK)
    o_f = gla_scan(qh, kh, vh, log_f[:, :, 0])
    o_b = _flip(gla_scan(_flip(qh), _flip(kh), _flip(vh), _flip(log_f[:, :, 1])))
    o = rmsnorm(o_f + o_b, norm_g) * jax.nn.silu(og.astype(f32)).reshape(B, S, GLA_HEADS, GLA_DV)
    return o.reshape(B, S, GLA_V_W).astype(q.dtype)

def rglru_mixer(xb, gb, conv_w, conv_b, w_a, b_a, w_x, b_x, lam):
    B, S, W = xb.shape
    f32 = jnp.float32
    u = (dwconv_centred(xb, conv_w) + conv_b).astype(f32)
    ub = u.reshape(B, S, LRU_BLOCKS, W // LRU_BLOCKS)

    def gate(w, b):
        return jax.nn.sigmoid(jnp.einsum('bsni,nio->bsno', ub, w.astype(f32)).reshape(B, S, W) + b.astype(f32))

    def direction(d, reverse):
        r = gate(w_a[d], b_a[d])
        i = gate(w_x[d], b_x[d])
        log_a = -LRU_C * r * jax.nn.softplus(-lam[d].astype(f32))
        a = jnp.exp(log_a)
        xin = jnp.sqrt(-jnp.expm1(2.0 * log_a)) * (i * u)
        _, hs = lax.associative_scan(_linrec_combine, (a, xin), axis=1, reverse=reverse)
        return hs

    hsum = direction(0, False) + direction(1, True)
    return (hsum * jax.nn.gelu(gb.astype(f32))).astype(xb.dtype)

def diff_attention(q, k, v, lq1, lk1, lq2, lk2, norm_g, lambda_init):
    B, S, _ = q.shape
    f32 = jnp.float32
    nb = S // Q_BLOCK
    qh = (q.astype(f32).reshape(B, nb, Q_BLOCK, DIFF_HEADS, 2, DIFF_DH)
          .transpose(1, 0, 3, 4, 2, 5) * DIFF_DH ** -0.5)
    kt = k.astype(f32).reshape(B, S, DIFF_HEADS, 2, DIFF_DH).transpose(0, 2, 3, 1, 4)
    vt = v.astype(f32).reshape(B, S, DIFF_HEADS, DIFF_DV).transpose(0, 2, 1, 3)
    lam = (jnp.exp(jnp.sum(lq1.astype(f32) * lk1.astype(f32)))
           - jnp.exp(jnp.sum(lq2.astype(f32) * lk2.astype(f32))) + lambda_init)
    slopes = alibi_slopes(DIFF_HEADS)
    k_pos = jnp.arange(S, dtype=jnp.int32)

    def block(args):
        q_blk, start = args
        q_pos = start + jnp.arange(Q_BLOCK, dtype=jnp.int32)
        dist = jnp.abs(q_pos[:, None] - k_pos[None, :]).astype(f32)
        bias = -slopes[:, None, None] * dist
        s = jnp.einsum('bhmqd,bhmkd->bhmqk', q_blk, kt) + bias[None, :, None]
        p = jax.nn.softmax(s, axis=-1)
        attn = p[:, :, 0] - lam * p[:, :, 1]
        return jnp.einsum('bhqk,bhkd->bhqd', attn, vt)

    o = lax.map(block, (qh, jnp.arange(nb, dtype=jnp.int32) * Q_BLOCK))
    o = o.transpose(1, 0, 3, 2, 4).reshape(B, S, DIFF_HEADS, DIFF_DV)
    o = rmsnorm(o, norm_g) * (1.0 - lambda_init)
    return o.reshape(B, S, DIFF_V_W).astype(q.dtype)

def gdn_scan(q, k, v, beta, log_a):
    b_, s_, h_, dk = q.shape
    dv = v.shape[-1]
    c = GDN_CHUNK
    qc, kc, vc, bc, gc = (_to_chunks(t, c) for t in (q, k, v, beta, log_a))
    gam = jnp.cumsum(gc, axis=-1)
    diff = gam[..., :, None] - gam[..., None, :]
    incl = jnp.tril(jnp.ones((c, c), dtype=bool))
    strict = jnp.tril(jnp.ones((c, c), dtype=bool), k=-1)
    decay = jnp.exp(jnp.where(incl, diff, -jnp.inf))
    kk = jnp.einsum('bhntd,bhnsd->bhnts', kc, kc)
    a_mat = jnp.where(strict, bc[..., None] * kk * decay, 0.0) + jnp.eye(c, dtype=jnp.float32)
    rhs = jnp.concatenate([vc * bc[..., None], kc * (bc * jnp.exp(gam))[..., None]], axis=-1)
    sol = lax.linalg.triangular_solve(a_mat, rhs, left_side=True, lower=True, unit_diagonal=True)
    u_val, k_cum = sol[..., :dv], sol[..., dv:]
    qk = jnp.einsum('bhntd,bhnsd->bhnts', qc, kc) * decay
    q_dec = qc * jnp.exp(gam)[..., None]
    k_dec = kc * jnp.exp(gam[..., -1:] - gam)[..., None]
    c_dec = jnp.exp(gam[..., -1])

    def step(state, inp):
        u_i, kc_i, qk_i, qd_i, kd_i, cd_i = inp
        v_new = u_i - jnp.einsum('bhtd,bhde->bhte', kc_i, state)
        o = jnp.einsum('bhtd,bhde->bhte', qd_i, state) + jnp.einsum('bhts,bhse->bhte', qk_i, v_new)
        state = cd_i[..., None, None] * state + jnp.einsum('bhsd,bhse->bhde', kd_i, v_new)
        return state, o

    xs = tuple(jnp.moveaxis(t, 2, 0) for t in (u_val, k_cum, qk, q_dec, k_dec, c_dec))
    _, o = lax.scan(step, jnp.zeros((b_, h_, dk, dv), jnp.float32), xs)
    return _from_chunks(o)

def gdn_mixer(qkv, z, ba, conv_w, a_log, dt_bias, norm_g):
    B, S, _ = qkv.shape
    f32 = jnp.float32
    qkv = jax.nn.silu(dwconv_centred(qkv, conv_w)).astype(f32)
    q, k, v = jnp.split(qkv, [GDN_QK_W, 2 * GDN_QK_W], axis=-1)
    q = l2norm(q.reshape(B, S, GDN_HEADS, GDN_DK)) * GDN_DK ** -0.5
    k = l2norm(k.reshape(B, S, GDN_HEADS, GDN_DK))
    v = v.reshape(B, S, GDN_HEADS, GDN_DV)
    ba = ba.astype(f32).reshape(B, S, 4, GDN_HEADS)
    beta = jax.nn.sigmoid(ba[:, :, :2])
    log_a = -jnp.exp(a_log.astype(f32)) * jax.nn.softplus(ba[:, :, 2:] + dt_bias.astype(f32))
    o_f = gdn_scan(q, k, v, beta[:, :, 0], log_a[:, :, 0])
    o_b = _flip(gdn_scan(_flip(q), _flip(k), _flip(v), _flip(beta[:, :, 1]), _flip(log_a[:, :, 1])))
    o = rmsnorm(o_f + o_b, norm_g) * jax.nn.silu(z.astype(f32)).reshape(B, S, GDN_HEADS, GDN_DV)
    return o.reshape(B, S, GDN_V_W).astype(z.dtype)

def gated_merge(h, branches, merge_w, merge_b, branch_up):
    out = None
    for i, y in enumerate(branches):
        term = jax.nn.sigmoid(h @ merge_w[i] + merge_b[i]) * (y @ branch_up[i])
        out = term if out is None else out + term
    return out

def memory_cross_attention(h, mem_n, w_q, w_kv, w_o):
    B, S, D = h.shape
    M = mem_n.shape[1]
    q = (h @ w_q).reshape(B, S, XATTN_HEADS, XATTN_DH)
    kv = (mem_n @ w_kv).reshape(B, M, 2, XATTN_HEADS, XATTN_DH)
    k, v = kv[:, :, 0], kv[:, :, 1]
    s = jnp.einsum('bshd,bmhd->bhsm', q, k).astype(jnp.float32) * XATTN_DH ** -0.5
    p = jax.nn.softmax(s, axis=-1)
    o = jnp.einsum('bhsm,bmhd->bshd', p.astype(v.dtype), v).reshape(B, S, D)
    return o @ w_o

def hier_moe(h, w_group, b_group, w_expert, b_expert, w1, w3, w2):
    B, S, D = h.shape
    T = B * S
    f32 = jnp.float32
    ht = h.reshape(T, D)
    g_logits = (ht @ w_group).astype(f32) + b_group.astype(f32)
    g_prob = jax.nn.softmax(g_logits, axis=-1)
    _, g_idx = lax.top_k(g_logits, 1)
    g_w = jnp.take_along_axis(g_prob, g_idx, axis=1)
    e_logits = ((ht @ w_expert).astype(f32) + b_expert.astype(f32)).reshape(T, N_GROUPS, EXPERTS_PER_GROUP)
    e_logits = jnp.take_along_axis(
        e_logits, jnp.broadcast_to(g_idx[:, :, None], (T, 1, EXPERTS_PER_GROUP)), axis=1)[:, 0]
    e_top, e_idx = lax.top_k(e_logits, TOP_K)
    gate = jax.nn.softmax(e_top, axis=-1) * g_w
    eid = (g_idx * EXPERTS_PER_GROUP + e_idx).reshape(-1)
    tok = jnp.repeat(jnp.arange(T, dtype=jnp.int32), TOP_K)
    wts = gate.reshape(-1)
    A = T * TOP_K
    n_blk = -(-A // MOE_BLOCK) + N_EXPERTS
    P = n_blk * MOE_BLOCK
    order = jnp.argsort(eid)
    eid_s, tok_s, w_s = eid[order], tok[order], wts[order]
    counts = jnp.zeros((N_EXPERTS,), jnp.int32).at[eid].add(1)
    padded = (counts + MOE_BLOCK - 1) // MOE_BLOCK * MOE_BLOCK
    pad_end = jnp.cumsum(padded)
    pad_start = pad_end - padded
    seg_start = jnp.cumsum(counts) - counts
    dest = pad_start[eid_s] + jnp.arange(A, dtype=jnp.int32) - seg_start[eid_s]
    row_tok = jnp.full((P,), T, jnp.int32).at[dest].set(tok_s)
    row_w = jnp.zeros((P,), f32).at[dest].set(w_s)
    blk_expert = jnp.minimum(
        jnp.searchsorted(pad_end, jnp.arange(n_blk, dtype=jnp.int32) * MOE_BLOCK, side='right'),
        N_EXPERTS - 1)
    h_pad = jnp.concatenate([ht, jnp.zeros((1, D), ht.dtype)], axis=0)
    xb = h_pad[row_tok].reshape(n_blk, MOE_BLOCK, D)

    def expert_block(args):
        xi, e = args
        return (jax.nn.silu(xi @ w1[e]) * (xi @ w3[e])) @ w2[e]

    yb = lax.map(expert_block, (xb, blk_expert)).reshape(P, D)
    out = jnp.zeros((T + 1, D), h.dtype).at[row_tok].add(yb * row_w[:, None].astype(yb.dtype))
    return out[:T].reshape(B, S, D)

def setup_inputs(seed: int = 0) -> dict:
    key = jax.random.key(seed)
    ks = iter(jax.random.split(key, 64))
    L = DEPTH
    f32 = jnp.float32

    def nrm(shape, fan_in):
        return jax.random.normal(next(ks), shape, f32) * fan_in ** -0.5

    def gain(shape):
        return 1.0 + 0.02 * jax.random.normal(next(ks), shape, f32)

    def small(shape, s=0.02):
        return s * jax.random.normal(next(ks), shape, f32)

    x = jax.random.normal(next(ks), (BATCH, SEQ, D_MODEL), f32)
    mem = jax.random.normal(next(ks), (BATCH, MEM_LEN, D_MODEL), f32)
    a0 = jax.random.uniform(next(ks), (L, 2, LRU_WIDTH), f32, minval=0.9, maxval=0.999) ** (1.0 / LRU_C)
    lru_lambda = jnp.log(a0) - jnp.log1p(-a0)
    gdn_a_log = jnp.log(jax.random.uniform(next(ks), (L, 2, GDN_HEADS), f32, minval=1.0, maxval=16.0))
    dt = jnp.exp(jax.random.uniform(next(ks), (L, 2, GDN_HEADS), f32,
                                    minval=math.log(1e-3), maxval=math.log(1e-1)))
    gdn_dt_bias = dt + jnp.log(-jnp.expm1(-dt))
    blk = LRU_WIDTH // LRU_BLOCKS
    return {
        'x': x,
        'mem': mem,
        'mix_norm': gain((L, D_MODEL)),
        'w_in': nrm((L, D_MODEL, D_IN), D_MODEL),
        'gla_lr_up': nrm((L, 2, GLA_RANK, GLA_QK_W), GLA_RANK),
        'gla_lr_bias': small((L, 2, GLA_QK_W), 0.1),
        'gla_norm': gain((L, GLA_DV)),
        'lru_conv_w': nrm((L, CONV_WIDTH, LRU_WIDTH), CONV_WIDTH),
        'lru_conv_b': small((L, LRU_WIDTH)),
        'lru_w_a': nrm((L, 2, LRU_BLOCKS, blk, blk), blk),
        'lru_b_a': small((L, 2, LRU_WIDTH)),
        'lru_w_x': nrm((L, 2, LRU_BLOCKS, blk, blk), blk),
        'lru_b_x': small((L, 2, LRU_WIDTH)),
        'lru_lambda': lru_lambda,
        'diff_lq1': small((L, DIFF_DH), 0.1),
        'diff_lk1': small((L, DIFF_DH), 0.1),
        'diff_lq2': small((L, DIFF_DH), 0.1),
        'diff_lk2': small((L, DIFF_DH), 0.1),
        'diff_norm': gain((L, DIFF_DV)),
        'gdn_conv_w': nrm((L, CONV_WIDTH, 2 * GDN_QK_W + GDN_V_W), CONV_WIDTH),
        'gdn_a_log': gdn_a_log,
        'gdn_dt_bias': gdn_dt_bias,
        'gdn_norm': gain((L, GDN_DV)),
        'merge_w': nrm((L, N_BRANCHES, D_MODEL, D_MODEL), D_MODEL),
        'merge_b': small((L, N_BRANCHES, D_MODEL)),
        'branch_up': nrm((L, N_BRANCHES, BRANCH_WIDTH, D_MODEL), BRANCH_WIDTH),
        'mix_out': nrm((L, D_MODEL, D_MODEL), D_MODEL),
        'xattn_norm': gain((L, D_MODEL)),
        'mem_norm': gain((L, D_MODEL)),
        'xattn_wq': nrm((L, D_MODEL, D_MODEL), D_MODEL),
        'xattn_wkv': nrm((L, D_MODEL, 2 * D_MODEL), D_MODEL),
        'xattn_wo': nrm((L, D_MODEL, D_MODEL), D_MODEL),
        'moe_norm': gain((L, D_MODEL)),
        'moe_w_group': nrm((L, D_MODEL, N_GROUPS), D_MODEL),
        'moe_b_group': small((L, N_GROUPS), 0.01),
        'moe_w_expert': nrm((L, D_MODEL, N_EXPERTS), D_MODEL),
        'moe_b_expert': small((L, N_EXPERTS), 0.01),
        'moe_w1': nrm((L, N_EXPERTS, D_MODEL, D_EXPERT), D_MODEL),
        'moe_w3': nrm((L, N_EXPERTS, D_MODEL, D_EXPERT), D_MODEL),
        'moe_w2': nrm((L, N_EXPERTS, D_EXPERT, D_MODEL), D_EXPERT),
        'final_norm': gain((D_MODEL,)),
    }

def reference(x, mem, mix_norm, w_in, gla_lr_up, gla_lr_bias, gla_norm,
              lru_conv_w, lru_conv_b, lru_w_a, lru_b_a, lru_w_x, lru_b_x, lru_lambda,
              diff_lq1, diff_lk1, diff_lq2, diff_lk2, diff_norm,
              gdn_conv_w, gdn_a_log, gdn_dt_bias, gdn_norm,
              merge_w, merge_b, branch_up, mix_out,
              xattn_norm, mem_norm, xattn_wq, xattn_wkv, xattn_wo,
              moe_norm, moe_w_group, moe_b_group, moe_w_expert, moe_b_expert,
              moe_w1, moe_w3, moe_w2, final_norm):
    split_at = np.cumsum(IN_SPLITS)[:-1].tolist()
    for l in range(DEPTH):
        h = rmsnorm(x, mix_norm[l])
        parts = jnp.split(h @ w_in[l], split_at, axis=-1)
        gq, gk, gv, gog, glr, lx, lg, dq, dk, dv, nqkv, nz, nba = parts
        y_gla = gla_mixer(gq, gk, gv, gog, glr, gla_lr_up[l], gla_lr_bias[l], gla_norm[l])
        y_lru = rglru_mixer(lx, lg, lru_conv_w[l], lru_conv_b[l], lru_w_a[l], lru_b_a[l],
                            lru_w_x[l], lru_b_x[l], lru_lambda[l])
        y_diff = diff_attention(dq, dk, dv, diff_lq1[l], diff_lk1[l], diff_lq2[l], diff_lk2[l],
                                diff_norm[l], 0.8 - 0.6 * math.exp(-0.3 * l))
        y_gdn = gdn_mixer(nqkv, nz, nba, gdn_conv_w[l], gdn_a_log[l], gdn_dt_bias[l], gdn_norm[l])
        merged = gated_merge(h, (y_gla, y_lru, y_diff, y_gdn), merge_w[l], merge_b[l], branch_up[l])
        x = x + merged @ mix_out[l]
        h = rmsnorm(x, xattn_norm[l])
        x = x + memory_cross_attention(h, rmsnorm(mem, mem_norm[l]), xattn_wq[l], xattn_wkv[l], xattn_wo[l])
        h = rmsnorm(x, moe_norm[l])
        x = x + hier_moe(h, moe_w_group[l], moe_b_group[l], moe_w_expert[l], moe_b_expert[l],
                         moe_w1[l], moe_w3[l], moe_w2[l])
    return rmsnorm(x, final_norm)


_drawn_inputs = setup_inputs


def setup_inputs(seed=0):
    import zlib

    import numpy as np

    out = dict(_drawn_inputs(seed))
    spreads = {}
    factors = {'gla_norm': 4.031,
     'lru_b_a': 8.0,
     'lru_b_x': 8.0,
     'diff_lq1': 5.343,
     'diff_lk1': 3.152,
     'diff_norm': 3.721,
     'gdn_norm': 4.416,
     'merge_b': 3.678,
     'xattn_norm': 8.0,
     'mem_norm': 5.877,
     'moe_b_group': 33.68,
     'moe_b_expert': 29.584,
     'moe_norm': 8.0}
    for name, (base, spread) in spreads.items():
        noise = np.random.default_rng([zlib.crc32(name.encode()), seed]).standard_normal(out[name].shape)
        drawn = base * np.exp(spread * noise) if base else spread * noise
        out[name] = jnp.asarray(drawn.astype(out[name].dtype))
    for name, factor in factors.items():
        out[name] = (out[name] * factor).astype(out[name].dtype)
    return out
```

```python
import math
from contextlib import ExitStack

import concourse.bass as bass
from concourse import mybir

P = 128
T = 1024
D = 1024
KT = D // P
TT = T // P
NH = 4
WS = 256.0
NLAND = 4
NE = 32
NG = 4
GE = NE // NG
DE = D // 2
KE = DE // P
NOV = (2 * T - 1) // P
NBLK = NE + NOV

F32 = mybir.dt.float32
F16 = mybir.dt.float16
I32 = mybir.dt.int32
U32 = mybir.dt.uint32
ALU = mybir.AluOpType
ACT = mybir.ActivationFunctionType
AX = mybir.AxisListType
EPS = 1e-6

GQ, GK, GV, GOG, GLR = 0, 128, 256, 512, 768
LX, LG = 800, 1056
DQ, DK, DV = 1312, 1568, 1824
NQKV, NZ, NBA = 2080, 2848, 3104

C_MERGEB = 0
C_LRB = 32
C_LCW = 34
C_LCB = 42
C_LBA = 44
C_LBX = 48
C_LAM = 52
C_GCW = 56
NCOLS = 80
R_GLAN, R_DIFFN, R_GDNN = 0, 64, 128
R_ALOG, R_DTB = 192, 200
R_DL = 208
R_BG, R_BE = 336, 340
NROWS = 372


class Counter:

    def __init__(self, sem, name, known):
        self.sem, self.name, self.n, self.known, self.found = sem, name, 0, known, {}

    def mark(self, *key):
        self.n += 1
        assert key not in self.found, (self.name, key)
        self.found[key] = self.n
        return self.sem, 1

    def at(self, *key):
        if self.known is None:
            return self.sem, 1
        return self.sem, self.known[self.name][key]

    def last(self):
        return self.sem, self.n


def plan_panels(A):
    panels = []

    def kview(w):
        return w.rearrange("(k p) n -> p k n", p=P)

    def add(name, parts, groups):
        nk = max(k0 + s.shape[1] for s, k0, c0 in parts)
        panels.append(dict(name=name, parts=parts, nk=nk, groups=groups))

    w_in = kview(A["w_in"])

    def fm(name, c, n=2):
        return [(name, jt, half) for jt in range(n) for half in range(2)]

    def tm(name):
        return [(name, tp) for tp in range(TT // 2)]

    def proj(name, col, groups):
        add(name, [(w_in[:, :, col:col + 256], 0, 0)], groups)

    def merge(i):
        mw = kview(A["merge_w"][i])
        up = kview(A["branch_up"][i])
        for q in range(4):
            add(f"merge{i}{q}", [(mw[:, :, q * 256:q * 256 + 256], 0, 0), (up[:, :, q * 256:q * 256 + 256], KT, 0)],
                [(kind, i, 2 * q + jt, half) for jt in range(2) for half in range(2) for kind in ("gate", "up")])

    proj("lx", LX, fm("lx", LX))
    proj("lg", LG, fm("lg", LG))
    add("glr_nba", [(w_in[:, :, GLR:GLR + 32], 0, 0), (w_in[:, :, NBA:NBA + 16], 0, 32)],
        [("glr", 0, 0), ("glr", 0, 1), ("nba", 0)])
    proj("gqk", GQ, fm("gqk", GQ))
    proj("gv", GV, tm("gv"))
    merge(1)
    proj("gog", GOG, tm("gog"))
    proj("dq", DQ, fm("dq", DQ))
    proj("dk", DK, fm("dk", DK))
    proj("dv", DV, tm("dv"))
    merge(0)
    proj("nq", NQKV, fm("nq", 0))
    proj("nk", NQKV + 256, fm("nk", 0))
    proj("nv", NQKV + 512, fm("nv", 0))
    merge(2)
    proj("nz", NZ, tm("nz"))
    merge(3)
    for q in range(4):
        add(f"mix{q}", [(kview(A["mix_out"])[:, :, q * 256:q * 256 + 256], 0, 0)], [("mix", q, tp) for tp in range(4)])
    for q in range(4):
        add(f"wk{q}", [(kview(A["xattn_wkv"])[:, :, q * 256:q * 256 + 256], 0, 0)], [("wk", q)])
    for q in range(4):
        add(f"wv{q}", [(kview(A["xattn_wkv"])[:, :, D + q * 256:D + q * 256 + 256], 0, 0)], [("wv", q)])
    for q in range(4):
        add(f"wq{q}", [(kview(A["xattn_wq"])[:, :, q * 256:q * 256 + 256], 0, 0)],
            [("wq", 2 * q + jt, half) for jt in range(2) for half in range(2)])
    for q in range(4):
        add(f"wo{q}", [(kview(A["xattn_wo"])[:, :, q * 256:q * 256 + 256], 0, 0)], [("wo", q, tp) for tp in range(4)])
    return panels


def plan_schedule(panels):
    order = []
    at = [0]
    index = {p["name"]: i for i, p in enumerate(panels)}

    def conv(i):
        if i < len(panels):
            order.append(("conv", i))

    def dense(*names, between=()):
        between = list(between)
        groups = sum(len(panels[index[n]]["groups"]) for n in names)
        done = placed = 0
        for n in names:
            i = index[n]
            assert i == at[0], (n, panels[at[0]]["name"])
            at[0] += 1
            conv(i + 1)
            for g in range(len(panels[i]["groups"])):
                order.append(("mm", i, g))
                order.append(("evac", i, g))
                done += 1
                while placed < len(between) * done // groups:
                    order.append(between[placed])
                    placed += 1
        order.extend(between[placed:])

    def norm(which, n):
        order.append(("norm_stats", which, n))
        for tt in range(n):
            order.append(("norm_tile", which, tt))

    merge = lambda i: [f"merge{i}{q}" for q in range(4)]
    norm("x", TT)
    conv(0)
    dense("lx", "lg")
    order.append(("lru_pre",))
    order.extend(("lru_dir", d, t) for d in range(2) for t in range(2))
    order.append(("lru_fin",))
    dense("glr_nba", "gqk", "gv")
    gla = []
    for d in range(2):
        gla += [("gla_pre", d)]
        gla += [("gla_chunk", d, i) for i in range(TT)]
    dense(*merge(1), between=gla)
    dense("gog")
    order.extend([("fin", "gla"), ("fin_tr", "gla")])
    dense("dq", "dk", "dv")
    diff = [("diff_pre",), ("diff_qk", 0)]
    for u in range(NH * TT):
        if u + 1 < NH * TT:
            diff.append(("diff_qk", u + 1))
        diff.append(("diff_pv", u))
    dense(*merge(0), between=diff)
    order.extend([("fin", "diff"), ("fin_tr", "diff")])
    for s in ("nq", "nk", "nv"):
        dense(s)
        order.append(("gdn_conv", s))
    order.append(("gdn_scal",))
    gdn = [("gdn", i, part) for i in range(TT) for part in range(9)]
    dense(*merge(2), between=gdn)
    dense("nz")
    order.extend([("fin", "gdn"), ("fin_tr", "gdn")])
    dense(*merge(3))
    order.append(("merged_pair",))
    dense(*[f"mix{q}" for q in range(4)])
    norm("mem", 2)
    dense(*[f"wk{q}" for q in range(4)], *[f"wv{q}" for q in range(4)])
    norm("x1", TT)
    dense(*[f"wq{q}" for q in range(4)])
    order.extend(("xattn", g) for g in range(2 * NH))
    dense(*[f"wo{q}" for q in range(4)])
    order.append(("norm_stats", "x2", TT))
    for tt in range(TT):
        order.append(("norm_tile", "x2", tt))
        if tt:
            order.append(("router", tt - 1))
    order.append(("router", TT - 1))
    return order


def build(nc, A, out, known):
    panels = plan_panels(A)
    schedule = plan_schedule(panels)
    counters = {}

    gid, chunk0, nchunk = {}, {}, 0
    for i, p in enumerate(panels):
        chunk0[i] = nchunk
        nchunk += p["nk"] // 2
        for g in range(len(p["groups"])):
            gid[i, g] = len(gid)
    last_group = {i: gid[i, len(p["groups"]) - 1] for i, p in enumerate(panels)}
    kind_of = [k for p in panels for k in p["groups"]]

    with ExitStack() as ctx:
        def sem(name):
            return ctx.enter_context(nc.semaphore(name))

        def counter(name):
            if name not in counters:
                counters[name] = Counter(sem(name), name, known)
            return counters[name]

        SB = ctx.enter_context(nc.sbuf_tensor("arena", [P, 52992], F32))
        PS = ctx.enter_context(nc.psum_tensor("psum", [P, 8, 512], F32))

        def f32(off, *shape):
            n = 1
            for s in shape:
                n *= s
            v = SB[:, off:off + n]
            if len(shape) == 2:
                v = v.rearrange("p (a b) -> p a b", b=shape[1])
            if len(shape) == 3:
                v = v.rearrange("p (a b c) -> p a b c", b=shape[1], c=shape[2])
            return v

        def f16(off, *shape):
            n = 1
            for s in shape:
                n *= s
            v = SB[:, off:off + n // 2].bitcast(F16)
            if len(shape) == 2:
                v = v.rearrange("p (a b) -> p a b", b=shape[1])
            if len(shape) == 3:
                v = v.rearrange("p (a b c) -> p a b c", b=shape[1], c=shape[2])
            return v

        at = [0]

        def take(n):
            at[0] += n
            return at[0] - n

        ident, inc_f, inc_b, st_f, st_b, ones, bd64 = (f32(take(P), P) for _ in range(7))
        gla_bd = f32(take(256), 256)
        nmask = f16(take(7 * P), 14, P)
        cols = f32(take(NCOLS), NCOLS)
        rows = f32(take(NROWS), NROWS)
        small = take(3840 - at[0])
        H = (f16(take(4096), KT, T), f16(take(4096), KT, T))
        H_OFF = at[0] - 8192
        MG_OFF = take(8192)
        merged = f32(MG_OFF, KT, T)
        YP_OFF = take(4096)
        Y = [(f16(YP_OFF + 2048 * s, 2, T), f16(YP_OFF + 2048 * s + 1024, 2, T)) for s in range(2)]
        LAND = [f32(take(512), 2, 256) for _ in range(NLAND)]
        W = [(f16(take(1280), 10, 256), f16(take(1280), 10, 256)) for _ in range(2)]
        SG_OFF = take(2048)
        SG = [f32(SG_OFF + 512 * s, 512) for s in range(4)]
        gain_row = f32(SG_OFF, D)
        BR = take(0)
        BR_N = 52992 - BR
        X = f32(BR + 8192, TT, D)
        MP = (f16(BR, KT, T), f16(BR + 4096, KT, T))
        XH = [f32(BR + 16384 + 1024 * s, D) for s in range(2)]
        SQ = f32(BR + 18432, D)
        sc0 = small

        def scol(n):
            nonlocal sc0
            sc0 += n
            assert sc0 <= 3840
            return f32(sc0 - n, n)

        norm_ss = scol(8)
        norm_r = scol(8)
        eps_col = scol(1)
        lneighth = scol(1)
        fin_ss = scol(32)
        fin_r = scol(32)
        MEMT = (f16(MG_OFF, KT, 256), f16(MG_OFF + 1024, KT, 256))
        MEM = f32(MG_OFF + 2048, 2, D)
        XK = (f16(MG_OFF + 4096, KT, 256), f16(MG_OFF + 5120, KT, 256))
        XV = (f16(MG_OFF + 6144, 2, D), f16(MG_OFF + 7168, 2, D))
        H2 = H
        XQ = MP
        XO = H
        XP = [f32(YP_OFF + 1024 * s, 4, 256) for s in range(2)]
        XPT = [(f16(YP_OFF + 2048 + 1024 * s, 2, 512), f16(YP_OFF + 2560 + 1024 * s, 2, 512)) for s in range(2)]
        o = BR
        LXP = SB[:, o:o + 2056].rearrange("p (a b) -> p a b", b=1028)
        LU = f32(o + 2056, 2, T)
        LG_ = f32(o + 4104, 2, T)
        LHS = f32(o + 6152, 2, T)
        LR_, LI_, LA_, LTH, LM, LXI, LH1 = (f32(o + 8200 + 1024 * j, T) for j in range(7))
        LW = f32(MG_OFF, 8, P)
        GQK = f32(BR, 2, T)
        GLRT = f32(BR + 2048, T)
        GVT = f32(BR + 3072, TT, 256)
        GO = f32(BR + 5120, TT, 256)
        QBD = f32(BR + 7168, NH, T)
        GOGT = f32(BR + 7168, TT, 256)
        GTMP = f32(BR + 7168 + 2048, TT, 256)
        QT_ = f32(BR + 11264, T)
        KTM = f32(BR + 12288, TT, P)
        GSM = f32(BR + 13312, TT, 256)
        GST = [f32(BR + 15360 + 512 * s, 512) for s in range(2)]
        TA, TB, TC = (f32(BR + 16384 + 1024 * j, T) for j in range(3))
        GS = f32(BR + 16384, 256)
        LRUP = scol(256)
        g_em, g_ee, g_eem, g_mid, g_end = (scol(TT) for _ in range(5))
        DQT = f32(BR, 2, T)
        DKT = f32(BR + 2048, 2, T)
        DVT = f32(BR + 4096, TT, 256)
        DO = f32(BR + 6144, TT, 256)
        DW = f32(BR + 8192, 1920)
        DWH = f32(BR + 10112, 1920)
        DS = [f32(BR + 12032 + 2048 * s, 2, T) for s in range(2)]
        DAT = [f32(BR + 16128 + 1024 * s, TT, P) for s in range(2)]
        DQZ = [f32(BR + 18176 + 128 * s, P) for s in range(8)]
        DTMP = f32(BR + 12032, TT, 256)
        d_lam = scol(4)
        d_mx = [scol(2) for _ in range(2)]
        d_l = [scol(2) for _ in range(2)]
        d_rl = [scol(2) for _ in range(2)]
        d_c = [scol(1) for _ in range(2)]
        NQ = f32(BR, 2, T)
        NK = f32(BR + 2048, 2, T)
        NKT = f32(BR + 4096, TT, 256)
        NVT = f32(BR + 6144, TT, 256)
        NO = f32(BR + 8192, TT, 256)
        NS = [f32(BR + 10240 + 256 * d, 2, P) for d in range(2)]
        NKB = [f32(BR + 10752 + 512 * d, NH, P) for d in range(2)]
        UN = BR + 11776
        NLT = [f32(UN + 3840 * d, NH, P) for d in range(2)]
        NQT = [f32(UN + 3840 * d + 512, NH, P) for d in range(2)]
        NX = [f32(UN + 3840 * d + 1024, NH, P) for d in range(2)]
        NZ_ = [f32(UN + 3840 * d + 1536, NH, P) for d in range(2)]
        NY = [f32(UN + 3840 * d + 2048, NH, P) for d in range(2)]
        NKE = [f32(UN + 3840 * d + 2560, 2, P) for d in range(2)]
        NKD = [f32(UN + 3840 * d + 2816, 2, P) for d in range(2)]
        NWK = [f32(UN + 3840 * d + 3072, 2, P) for d in range(2)]
        NQD = [f32(UN + 3840 * d + 3328, 2, P) for d in range(2)]
        NVN = [f32(UN + 3840 * d + 3584, 2, P) for d in range(2)]
        RAW = SB[:, UN:UN + 2056].rearrange("p (a b) -> p a b", b=1028)
        NVF = f32(UN + 2056, 2, T)
        NSQ = f32(UN + 4104, 2, T)
        NZT = f32(UN, TT, 256)
        NTMP = f32(UN + 2048, TT, 256)
        assert UN + 7680 <= 52992, UN
        NBA_ = scol(128)
        n_beta = scol(64)
        n_la = scol(64)
        n_t = [scol(64) for _ in range(4)]
        n_eg = scol(192)
        n_cd = scol(32)
        n_al = scol(8)
        BETA = n_beta.rearrange("p (d c h) -> p d c h", d=2, c=TT)
        LAd = n_la.rearrange("p (d c h) -> p d c h", d=2, c=TT)
        EG = n_eg.rearrange("p (k d c h) -> p k d c h", k=3, d=2, c=TT)
        CD = n_cd.rearrange("p (d c t) -> p d c t", d=2, c=TT)
        FIN = {
            "gla": dict(o=GO, gate=GOGT, tmp=GTMP, row=R_GLAN, scale=1.0, y=1),
            "diff": dict(o=DO, gate=None, tmp=DTMP, row=R_DIFFN, scale=0.8, y=0),
            "gdn": dict(o=NO, gate=NZT, tmp=NTMP, row=R_GDNN, scale=1.0, y=1),
        }
        l_t, l_e, l_z, l_q, l_s, l_pc, l_nc = (scol(4) for _ in range(7))
        x_mx = [scol(4) for _ in range(2)]
        x_l = [scol(4) for _ in range(2)]
        d_dot = scol(64)
        YSLOT = {1: 0, 0: 1, 2: 0, 3: 1}

        XW1, XW3 = ([f32(H_OFF + 12288 * s + o, KT, DE) for s in range(2)] for o in (0, 4096))
        XW2 = [f32(H_OFF + 12288 * s + 8192, KE, D) for s in range(2)]
        XR = [f32(H_OFF + 24576 + 1024 * s, D) for s in range(2)]
        GU = f32(H_OFF + 26624, DE)
        GUT = f32(H_OFF + 27136, KE, P)
        assert H_OFF + 27648 <= SG_OFF
        ZROW = GU[:, 0:P]
        TROWS = GUT[:, 0, :]
        o = SG_OFF + 1024
        WR = f32(o, KT, 36)
        K_INT = f32(o + 288, 88).bitcast(I32)
        K_F = f32(o + 376, 88)
        K_DESC, K_E, K_J, K_TOK = K_F[:, 0:32], K_F[:, 32:64], K_F[:, 64:80], K_F[:, 80:88]
        GATE = f32(o + 464, 2, TT)
        SLOT = f32(o + 480, 2, TT)
        SLOTU = f32(o + 496, 2 * TT).bitcast(U32)
        IDX = f32(o + 512, NBLK).bitcast(U32)
        OVI = f32(o + 561, 17).bitcast(I32)
        f_ss, f_r = f32(o + 580, TT), f32(o + 588, TT)
        H3 = f32(BR, KT, T)
        XT = [f32(BR + 1024 * s, KT, P) for s in range(2)]
        YB = [f32(BR + 2048 + 1024 * s, 2, 512) for s in range(2)]
        SL = f32(BR + 4096, DE)
        o = BR + 4608
        r_l = f32(o, TT, 36)
        r_e, r_w, r_o1, r_o2, r_a, r_ap, r_pos, r_mk = (f32(o + 288 + 256 * j, TT, NE) for j in range(8))
        r_cmp = f32(o + 2336, 16, NE)
        o += 2848
        r_at, r_cnt, r_nov, r_inc, r_sb, r_g4, r_w4 = (f32(o + 32 * j, NE) for j in range(7))
        r_gm, r_gs, r_m1, r_m2, r_x, r_ex, r_wm = (f32(o + 224 + 8 * j, TT) for j in range(7))
        r_ov = f32(o + 280, 17)
        YG = [f32(H_OFF + 8192 * k, TT, D) for k in range(2)]
        XH_OUT = [YG[0][:, tt, :] for tt in range(TT)]

        W1, W3, W2 = (A[n].rearrange("e (p k) n -> p e k n", p=P) for n in ("w1", "w3", "w2"))
        XH_D, TABLE, YROWS = A["xhat"], A["table"], A["yrows"]

        def bc(ap, *shape):
            return ap.broadcast_to(list(shape))

        def heads(ap):
            return bc(ap.unsqueeze(2), P, NH, 64)

        def over(ap, n=NH):
            return bc(ap.unsqueeze(1), P, n, P)

        def products(kind, panel):
            w = W[panel % 2]
            name = kind[0]

            def wt(c0, c1, k0=0):
                return [lambda k, q=q: w[q][:, k0 + k, c0:c1] for q in range(2)]

            def act(pair, c0, c1):
                return [lambda k, q=q: pair[q][:, k, c0:c1] for q in range(2)]

            if name in ("gv", "gog", "dv", "nz", "mix", "wo"):
                src = {"mix": MP, "wo": XO}.get(name, H)
                tp = kind[-1]
                return [((0, P), (256 * s, 256 * s + 256), act(src, (2 * tp + s) * P, (2 * tp + s + 1) * P),
                         wt(0, 256), KT) for s in range(2)]
            if name == "nba":
                return [((0, P), (16 * t, 16 * t + 16), act(H, t * P, t * P + P), wt(32, 48), KT) for t in range(TT)]
            if name == "glr":
                return [((0, 32), (0, 512), wt(0, 32), act(H, kind[2] * 512, kind[2] * 512 + 512), KT)]
            if name == "gate":
                j = kind[2] % 2
                return [((0, P), (0, 512), wt(j * P, j * P + P), act(H, kind[3] * 512, kind[3] * 512 + 512), KT)]
            if name == "up":
                j = kind[2] % 2
                return [((0, P), (0, 512), wt(j * P, j * P + P, KT),
                         act(Y[YSLOT[kind[1]]], kind[3] * 512, kind[3] * 512 + 512), 2)]
            if name == "wk":
                return [((0, P), (256 * j, 256 * j + 256), wt(j * P, j * P + P), act(MEMT, 0, 256), KT) for j in range(2)]
            if name == "wv":
                return [((0, P), (256 * m, 256 * m + 256), act(MEMT, m * P, m * P + P), wt(0, 256), KT) for m in range(2)]
            src = H2 if name == "wq" else H
            j = kind[1] % 2
            return [((0, P), (0, 512), wt(j * P, j * P + P), act(src, kind[2] * 512, kind[2] * 512 + 512), KT)]

        land = [sem(f"land{s}") for s in range(NLAND)]
        pe_mm = counter("pe_mm")
        act_hi = counter("act_w_hi")
        vec_lo = counter("vec_w_lo")

        def emptied(g):
            kind = kind_of[g]
            if kind[0] in ("up", "mix", "wo", "wk", "wv", "wq"):
                return counter("vec_evac").at(g)
            return counter("act_evac").at(g)

        block = ctx.enter_context(nc.Block())
        g_of = {k: n for n, k in enumerate(kind_of)}
        gate_no = {n: sum(k[0] == "gate" for k in kind_of[:n]) for n in range(len(kind_of))}
        par_in = sem("params_in")
        N_PAR = 4
        x_in = [sem(f"x_in{tt}") for tt in range(TT)]
        x_again = sem("x_again")
        gain_in = sem("gain_in")
        GAINS = ["x", "mem", "x1", "x2"]

        xhat_out = [sem(f"xhat_out{s}") for s in range(2)]
        wr_in, zero_out, scattered, table_in = (sem(n) for n in ("router_w_in", "table_zeroed", "table_written", "table_back"))
        LAST_MM = len(kind_of) - 1

        w1_in = [sem(f"w1_in{s}") for s in range(2)]
        w3_in = [sem(f"w3_in{s}") for s in range(2)]
        w2_in = [sem(f"w2_in{s}") for s in range(2)]
        rows_in = [sem(f"rows_in{s}") for s in range(2)]
        y_out = [sem(f"y_out{s}") for s in range(2)]
        pe_xt, pe_a1, pe_a3, pe_gt, pe_y = (sem(f"expert_pe_{n}") for n in ("xt", "a1", "a3", "gt", "y"))
        act_sl, act_xt, act_gt, act_y = (sem(f"expert_act_{n}") for n in ("silu", "xt", "gt", "y"))
        vec_g, vec_xt, vec_y = (sem(f"expert_vec_{n}") for n in ("g", "xt", "y"))
        y_in = [sem(f"y_in{tt}") for tt in range(TT)]
        out_done = sem("out_done")
        spare_rows = sem("spare_rows")

        def after(eng, semaphore, value):
            if not (isinstance(value, int) and value <= 0):
                eng.wait_ge(semaphore, value)

        def experts(eng, prologue, period, epilogue):
            prologue()
            period(0, 0, 0)
            period(1, 1, 0)
            with eng.Fori(1, NE // 2 - 1) as n:
                period(2 * n, 0, n)
                period(2 * n + 1, 1, n)
            period(NE - 2, 0, NE // 2 - 1)
            period(NE - 1, 1, NE // 2 - 1)
            epilogue()

        def beyond(eng, body):
            number = eng.value_load(OVI[0:1, 16:17], min_val=0, max_val=NOV)
            with eng.Fori(0, NOV) as j:
                with eng.If(number > j):
                    body(j + NE, j)
            return number

        @block.tensor
        def _(pe):
            for step in schedule:
                what = step[0]
                if what == "mm":
                    i, g = step[1:]
                    n = gid[i, g]
                    if n >= 2:
                        pe.wait_ge(*emptied(n - 2))
                    bank = PS[:, n % 2, :]
                    kind = kind_of[n]
                    if kind[0] == "up":
                        pe.wait_ge(*counter("vec_fin").at("y", kind[1]))
                    if kind[0] == "mix" and g == 0:
                        pe.wait_ge(*counter("vec_pair").at("merged", KT - 1))
                    if kind[0] in ("wk", "wv") and g == 0:
                        pe.wait_ge(*counter("vec_norm").at("mem", "lo", 1))
                    if kind[0] == "wq" and g == 0:
                        pe.wait_ge(*counter("vec_norm").at("x1", "lo", TT - 1))
                    if kind[0] == "wo" and g == 0:
                        pe.wait_ge(*counter("vec_xattn").at("o", 2 * NH - 1))
                    if n == 0:
                        pe.wait_ge(*counter("vec_norm").at("x", "lo", TT - 1))
                    for ip, (prt, (c0, c1), lhs, rhs, nk) in enumerate(products(kind, i)):
                        for k in range(nk):
                            if g == 0 and ip == 0 and k % 2 == 0:
                                for c in range(k // 2, panels[i]["nk"] // 2) if k + 2 >= nk else [k // 2]:
                                    pe.wait_ge(*vec_lo.at(chunk0[i] + c))
                            for a, b in ((0, 0), (0, 1), (1, 0)):
                                mm = nc.tensor.matmul(bank[prt[0]:prt[1], c0:c1], lhs[a](k), rhs[b](k),
                                                      start=(k == 0 and a + b == 0), stop=(k == nk - 1 and a == 1))
                    mm.then_inc(*pe_mm.mark(n))
                elif what == "norm_tile":
                    which, tt = step[1:]
                    v, a, q = counter("vec_norm"), counter("act_norm"), counter("pe_norm")
                    pe.wait_ge(*v.at(which, "xh", tt))
                    if tt >= 2 and which == "x2":
                        pe.wait_ge(*a.at(which, "hi", tt - 2, 1))
                    elif tt >= 2:
                        pe.wait_ge(*v.at(which, "lo", tt - 2))
                    elif which == "mem":
                        pe.wait_ge(*counter("vec_fin").at("y", 3))
                    elif which in ("x1", "x2"):
                        pe.wait_ge(*v.at("mem", "lo", 1))
                    elif tt == 0:
                        pe.wait_ge(*counter("pool_const").at("ident"))
                    for k in range(KT):
                        tr = nc.tensor.transpose(PS[:, 2 + 2 * (tt % 2) + k // 4, (k % 4) * P:(k % 4) * P + P],
                                                 XH[tt % 2][:, k * P:k * P + P], ident)
                    tr.then_inc(*q.mark(which, "tr", tt))
                elif what == "lru_dir":
                    d, t = step[1:]
                    q, a = counter("pe_lru"), counter("act_lru")
                    if d + t == 0:
                        pe.wait_ge(*counter("vec_lru").at("u", 1))
                        pe.wait_ge(par_in, 16 * N_PAR)
                        pe.wait_ge(*counter("vec_norm").at("x", "lo", TT - 1))
                    else:
                        dp, tp = divmod(2 * d + t - 1, 2)
                        pe.wait_ge(*a.at("i", dp, tp))
                    for gate in range(2):
                        for half in range(2):
                            mm = nc.tensor.matmul(PS[:, 2 + 2 * gate + half, :], LW[:, 4 * d + 2 * gate + t, :],
                                                  LU[:, t, half * 512:half * 512 + 512], start=True, stop=True)
                        mm.then_inc(*q.mark("gate", d, t, gate))
                elif what == "gla_pre":
                    d = step[1]
                    q, a, v = counter("pe_gla"), counter("act_gla"), counter("vec_gla")
                    pe.wait_ge(*counter("act_evac").at(g_of["glr", 0, 1]))
                    if d == 0:
                        pe.wait_ge(*counter("act_lru").at("i", 1, 1))
                    else:
                        pe.wait_ge(*v.at("st", 0, TT - 1))
                    for half in range(2):
                        mm = nc.tensor.matmul(PS[:, 2 + half, :], LRUP[0:32, d * P:d * P + P],
                                              GLRT[0:32, half * 512:half * 512 + 512], start=True, stop=True)
                    mm.then_inc(*q.mark("z", d))
                    pe.wait_ge(*v.at("kt", d))
                    if d == 1:
                        pe.wait_ge(*v.at("u", 0, TT - 2))
                    for c in range(TT):
                        mm = nc.tensor.transpose(PS[:, 6 + c // 4, (c % 4) * P:(c % 4) * P + P], TC[:, c * P:c * P + P], ident)
                        if c % 4 == 3:
                            mm.then_inc(*q.mark("ktt", d, c // 4))
                elif what == "gla_chunk":
                    d, i = step[1:]
                    c = i if d == 0 else TT - 1 - i
                    q, a, v = counter("pe_gla"), counter("act_gla"), counter("vec_gla")
                    cs = slice(c * P, c * P + P)
                    if i == 0:
                        pe.wait_ge(*v.at("qbd", d))
                        pe.wait_ge(*a.at("ktm", d, 1))
                        pe.wait_ge(*counter("act_evac").at(g_of["gv", 3]))
                    if i >= 2:
                        pe.wait_ge(*v.at("st", d, i - 2))
                    elif d == 1:
                        pe.wait_ge(*v.at("st", 0, TT - 2 + i))
                    pe.wait_ge(*v.at("z", d))
                    nc.tensor.matmul(PS[:, 2 + i % 2, :], TC[:, cs], QBD[:, :, cs], start=True, stop=True)\
                        .then_inc(*q.mark("s", d, i))
                    if i < TT - 1:
                        if i >= 2:
                            pe.wait_ge(*v.at("u", d, i - 2))
                        nc.tensor.matmul(PS[:, 6 + i % 2, 0:256], KTM[:, c, :], GVT[:, c, :], start=True, stop=True)\
                            .then_inc(*q.mark("u", d, i))
                    bank = PS[:, 4 + i % 2, 0:256]
                    n = TT * d + i
                    if n >= 2:
                        dp, ip = divmod(n - 2, TT)
                        pe.wait_ge(*(a if dp == 0 else v).at("o", dp, ip))
                    pe.wait_ge(*v.at("state", d, i))
                    nc.tensor.matmul(bank, QT_[:, cs], GSM[:, c, :], start=True, stop=False)
                    pe.wait_ge(*v.at("st", d, i))
                    for h in range(NH):
                        mm = nc.tensor.matmul(bank[:, h * 64:h * 64 + 64], GST[i % 2][:, h * P:h * P + P],
                                              GVT[:, c, h * 64:h * 64 + 64], start=False, stop=h == NH - 1)
                    mm.then_inc(*q.mark("o", d, i))
                elif what == "fin_tr":
                    br = step[1]
                    q, v, a = counter("pe_fin"), counter("vec_fin"), counter("act_fin")
                    pe.wait_ge(*v.at("done", br))
                    for ft in range(2):
                        for c in range(TT):
                            tr = nc.tensor.transpose(PS[:, 2 + 2 * ft + c // 4, (c % 4) * P:(c % 4) * P + P],
                                                     FIN[br]["o"][:, c, ft * P:ft * P + P], ident)
                        tr.then_inc(*q.mark("tr", br, ft))
                elif what == "diff_qk":
                    u = step[1]
                    h, qt = divmod(u, TT)
                    q, v, po = counter("pe_diff"), counter("vec_diff"), counter("pool_diff")
                    if u == 0:
                        pe.wait_ge(*counter("act_evac").at(g_of["dv", 3]))
                        pe.wait_ge(*counter("vec_fin").at("y", 0))
                    pe.wait_ge(*po.at("q", u))
                    for m in range(2):
                        if u:
                            pe.wait_ge(*v.at("max", u - 1, m))
                        for half in range(2):
                            mm = nc.tensor.matmul(PS[:, 2 + 2 * m + half, :], DQZ[4 * (u % 2) + 2 * (h % 2) + m],
                                                  DKT[:, h // 2, half * 512:half * 512 + 512], start=True, stop=True)
                        mm.then_inc(*q.mark("s", u, m))
                elif what == "diff_pv":
                    u = step[1]
                    h, qt = divmod(u, TT)
                    q, v, a = counter("pe_diff"), counter("vec_diff"), counter("act_diff")
                    pe.wait_ge(*v.at("comb", u))
                    for r in range(2):
                        if r:
                            pe.wait_ge(*a.at("at", u, 0))
                        elif u:
                            pe.wait_ge(*v.at("at", u - 1, 1))
                        for k in range(4):
                            tr = nc.tensor.transpose(PS[:, 6, k * P:k * P + P], DS[u % 2][:, 0, (4 * r + k) * P:(4 * r + k + 1) * P], ident)
                        tr.then_inc(*q.mark("tr", u, r))
                    if u:
                        pe.wait_ge(*a.at("o", u - 1))
                    pe.wait_ge(*v.at("at", u, 1))
                    for k in range(TT):
                        mm = nc.tensor.matmul(PS[:, 7, 0:64], DAT[u % 2][:, k, :], DVT[:, k, h * 64:h * 64 + 64],
                                              start=k == 0, stop=k == TT - 1)
                    mm.then_inc(*q.mark("o", u))
                elif what == "gdn_conv":
                    s = step[1]
                    q, v, a = counter("pe_gdn"), counter("vec_gdnp"), counter("act_gdnp")
                    dst = {"nq": NQ, "nk": NK, "nv": NVF}[s]
                    if s != "nv":
                        pe.wait_ge(*counter("vec_fin").at("y", 2))
                        pe.wait_ge(*a.at("sq", s))
                        if s == "nk":
                            pe.wait_ge(*a.at("ln", "nq", 3))
                        for j in range(4):
                            nc.tensor.matmul(PS[:, 2 + j, :], bd64, NSQ[:, j // 2, (j % 2) * 512:(j % 2) * 512 + 512],
                                             start=True, stop=True).then_inc(*q.mark("ss", s, j))
                    if s != "nq":
                        pe.wait_ge(*(v.at("norm", "nk") if s == "nk" else a.at("silu", "nv")))
                        for j in range(4):
                            pe.wait_ge(*(a.at("ln", "nk", j) if s == "nk" else a.at("tm", "nk", j)))
                            for cc in range(2):
                                for t in range(2):
                                    c = 2 * j + cc
                                    tr = nc.tensor.transpose(PS[:, 2 + j, cc * 256 + t * P:cc * 256 + t * P + P],
                                                             dst[:, t, c * P:c * P + P], ident)
                            tr.then_inc(*q.mark("tm", s, j))
                elif what == "gdn_scal":
                    q, v, a = counter("pe_gdn"), counter("vec_gdnp"), counter("act_gdnp")
                    pe.wait_ge(*v.at("la"))
                    pe.wait_ge(*counter("vec_fin").at("y", 2))
                    for k, mats in enumerate(((inc_f, inc_b), (st_b, st_f), (ones, ones))):
                        for d in range(2):
                            mm = nc.tensor.matmul(PS[:, 6, 64 * k + 32 * d:64 * k + 32 * d + 32], mats[d],
                                                  n_la[:, 32 * d:32 * d + 32], start=True, stop=True)
                    mm.then_inc(*q.mark("gam"))
                elif what == "gdn":
                    i, part = step[1:]
                    q, v, a, po = (counter(f"{e}_gdn") for e in ("pe", "vec", "act", "pool"))
                    for d in range(2):
                        c = i if d == 0 else TT - 1 - i
                        cs = slice(c * P, c * P + P)
                        B0, B1, B2 = (PS[:, 2 + 3 * d + b, :].rearrange("p (h n) -> p h n", h=NH) for b in range(3))
                        inc = inc_b if d else inc_f
                        if part == 0:
                            if i == 0 and d == 0:
                                pe.wait_ge(*counter("act_gdnp").at("tm", "nv", 3))
                                pe.wait_ge(*counter("act_gdnp").at("eg"))
                            pe.wait_ge(*po.at("in", i, d))
                            if i:
                                pe.wait_ge(*v.at("state", i - 1, d))
                                pe.wait_ge(*(a if i - 1 < 4 else v).at("o", i - 1, d))
                            nc.tensor.matmul(B0[:, :, :], st_f if d else st_b, NX[d], start=True, stop=True)\
                                .then_inc(*q.mark("seg", i, d))
                            for h in range(NH):
                                mm = nc.tensor.matmul(B1[:, h, :], NKB[d][:, h, :], NK[:, h // 2, cs], start=True, stop=True)
                            mm.then_inc(*q.mark("kk", i, d))
                            for h in range(NH):
                                mm = nc.tensor.matmul(B2[:, h, :], NKB[d][:, h, :], NQ[:, h // 2, cs], start=True, stop=True)
                            mm.then_inc(*q.mark("qk", i, d))
                        elif part == 1:
                            pe.wait_ge(*v.at("lt", i, d))
                            for h in range(NH):
                                tr = nc.tensor.transpose(B0[:, h, :], NLT[d][:, h, :], ident)
                            tr.then_inc(*q.mark("l0", i, d))
                            for t in range(2):
                                mm = nc.tensor.matmul(B1[:, t, :], NWK[d][:, t, :], inc, start=True, stop=True)
                            mm.then_inc(*q.mark("gbc", i, d))
                            pe.wait_ge(*v.at("qt", i, d))
                        elif part < 8:
                            lv = part - 1
                            if part == 2:
                                pe.wait_ge(*v.at("x", i, d, 0))
                                pe.wait_ge(*po.at("z", i, d))
                            else:
                                pe.wait_ge(*v.at("z", i, d, lv - 1))
                            for h in range(NH):
                                mm = nc.tensor.matmul(B0[:, h, :], NLT[d][:, h, :], NX[d][:, h, :], start=True, stop=True)
                            mm.then_inc(*q.mark("y", i, d, lv))
                        else:
                            pe.wait_ge(*v.at("z", i, d, 6))
                            for h in range(NH):
                                mm = nc.tensor.matmul(PS[64 * (h % 2):64 * (h % 2) + 64, 2 + 3 * d, (h // 2) * P:(h // 2) * P + P],
                                                      NKE[d][:, h // 2, (h % 2) * 64:(h % 2) * 64 + 64], NZ_[d][:, h, :],
                                                      start=True, stop=True)
                            mm.then_inc(*q.mark("wk", i, d))
                    for d in range(2):
                        c = i if d == 0 else TT - 1 - i
                        B0, B1, B2 = (PS[:, 2 + 3 * d + b, :].rearrange("p (h n) -> p h n", h=NH) for b in range(3))
                        if 2 <= part < 8:
                            lv = part - 1
                            pe.wait_ge(*v.at("yn", i, d, lv))
                            if part == 2:
                                pe.wait_ge(*a.at("qd", i, d))
                            if lv < 6:
                                for h in range(NH):
                                    mm = nc.tensor.matmul(B1[:, h, :], NZ_[d][:, h, :], NY[d][:, h, :], start=True, stop=True)
                                mm.then_inc(*q.mark("xy", i, d, lv))
                            for h in range(NH):
                                mm = nc.tensor.matmul(B2[:, h, :], NY[d][:, h, :], NZ_[d][:, h, :], start=True, stop=True)
                            mm.then_inc(*q.mark("zy", i, d, lv))
                        elif part == 8:
                            for h in range(NH):
                                nc.tensor.matmul(PS[:, 3 + 3 * d, h * 64:h * 64 + 64], NZ_[d][:, h, :],
                                                 NVT[:, c, h * 64:h * 64 + 64], start=h == 0, stop=False)
                            pe.wait_ge(*a.at("wk", i, d))
                            if i:
                                pe.wait_ge(*v.at("state", i - 1, d))
                            else:
                                pe.wait_ge(*counter("pool_gdnp").at("s0"))
                            for t in range(2):
                                mm = nc.tensor.matmul(PS[:, 3 + 3 * d, t * P:t * P + P], NWK[d][:, t, :], NS[d][:, t, :],
                                                      start=False, stop=t == 1)
                            mm.then_inc(*q.mark("v", i, d))
                    if part == 8:
                        for d in range(2):
                            c = i if d == 0 else TT - 1 - i
                            pe.wait_ge(*v.at("vn", i, d))
                            for t in range(2):
                                mm = nc.tensor.matmul(PS[:, 4 + 3 * d, t * P:t * P + P], NKD[d][:, t, :], NVN[d][:, t, :],
                                                      start=True, stop=True)
                            mm.then_inc(*q.mark("u", i, d))
                            for t in range(2):
                                nc.tensor.matmul(PS[:, 2 + 3 * d, t * P:t * P + P], NQD[d][:, t, :], NS[d][:, t, :],
                                                 start=t == 0, stop=False)
                            for h in range(NH):
                                mm = nc.tensor.matmul(PS[:, 2 + 3 * d, h * 64:h * 64 + 64], NQT[d][:, h, :],
                                                      NVN[d].rearrange("p t n -> p (t n)")[:, h * 64:h * 64 + 64],
                                                      start=False, stop=h == NH - 1)
                            mm.then_inc(*q.mark("o", i, d))
                elif what == "xattn":
                    g = step[1]
                    h, half = divmod(g, 2)
                    q, v, a = (counter(f"{e}_xattn") for e in ("pe", "vec", "act"))
                    if g == 0:
                        pe.wait_ge(*counter("vec_evac").at(g_of["wq", 7, 1]))
                        pe.wait_ge(*counter("vec_norm").at("x1", "lo", TT - 1))
                    for j in range(4):
                        tt = 4 * half + j
                        if g and j % 2 == 0:
                            for jj in range(2):
                                pe.wait_ge(*a.at("p", g - 1, j + jj))
                        for k in range(2):
                            for x, y in ((0, 0), (0, 1), (1, 0)):
                                mm = nc.tensor.matmul(PS[:, 2 + j // 2, (j % 2) * 256:(j % 2) * 256 + 256],
                                                      XQ[x][:, 2 * h + k, tt * P:tt * P + P], XK[y][:, 2 * h + k, :],
                                                      start=(k == 0 and x + y == 0), stop=(k == 1 and x == 1))
                        if j % 2:
                            mm.then_inc(*q.mark("s", g, j // 2))
                    if g:
                        pe.wait_ge(*v.at("pt", g - 1, 1))
                    for j in range(4):
                        pe.wait_ge(*v.at("pn", g, j // 2))
                        for m in range(2):
                            tr = nc.tensor.transpose(PS[:, 4 + m, j * P:j * P + P], XP[g % 2][:, j, m * P:m * P + P], ident)
                    tr.then_inc(*q.mark("t", g))
                    pe.wait_ge(*v.at("pt", g, 1))
                    if g:
                        pe.wait_ge(*v.at("o", g - 1))
                    for j in range(2):
                        for m in range(2):
                            for x, y in ((0, 0), (0, 1), (1, 0)):
                                mm = nc.tensor.matmul(PS[:, 6 + j, :], XV[x][:, m, (2 * h + j) * P:(2 * h + j + 1) * P],
                                                      XPT[g % 2][y][:, m, :], start=(m == 0 and x + y == 0),
                                                      stop=(m == 1 and x == 1))
                        mm.then_inc(*q.mark("o", g, j))
                elif what == "router":
                    tt = step[1]
                    if tt == 0:
                        pe.wait_ge(wr_in, 16)
                        pe.wait_ge(*counter("act_xattn").at("o", 2 * NH - 1, 1))
                        pe.wait_ge(*counter("vec_xattn").at("o", 2 * NH - 1))
                    for b in range(2):
                        pe.wait_ge(*counter("act_norm").at("x2", "hi", tt, b))
                    for k in range(KT):
                        mm = nc.tensor.matmul(PS[:, 6, 36 * tt:36 * tt + 36], H3[:, k, tt * P:tt * P + P], WR[:, k, :],
                                              start=k == 0, stop=k == KT - 1)
                    mm.then_inc(*counter("pe_route").mark("logits", tt))
            q, v = counter("pe_route"), counter("vec_route")
            pe.wait_ge(*v.at("prefix", TT))
            nc.tensor.matmul(PS[:, 7, 0:TT * NE], st_f, r_a.rearrange("p t e -> p (t e)"), start=True, stop=False)
            nc.tensor.matmul(PS[:, 7, 0:TT * NE], ones, r_ap.rearrange("p t e -> p (t e)"), start=False, stop=True)\
                .then_inc(*q.mark("rank"))
            nc.tensor.matmul(PS[:, 6, 0:NE], ones, r_at, start=True, stop=True).then_inc(*q.mark("count"))
            pe.wait_ge(table_in, 16)
            nc.tensor.transpose(PS[:, 6, 64:64 + NBLK], TROWS[0:NBLK, :], ident[0:NBLK, 0:NBLK]).then_inc(*q.mark("table"))

            def x_tr(e, s, n):
                pe.wait_ge(rows_in[s], 16 * n + 16)
                after(pe, act_xt, e)
                after(pe, vec_xt, e)
                xs = XR[s].rearrange("p (q k) -> p k q", k=KT)
                for k in range(KT):
                    tr = nc.tensor.transpose(PS[:, k // 4, (k % 4) * P:(k % 4) * P + P], xs[:, k, :], ident)
                    if k % 4 == 3:
                        tr.then_inc(pe_xt, 1)

            def up(e, s, n):
                pe.wait_ge(act_xt, e + 1)
                pe.wait_ge(vec_xt, e + 1)
                pe.wait_ge(w1_in[s], 16 * n + 16)
                after(pe, vec_g, e)
                for k in range(KT):
                    mm = nc.tensor.matmul(PS[:, 2, :], XT[s][:, k, :], XW1[s][:, k, :], start=k == 0, stop=k == KT - 1)
                mm.then_inc(pe_a1, 1)
                pe.wait_ge(w3_in[s], 16 * n + 16)
                for k in range(KT):
                    mm = nc.tensor.matmul(PS[:, 3, :], XT[s][:, k, :], XW3[s][:, k, :], start=k == 0, stop=k == KT - 1)
                mm.then_inc(pe_a3, 1)

            def g_tr(e):
                pe.wait_ge(vec_g, e + 1)
                after(pe, act_gt, e)
                gs = GU.rearrange("p (q k) -> p k q", k=KE)
                for k in range(KE):
                    tr = nc.tensor.transpose(PS[:, 4, k * P:k * P + P], gs[:, k, :], ident)
                tr.then_inc(pe_gt, 1)

            def down(e, s, n):
                pe.wait_ge(act_gt, e + 1)
                pe.wait_ge(w2_in[s], 16 * n + 16)
                after(pe, act_y, e)
                after(pe, vec_y, e)
                for half in range(2):
                    for k in range(KE):
                        mm = nc.tensor.matmul(PS[:, 5 + half, :], GUT[:, k, :], XW2[s][:, k, half * 512:half * 512 + 512],
                                              start=k == 0, stop=k == KE - 1)
                    mm.then_inc(pe_y, 1)

            def period(e, s, n):
                up(e, s, n)
                if not (isinstance(e, int) and e == NE - 1):
                    x_tr(e + 1, 1 - s, n + s)
                if not (isinstance(e, int) and e == 0):
                    down(e - 1, 1 - s, n - 1 + s)
                g_tr(e)

            def block_beyond(e, j):
                x_tr(e, 0, j + NE // 2)
                up(e, 0, j + NE // 2)
                g_tr(e)
                down(e, 0, j + NE // 2)

            pe.wait_ge(*v.at("gates"))
            experts(pe, lambda: x_tr(0, 0, 0), period, lambda: down(NE - 1, 1, NE // 2 - 1))
            beyond(pe, block_beyond)

        @block.sync
        def _(sp):
            for step in schedule:
                if step[0] == "conv":
                    i = step[1]
                    c = chunk0[i]
                    for k in range(0, panels[i]["nk"], 2):
                        if c >= NLAND:
                            sp.wait_ge(*vec_lo.at(c - NLAND))
                        for src, k0, c0 in panels[i]["parts"]:
                            if k0 <= k < k0 + src.shape[1]:
                                sp.dma_start(LAND[c % NLAND][:, :, c0:c0 + src.shape[2]], src[:, k - k0:k - k0 + 2, :])\
                                    .then_inc(land[c % NLAND], 16)
                        c += 1
                elif step[0] == "norm_stats" and step[1] == "x2":
                    sp.wait_ge(*pe_mm.at(LAST_MM))
                    sp.wait_ge(*counter("pool_merge").at(g_of["up", 3, KT - 1, 1]))
                    sp.dma_start(WR, A["router_w"].rearrange("(k p) n -> p k n", p=P)).then_inc(wr_in, 16)
                    for s in range(2):
                        sp.dma_start(XW1[s], W1[:, s]).then_inc(w1_in[s], 16)
                        sp.dma_start(XW3[s], W3[:, s]).then_inc(w3_in[s], 16)
                        if s == 0:
                            sp.dma_start(XW2[s], W2[:, s]).then_inc(w2_in[s], 16)
                elif step[0] == "norm_tile" and step[1] == "x2":
                    tt = step[2]
                    sp.wait_ge(*counter("vec_norm").at("x2", "xh", tt))
                    sp.dma_start(XH_D[tt * P:tt * P + P, :], XH[tt % 2]).then_inc(xhat_out[tt % 2], 16)

            sp.wait_ge(*counter("pool_route").at("zeros"))
            sp.dma_start(TABLE.rearrange("(b p) o -> b (p o)", p=P), ZROW[0:NBLK, :]).then_inc(zero_out, 16)
            sp.wait_ge(*counter("vec_norm").at("x2", "xh", TT - 1))
            sp.dma_start(gain_row, A["gains"][4].partition_broadcast(P)).then_inc(gain_in, 16)
            sp.wait_ge(scattered, 16 * 2 * TT)
            sp.dma_start(TROWS[0:NBLK, :], TABLE.rearrange("(b p) o -> b (p o)", p=P)).then_inc(table_in, 16)

            def load(e, s, parts):
                if 1 in parts:
                    sp.dma_start(XW1[s].unsqueeze(1), W1[:, bass.ds(e, 1)]).then_inc(w1_in[s], 16)
                    sp.dma_start(XW3[s].unsqueeze(1), W3[:, bass.ds(e, 1)]).then_inc(w3_in[s], 16)
                if 2 in parts:
                    sp.dma_start(XW2[s].unsqueeze(1), W2[:, bass.ds(e, 1)]).then_inc(w2_in[s], 16)

            def ahead(e, s, n):
                if not (isinstance(e, int) and e >= NE - 2):
                    sp.wait_ge(pe_a3, e + 1)
                    load(e + 2, s, [1])
                if not (isinstance(e, int) and e >= NE - 1):
                    after(sp, pe_y, 2 * e)
                    load(e + 1, 1 - s, [2])

            def load_beyond(e, j):
                sp.wait_ge(pe_y, 2 * e)
                load(sp.value_load(OVI[0:1, bass.ds(j, 1)], min_val=0, max_val=NE - 1), 0, [1, 2])

            sp.wait_ge(*counter("vec_route").at("gates"))
            experts(sp, lambda: None, ahead, lambda: None)
            beyond(sp, load_beyond)
            for tt in range(TT):
                sp.wait_ge(*counter("vec_final").at("out", tt))
                sp.dma_start(out[tt * P:tt * P + P, :], XH_OUT[tt]).then_inc(out_done, 16)
            sp.wait_ge(out_done, 16 * TT)

        landed, n_land = {}, [0] * NLAND
        for i, p in enumerate(panels):
            for k in range(0, p["nk"], 2):
                c = chunk0[i] + k // 2
                n_land[c % NLAND] += 16 * sum(k0 <= k < k0 + s.shape[1] for s, k0, c0 in p["parts"])
                landed[c] = n_land[c % NLAND]

        @block.scalar
        def _(act):
            S = nc.scalar
            S.dma_start(cols, A["cols"]).then_inc(par_in, 16)
            S.dma_start(rows, A["rows"].partition_broadcast(P)).then_inc(par_in, 16)
            S.dma_start(LW, A["lru_w"]).then_inc(par_in, 16)
            S.dma_start(LRUP[0:32, :], A["lr_up"]).then_inc(par_in, 16)
            for step in schedule:
                what = step[0]
                if what == "conv":
                    i = step[1]
                    for j in range(panels[i]["nk"] // 2):
                        c = chunk0[i] + j
                        act.wait_ge(land[c % NLAND], landed[c])
                        if j == 0 and i >= 2:
                            act.wait_ge(*pe_mm.at(last_group[i - 2]))
                        wide = max(c0 + s.shape[2] for s, _, c0 in panels[i]["parts"])
                        S.activation(W[i % 2][0][:, 2 * j:2 * j + 2, 0:wide], LAND[c % NLAND][:, :, 0:wide],
                                     ACT.Copy, scale=WS).then_inc(*act_hi.mark(c))
                elif what == "evac":
                    i, g = step[1:]
                    n = gid[i, g]
                    kind = kind_of[n]
                    name = kind[0]
                    bank = PS[:, n % 2, :]
                    e = counter("act_evac")
                    act.wait_ge(*pe_mm.at(n))
                    if name == "gate":
                        if n >= 4 and kind_of[n - 4][0] == "gate":
                            act.wait_ge(*counter("vec_evac").at(n - 3))
                        if n == g_of["gate", 1, 0, 0]:
                            act.wait_ge(par_in, 16 * N_PAR)
                        S.activation(SG[gate_no[n] % 2], bank, ACT.Sigmoid, scale=1 / WS,
                                     bias=cols[:, C_MERGEB + 8 * kind[1] + kind[2]:C_MERGEB + 8 * kind[1] + kind[2] + 1])\
                            .then_inc(*e.mark(n))
                    elif name in ("wk", "wv", "wq"):
                        if name == "wk" and g == 0:
                            act.wait_ge(*counter("vec_pair").at("merged", KT - 1))
                        if n == g_of["wq", 0, 0]:
                            act.wait_ge(*pe_mm.at(g_of["mix", 3, 3]))
                        if name == "wq":
                            dst = XQ[0][:, kind[1], kind[2] * 512:kind[2] * 512 + 512]
                            src = bank
                        else:
                            src = bank.rearrange("p (a b) -> p a b", a=2)
                            q = kind[1]
                            dst = XK[0][:, 2 * q:2 * q + 2, :] if name == "wk" else XV[0][:, :, q * 256:q * 256 + 256]
                        S.activation(dst, src, ACT.Copy, scale=1 / WS).then_inc(*e.mark(n))
                    elif name not in ("up", "mix", "wo"):
                        if name in ("gv", "gog", "dv", "nz"):
                            dst = {"gv": GVT, "gog": GOGT, "dv": DVT, "nz": NZT}[name][:, 2 * kind[1]:2 * kind[1] + 2, :]
                            src = bank.rearrange("p (a b) -> p a b", a=2)
                        elif name == "nba":
                            dst, src = NBA_, bank[:, 0:P]
                        elif name == "glr":
                            dst, src = GLRT[0:32, kind[2] * 512:kind[2] * 512 + 512], bank[0:32, :]
                        elif name in ("lx", "nq", "nk", "nv"):
                            base = LXP if name == "lx" else RAW
                            dst, src = base[:, kind[1], 2 + kind[2] * 512:2 + kind[2] * 512 + 512], bank
                        else:
                            base = {"lg": LG_, "gqk": GQK, "dq": DQT, "dk": DKT}[name]
                            dst, src = base[:, kind[1], kind[2] * 512:kind[2] * 512 + 512], bank
                        if g == 0:
                            if name == "lx":
                                act.wait_ge(*counter("pe_norm").at("x", "tr", TT - 1))
                            elif name in ("gqk", "gv", "glr"):
                                act.wait_ge(*counter("vec_fin").at("y", 1))
                            elif name == "gog":
                                act.wait_ge(*counter("pe_gla").at("o", 1, TT - 1))
                            elif name in ("dq", "dk", "dv"):
                                act.wait_ge(*counter("pe_fin").at("tr", "gla", 1))
                                act.wait_ge(*counter("vec_fin").at("y", 0))
                            elif name == "nq":
                                act.wait_ge(*counter("vec_fin").at("y", 2))
                            elif name in ("nk", "nv"):
                                act.wait_ge(*counter("vec_gdnp").at("conv", {"nk": "nq", "nv": "nk"}[name], 1))
                            elif name == "nz":
                                act.wait_ge(*counter("pe_gdn").at("o", TT - 1, 1))
                                act.wait_ge(*counter("vec_gdn").at("state", TT - 1, 1))
                        S.activation(dst, src, ACT.Copy, scale=1 / WS).then_inc(*e.mark(n))
                elif what == "norm_stats":
                    which, n = step[1:]
                    a = counter("act_norm")
                    if which == "x":
                        S.dma_start(gain_row, A["gains"][0].partition_broadcast(P)).then_inc(gain_in, 16)
                        for tt in range(TT):
                            S.dma_start(X[:, tt, :], A["x"][tt * P:tt * P + P, :]).then_inc(x_in[tt], 16)
                        src = X
                    elif which == "mem":
                        act.wait_ge(*counter("vec_pair").at("merged", KT - 1))
                        act.wait_ge(*counter("pool_merge").at(g_of["up", 3, KT - 1, 1]))
                        act.wait_ge(*counter("vec_evac").at(g_of["up", 3, KT - 1, 1]))
                        S.dma_start(gain_row, A["gains"][1].partition_broadcast(P)).then_inc(gain_in, 16)
                        S.dma_start(MEM[:, 0, :], A["mem"][0:P, :]).then_inc(x_in[0], 16)
                        S.dma_start(MEM[:, 1, :], A["mem"][P:2 * P, :]).then_inc(x_in[1], 16)
                        src = MEM
                    else:
                        act.wait_ge(*counter("vec_norm").at(*(("mem", "xh", 1) if which == "x1" else ("x1", "xh", TT - 1))))
                        S.dma_start(gain_row, A["gains"][GAINS.index(which)].partition_broadcast(P)).then_inc(gain_in, 16)
                        src = X
                    for tt in range(n):
                        if which == "x":
                            act.wait_ge(x_in[tt], 16)
                        elif which == "mem":
                            act.wait_ge(x_in[tt], 32)
                        elif tt == 0:
                            act.wait_ge(*counter("vec_evac").at(g_of["mix" if which == "x1" else "wo", 3, 3]))
                        if tt or which != "x":
                            act.wait_ge(*a.last())
                        S.activation(SQ, src[:, tt, :], ACT.Square, accum_out=norm_ss[:, tt:tt + 1]).then_inc(*a.mark(which, "sq", tt))
                    act.wait_ge(*a.last())
                    act.wait_ge(*counter("pool_const").at("cols"))
                    S.activation(norm_r[:, 0:n], norm_ss[:, 0:n], ACT.Ln, scale=1 / D, bias=eps_col).then_inc(*a.mark(which, "ln"))
                    act.wait_ge(*a.last())
                    S.activation(norm_r[:, 0:n], norm_r[:, 0:n], ACT.Exp, scale=-0.5).then_inc(*a.mark(which, "r"))
                elif what == "norm_tile":
                    which, tt = step[1:]
                    dst = {"x": H, "mem": MEMT, "x1": H2, "x2": (H3,)}[which]
                    a = counter("act_norm")
                    act.wait_ge(*counter("pe_norm").at(which, "tr", tt))
                    if which == "mem" and tt == 0:
                        act.wait_ge(*counter("vec_pair").at("merged", KT - 1))
                    for b in range(2):
                        S.activation(dst[0][:, 4 * b:4 * b + 4, tt * P:tt * P + P],
                                     PS[:, 2 + 2 * (tt % 2) + b, :].rearrange("p (k n) -> p k n", k=4), ACT.Copy)\
                            .then_inc(*a.mark(which, "hi", tt, b))
                elif what == "lru_pre":
                    a, v = counter("act_lru"), counter("vec_lru")
                    act.wait_ge(par_in, 16 * N_PAR)
                    act.wait_ge(*counter("vec_lru").at("nabs"))
                    S.activation(l_e, l_t, ACT.Exp).then_inc(*a.mark("e"))
                elif what == "lru_dir":
                    d, t = step[1:]
                    a, v, q = counter("act_lru"), counter("vec_lru"), counter("pe_lru")
                    k = 2 * d + t
                    act.wait_ge(*q.at("gate", d, t, 0))
                    if k:
                        dp, tp = divmod(k - 1, 2)
                        act.wait_ge(*v.at("hs", dp, tp))
                        act.wait_ge(*counter("pool_lru").at("iu", dp, tp))
                    S.activation(LR_, PS[:, 2:4, :].rearrange("p a b -> p (a b)"), ACT.Sigmoid,
                                 bias=cols[:, C_LBA + k:C_LBA + k + 1]).then_inc(*a.mark("r", d, t))
                    act.wait_ge(*q.at("gate", d, t, 1))
                    S.activation(LI_, PS[:, 4:6, :].rearrange("p a b -> p (a b)"), ACT.Sigmoid,
                                 bias=cols[:, C_LBX + k:C_LBX + k + 1]).then_inc(*a.mark("i", d, t))
                    act.wait_ge(*v.at("coef"))
                    act.wait_ge(*a.last())
                    S.activation(LA_, LR_, ACT.Exp, scale=l_nc[:, k:k + 1]).then_inc(*a.mark("a", d, t))
                    S.activation(LTH, LR_, ACT.Tanh, scale=l_pc[:, k:k + 1]).then_inc(*a.mark("th", d, t))
                    act.wait_ge(*v.at("m", d, t))
                    S.activation(LM, LM, ACT.Sqrt).then_inc(*a.mark("s", d, t))
                elif what == "lru_fin":
                    a, v = counter("act_lru"), counter("vec_lru")
                    act.wait_ge(*counter("act_evac").at(g_of["lg", 1, 1]))
                    S.activation(LG_[:, :, :], LG_[:, :, :], ACT.Gelu_apprx_tanh).then_inc(*a.mark("gelu"))
                    act.wait_ge(*v.at("y32"))
                    act.wait_ge(spare_rows, 16)
                    S.activation(Y[0][0], LHS, ACT.Copy).then_inc(*a.mark("yhi"))
                elif what == "gla_pre":
                    d = step[1]
                    a, v, q = counter("act_gla"), counter("vec_gla"), counter("pe_gla")
                    act.wait_ge(*v.at("z", d))
                    S.activation(TB, TA, ACT.Abs).then_inc(*a.mark("abs", d))
                    act.wait_ge(*a.last())
                    S.activation(TB, TB, ACT.Exp, scale=-1.0).then_inc(*a.mark("exp", d))
                    act.wait_ge(*a.last())
                    S.activation(TB, TB, ACT.Ln, bias=1.0).then_inc(*a.mark("ln", d))
                    act.wait_ge(*v.at("td", d))
                    S.activation(g_em, g_mid, ACT.Exp, scale=-1 / 16).then_inc(*a.mark("em", d))
                    S.activation(g_ee, g_end, ACT.Exp, scale=-1 / 16).then_inc(*a.mark("ee", d))
                    S.activation(TC, TA, ACT.Exp, scale=1 / 16).then_inc(*a.mark("e2", d))
                    S.activation(TB, TA, ACT.Exp, scale=-1 / 16).then_inc(*a.mark("e1", d))
                    for b in range(2):
                        act.wait_ge(*q.at("ktt", d, b))
                        if d and b == 0:
                            act.wait_ge(*q.at("u", 0, TT - 2))
                        S.activation(KTM[:, 4 * b:4 * b + 4, :], PS[:, 6 + b, :].rearrange("p (c n) -> p c n", c=4), ACT.Copy)\
                            .then_inc(*a.mark("ktm", d, b))
                elif what == "gla_chunk":
                    d, i = step[1:]
                    if d == 0:
                        act.wait_ge(*counter("pe_gla").at("o", d, i))
                        S.activation(GO[:, i, :], PS[:, 4 + i % 2, 0:256], ACT.Copy).then_inc(*counter("act_gla").mark("o", d, i))
                elif what == "fin":
                    br = step[1]
                    f = FIN[br]
                    a, v = counter("act_fin"), counter("vec_fin")
                    if br == "diff":
                        act.wait_ge(*counter("act_diff").at("o", NH * TT - 1))
                    if br == "gdn":
                        act.wait_ge(*counter("act_gdn").at("o", 3, 1))
                        act.wait_ge(*counter("vec_gdn").at("o", TT - 1, 1))
                        act.wait_ge(*counter("vec_gdn").at("state", TT - 1, 1))
                    if br == "gla":
                        act.wait_ge(*counter("vec_gla").at("o", 1, TT - 1))
                        act.wait_ge(*counter("pe_gla").at("o", 1, TT - 1))
                    S.activation(f["tmp"], f["o"], ACT.Square).then_inc(*a.mark("sq", br))
                    if f["gate"] is not None:
                        act.wait_ge(*counter("act_evac").at(g_of[{"gla": "gog", "gdn": "nz"}[br], 3]))
                        S.activation(f["gate"], f["gate"], ACT.Silu).then_inc(*a.mark("silu", br))
                    act.wait_ge(*v.at("ss", br))
                    S.activation(fin_r, fin_ss, ACT.Ln, scale=1 / 64, bias=eps_col).then_inc(*a.mark("ln", br))
                    act.wait_ge(*a.last())
                    S.activation(fin_r, fin_r, ACT.Exp, scale=-0.5).then_inc(*a.mark("r", br))
                elif what == "fin_tr":
                    br = step[1]
                    a = counter("act_fin")
                    slot = FIN[br]["y"]
                    if br != "gla":
                        act.wait_ge(*pe_mm.at(g_of["up", {"diff": 1, "gdn": 0}[br], KT - 1, 1]))
                    for ft in range(2):
                        act.wait_ge(*counter("pe_fin").at("tr", br, ft))
                        S.activation(Y[slot][0][:, ft, :], PS[:, 2 + 2 * ft:4 + 2 * ft, :].rearrange("p a b -> p (a b)"),
                                     ACT.Copy).then_inc(*a.mark("yhi", br, ft))
                elif what == "diff_pre":
                    a = counter("act_diff")
                    act.wait_ge(*counter("pool_diff").at("iota"))
                    S.activation(DW, DWH.bitcast(I32), ACT.Abs).then_inc(*a.mark("w"))
                    act.wait_ge(*counter("vec_diff").at("dots"))
                    S.activation(d_lam[:, 0:2], d_lam[:, 0:2], ACT.Exp).then_inc(*a.mark("lam"))
                elif what == "diff_qk":
                    u = step[1]
                    a, v = counter("act_diff"), counter("vec_diff")
                    act.wait_ge(*v.at("nm", u))
                    if u >= 2:
                        act.wait_ge(*v.at("comb", u - 2))
                    for m in range(2):
                        S.activation(DS[u % 2][:, m, :], DS[u % 2][:, m, :], ACT.Exp, scale=32 ** -0.5,
                                     bias=d_mx[u % 2][:, m:m + 1], accum_out=d_l[u % 2][:, m:m + 1])\
                            .then_inc(*a.mark("p", u, m))
                elif what == "diff_pv":
                    u = step[1]
                    h, qt = divmod(u, TT)
                    a, q = counter("act_diff"), counter("pe_diff")
                    act.wait_ge(*q.at("tr", u, 0))
                    if u >= 2:
                        act.wait_ge(*q.at("o", u - 2))
                    S.activation(DAT[u % 2][:, 0:4, :], PS[:, 6, :].rearrange("p (k n) -> p k n", k=4), ACT.Copy)\
                        .then_inc(*a.mark("at", u, 0))
                    act.wait_ge(*q.at("o", u))
                    S.activation(DO[:, qt, h * 64:h * 64 + 64], PS[:, 7, 0:64], ACT.Copy, scale=d_rl[u % 2][:, 0:1])\
                        .then_inc(*a.mark("o", u))
                elif what == "gdn_conv":
                    s = step[1]
                    a, v, q = counter("act_gdnp"), counter("vec_gdnp"), counter("pe_gdn")
                    dst = {"nq": NQ, "nk": NK, "nv": NVF}[s]
                    act.wait_ge(*v.at("conv", s, 1))
                    S.activation(dst, dst, ACT.Silu).then_inc(*a.mark("silu", s))
                    if s != "nv":
                        act.wait_ge(*a.last())
                        if s == "nk":
                            act.wait_ge(*v.at("norm", "nq"))
                        S.activation(NSQ, dst, ACT.Square).then_inc(*a.mark("sq", s))
                        for j in range(4):
                            act.wait_ge(*q.at("ss", s, j))
                            if j == 0:
                                act.wait_ge(*q.at("ss", s, 3))
                            S.activation(NSQ[:, j // 2, (j % 2) * 512:(j % 2) * 512 + 512], PS[:, 2 + j, :], ACT.Ln,
                                         bias=eps_col).then_inc(*a.mark("ln", s, j))
                        act.wait_ge(*a.last())
                        S.activation(NSQ, NSQ, ACT.Exp, scale=-0.5, bias=lneighth if s == "nq" else 0.0).then_inc(*a.mark("rn", s))
                    if s != "nq":
                        for j in range(4):
                            act.wait_ge(*q.at("tm", s, j))
                            S.activation((NKT if s == "nk" else NVT)[:, 2 * j:2 * j + 2, :],
                                         PS[:, 2 + j, :].rearrange("p (c n) -> p c n", c=2), ACT.Copy).then_inc(*a.mark("tm", s, j))
                elif what == "gdn_scal":
                    a, v = counter("act_gdnp"), counter("vec_gdnp")
                    ba = NBA_.rearrange("p (c k d h) -> p k d c h", c=TT, k=2, d=2)
                    act.wait_ge(*counter("act_evac").at(g_of["nba", 0]))
                    for d in range(2):
                        S.activation(BETA[:, d], ba[:, 0, d], ACT.Sigmoid).then_inc(*a.mark("beta", d))
                    act.wait_ge(*v.at("nabs"))
                    S.activation(n_t[1], n_t[1], ACT.Exp).then_inc(*a.mark("e"))
                    S.activation(n_al, rows[:, R_ALOG:R_ALOG + 8], ACT.Exp).then_inc(*a.mark("al"))
                    act.wait_ge(*counter("pe_gdn").at("gam"))
                    S.activation(n_eg, PS[:, 6, 0:192], ACT.Exp).then_inc(*a.mark("eg"))
                elif what == "gdn":
                    i, part = step[1:]
                    a, v, q = (counter(f"{e}_gdn") for e in ("act", "vec", "pe"))
                    for d in range(2):
                        c = i if d == 0 else TT - 1 - i
                        if part == 0:
                            act.wait_ge(*q.at("seg", i, d))
                            S.activation(NY[d], PS[:, 2 + 3 * d, :].rearrange("p (h n) -> p h n", h=NH), ACT.Exp)\
                                .then_inc(*a.mark("dt", i, d))
                        elif part == 1:
                            act.wait_ge(*q.at("gbc", i, d))
                            S.activation(NQD[d], PS[:, 3 + 3 * d, 0:256].rearrange("p (t n) -> p t n", t=2), ACT.Exp)\
                                .then_inc(*a.mark("qd", i, d))
                        elif part == 8:
                            act.wait_ge(*q.at("wk", i, d))
                            S.activation(NWK[d], PS[:, 2 + 3 * d, 0:256].rearrange("p (t n) -> p t n", t=2), ACT.Copy, scale=-1.0)\
                                .then_inc(*a.mark("wk", i, d))
                    if part == 8 and i < 4:
                        for d in range(2):
                            c = i if d == 0 else TT - 1 - i
                            act.wait_ge(*q.at("o", i, d))
                            S.activation(NO[:, c, :], PS[:, 2 + 3 * d, 0:256], ACT.Copy).then_inc(*a.mark("o", i, d))
                elif what == "merged_pair":
                    a = counter("act_pair")
                    act.wait_ge(*counter("pe_fin").at("tr", "gdn", 1))
                    act.wait_ge(*counter("vec_fin").at("y", 3))
                    for tt in range(TT):
                        S.dma_start(X[:, tt, :], A["x"][tt * P:tt * P + P, :]).then_inc(x_again, 16)
                    act.wait_ge(*counter("pool_merge").at(g_of["up", 3, KT - 1, 1]))
                    for k in range(KT):
                        S.activation(MP[0][:, k, :], merged[:, k, :], ACT.Copy).then_inc(*a.mark("merged", k))
                elif what == "xattn":
                    g = step[1]
                    a, v, q = (counter(f"{e}_xattn") for e in ("act", "vec", "pe"))
                    for j in range(4):
                        act.wait_ge(*v.at("mx", g, j // 2))
                        if j == 0 and g >= 2:
                            act.wait_ge(*q.at("t", g - 2))
                        S.activation(XP[g % 2][:, j, :], PS[:, 2 + j // 2, (j % 2) * 256:(j % 2) * 256 + 256], ACT.Exp,
                                     scale=1 / 16, bias=x_mx[g % 2][:, j:j + 1], accum_out=x_l[g % 2][:, j:j + 1])\
                            .then_inc(*a.mark("p", g, j))
                    for m in range(2):
                        act.wait_ge(*q.at("t", g))
                        if g >= 2 and m == 0:
                            act.wait_ge(*q.at("o", g - 2, 1))
                        S.activation(XPT[g % 2][0][:, m, :], PS[:, 4 + m, :], ACT.Copy).then_inc(*a.mark("pt", g, m))
                    h, half = divmod(g, 2)
                    for j in range(2):
                        act.wait_ge(*q.at("o", g, j))
                        S.activation(XO[0][:, 2 * h + j, half * 512:half * 512 + 512], PS[:, 6 + j, :], ACT.Copy)\
                            .then_inc(*a.mark("o", g, j))


            a, v = counter("act_route"), counter("vec_route")
            act.wait_ge(*v.at("group_diff"))
            S.activation(r_g4, r_g4, ACT.Exp).then_inc(*a.mark("group_exp"))
            act.wait_ge(*v.at("top_diff"))
            S.activation(r_ex, r_x, ACT.Exp).then_inc(*a.mark("top_exp"))

            def silu(e):
                act.wait_ge(pe_a1, e + 1)
                after(act, vec_g, e)
                S.activation(SL, PS[:, 2, :], ACT.Silu).then_inc(act_sl, 1)

            def x_copy(e, s):
                act.wait_ge(pe_xt, 2 * e + 1)
                S.activation(XT[s][:, 0:4, :], PS[:, 0, :].rearrange("p (k n) -> p k n", k=4), ACT.Copy).then_inc(act_xt, 1)

            def y_copy(e, s, n):
                act.wait_ge(pe_y, 2 * e + 1)
                after(act, y_out[s], 16 * n)
                S.activation(YB[s][:, 0, :], PS[:, 5, :], ACT.Copy).then_inc(act_y, 1)
                act.wait_ge(act_y, e + 1)
                act.wait_ge(vec_y, e + 1)
                S.dma_start(YROWS[bass.ds(e * P, P), :], YB[s].rearrange("p a b -> p (a b)")).then_inc(y_out[s], 16)

            def g_copy(e):
                act.wait_ge(pe_gt, e + 1)
                S.activation(GUT, PS[:, 4, :].rearrange("p (k n) -> p k n", k=KE), ACT.Copy).then_inc(act_gt, 1)

            def period(e, s, n):
                silu(e)
                if not (isinstance(e, int) and e == NE - 1):
                    x_copy(e + 1, 1 - s)
                if not (isinstance(e, int) and e == 0):
                    y_copy(e - 1, 1 - s, n - 1 + s)
                g_copy(e)

            def block_beyond(e, j):
                x_copy(e, 0)
                silu(e)
                g_copy(e)
                y_copy(e, 0, j + NE // 2)

            act.wait_ge(*v.at("gates"))
            experts(act, lambda: x_copy(0, 0), period, lambda: y_copy(NE - 1, 1, NE // 2 - 1))
            beyond(act, block_beyond)
            a, v = counter("act_final"), counter("vec_final")
            for tt in range(TT):
                act.wait_ge(*v.at("sum", tt))
                S.activation(YG[1][:, tt, :], X[:, tt, :], ACT.Square, accum_out=f_ss[:, tt:tt + 1]).then_inc(*a.mark("sq", tt))
                act.wait_ge(*a.last())
                S.activation(f_r[:, tt:tt + 1], f_ss[:, tt:tt + 1], ACT.Ln, scale=1 / D, bias=eps_col).then_inc(*a.mark("ln", tt))
                act.wait_ge(*a.last())
                S.activation(f_r[:, tt:tt + 1], f_r[:, tt:tt + 1], ACT.Exp, scale=-0.5).then_inc(*a.mark("r", tt))

        @block.vector
        def _(dve):
            V = nc.vector

            def log1p(x, z, q, s, c, key, half=1.0):
                dve.wait_ge(*c.last())
                V.tensor_scalar(z, x, 2.0, None, ALU.add).then_inc(*c.mark(key, "d"))
                dve.wait_ge(*c.last())
                V.reciprocal(z, z).then_inc(*c.mark(key, "r"))
                dve.wait_ge(*c.last())
                V.tensor_tensor(z, z, x, ALU.mult).then_inc(*c.mark(key, "z"))
                dve.wait_ge(*c.last())
                V.tensor_tensor(q, z, z, ALU.mult).then_inc(*c.mark(key, "q"))
                dve.wait_ge(*c.last())
                V.tensor_scalar(s, q, 1 / 17, None, ALU.mult).then_inc(*c.mark(key, 17))
                for n in (15, 13, 11, 9, 7, 5, 3):
                    dve.wait_ge(*c.last())
                    V.scalar_tensor_tensor(s, s, 1 / n, q, ALU.add, ALU.mult).then_inc(*c.mark(key, n))
                dve.wait_ge(*c.last())
                V.scalar_tensor_tensor(s, s, 1.0, z, ALU.add, ALU.mult).then_inc(*c.mark(key, 1))
                dve.wait_ge(*c.last())
                V.tensor_scalar(s, s, 2.0 / half, None, ALU.mult).then_inc(*c.mark(key, "s"))
                dve.wait_ge(*c.last())

            for step in schedule:
                what = step[0]
                if what == "conv":
                    i = step[1]
                    for j in range(panels[i]["nk"] // 2):
                        c = chunk0[i] + j
                        wide = max(c0 + s.shape[2] for s, _, c0 in panels[i]["parts"])
                        dve.wait_ge(*act_hi.at(c))
                        V.scalar_tensor_tensor(W[i % 2][1][:, 2 * j:2 * j + 2, 0:wide], LAND[c % NLAND][:, :, 0:wide], WS,
                                               W[i % 2][0][:, 2 * j:2 * j + 2, 0:wide], ALU.mult, ALU.subtract)\
                            .then_inc(*vec_lo.mark(c))
                elif what == "evac":
                    i, g = step[1:]
                    n = gid[i, g]
                    kind = kind_of[n]
                    name = kind[0]
                    bank = PS[:, n % 2, :]
                    e = counter("vec_evac")
                    if name == "up":
                        first = kind[1] == 1
                        dst = merged[:, kind[2], kind[3] * 512:kind[3] * 512 + 512]
                        o = gate_no[n] - 1
                        dve.wait_ge(*counter("act_evac").at(n - 1))
                        dve.wait_ge(*pe_mm.at(n))
                        if not first:
                            dst = SG[2 + o % 2]
                            if n >= 4 and kind_of[n - 4][0] == "up" and kind_of[n - 4][1] != 1:
                                dve.wait_ge(*counter("pool_merge").at(n - 4))
                            elif o >= 34 and n >= 4 and kind_of[n - 4][0] != "up":
                                prev = [m for m in range(n) if kind_of[m][0] == "up"][-2]
                                dve.wait_ge(*counter("pool_merge").at(prev))
                        V.scalar_tensor_tensor(dst, bank, 1 / WS, SG[o % 2], ALU.mult, ALU.mult).then_inc(*e.mark(n))
                    elif name in ("mix", "wo"):
                        dve.wait_ge(*pe_mm.at(n))
                        if n == g_of["mix", 0, 0]:
                            dve.wait_ge(x_again, 16 * TT)
                        xs = X[:, 2 * kind[2]:2 * kind[2] + 2, kind[1] * 256:kind[1] * 256 + 256]
                        V.scalar_tensor_tensor(xs, bank.rearrange("p (a b) -> p a b", a=2), 1 / WS, xs, ALU.mult, ALU.add)\
                            .then_inc(*e.mark(n))
                    elif name in ("wk", "wv", "wq"):
                        dve.wait_ge(*counter("act_evac").at(n))
                        if name == "wq":
                            hi, lo = (XQ[s][:, kind[1], kind[2] * 512:kind[2] * 512 + 512] for s in range(2))
                            src = bank
                        else:
                            q = kind[1]
                            src = bank.rearrange("p (a b) -> p a b", a=2)
                            hi, lo = ((XK[s][:, 2 * q:2 * q + 2, :] if name == "wk" else XV[s][:, :, q * 256:q * 256 + 256])
                                      for s in range(2))
                        V.scalar_tensor_tensor(lo, src, 1 / WS, hi, ALU.mult, ALU.subtract).then_inc(*e.mark(n))
                elif what == "norm_tile":
                    which, tt = step[1:]
                    v, a = counter("vec_norm"), counter("act_norm")
                    src = MEM if which == "mem" else X
                    dst = {"x": H, "mem": MEMT, "x1": H2, "x2": None}[which]
                    if tt == 0:
                        dve.wait_ge(gain_in, 16 * (GAINS.index(which) + 1))
                        dve.wait_ge(*a.at(which, "r"))
                    if tt >= 2:
                        dve.wait_ge(*counter("pe_norm").at(which, "tr", tt - 2))
                        if which == "x2":
                            dve.wait_ge(xhat_out[tt % 2], 16 * (tt // 2))
                    V.scalar_tensor_tensor(XH[tt % 2], src[:, tt, :], norm_r[:, tt:tt + 1], gain_row, ALU.mult, ALU.mult)\
                        .then_inc(*v.mark(which, "xh", tt))
                    for b in range(0 if which == "x2" else 2):
                        dve.wait_ge(*a.at(which, "hi", tt, b))
                        ts = slice(tt * P, tt * P + P)
                        V.tensor_tensor(dst[1][:, 4 * b:4 * b + 4, ts],
                                        PS[:, 2 + 2 * (tt % 2) + b, :].rearrange("p (k n) -> p k n", k=4),
                                        dst[0][:, 4 * b:4 * b + 4, ts], ALU.subtract)\
                            .then_inc(*v.mark(*((which, "lo", tt) if b else (which, "lo0", tt))))
                elif what == "lru_pre":
                    v = counter("vec_lru")
                    dve.wait_ge(par_in, 16 * N_PAR)
                    lam = cols[:, C_LAM:C_LAM + 4]
                    V.tensor_scalar(l_q, lam, -1.0, None, ALU.mult).then_inc(*v.mark("neg"))
                    dve.wait_ge(*v.last())
                    V.tensor_tensor(l_t, lam, l_q, ALU.min).then_inc(*v.mark("nabs"))
                    dve.wait_ge(*counter("act_lru").at("e"))
                    log1p(l_e, l_z, l_q, l_s, v, "log1p")
                    V.tensor_scalar(l_q, lam, -1.0, 0.0, ALU.mult, ALU.max).then_inc(*v.mark("relu"))
                    dve.wait_ge(*v.last())
                    V.tensor_tensor(l_s, l_s, l_q, ALU.add).then_inc(*v.mark("sp"))
                    dve.wait_ge(*v.last())
                    V.tensor_scalar(l_pc, l_s, 8.0, None, ALU.mult).then_inc(*v.mark("pc"))
                    V.tensor_scalar(l_nc, l_s, -8.0, None, ALU.mult).then_inc(*v.mark("coef"))
                    dve.wait_ge(*counter("act_evac").at(g_of["lx", 1, 1]))
                    dve.wait_ge(*counter("pool_const").at("lxpad"))
                    for t in range(2):
                        w = cols[:, C_LCW + 4 * t:C_LCW + 4 * t + 4]
                        V.tensor_scalar(LU[:, t, :], LXP[:, t, 0:T], w[:, 0:1], cols[:, C_LCB + t:C_LCB + t + 1], ALU.mult, ALU.add)\
                            .then_inc(*v.mark("u0", t))
                        for j in range(1, 4):
                            dve.wait_ge(*v.last())
                            V.scalar_tensor_tensor(LU[:, t, :], LXP[:, t, j:j + T], w[:, j:j + 1], LU[:, t, :], ALU.mult, ALU.add)\
                                .then_inc(*v.mark(*(("u", t) if j == 3 else ("uj", t, j))))
                elif what == "lru_dir":
                    d, t = step[1:]
                    v, a = counter("vec_lru"), counter("act_lru")
                    dve.wait_ge(*a.at("th", d, t))
                    V.tensor_tensor(LM, LA_, LA_, ALU.mult).then_inc(*v.mark("a2", d, t))
                    dve.wait_ge(*v.last())
                    V.scalar_tensor_tensor(LM, LM, 1.0, LTH, ALU.add, ALU.mult).then_inc(*v.mark("m", d, t))
                    dve.wait_ge(*a.at("s", d, t))
                    dve.wait_ge(*counter("pool_lru").at("iu", d, t))
                    V.tensor_tensor(LXI, LM, LI_, ALU.mult).then_inc(*v.mark("xin", d, t))
                    dve.wait_ge(*v.last())
                    if d == 0:
                        V.tensor_tensor_scan(LHS[:, t, :], LA_, LXI, 0.0, ALU.mult, ALU.add).then_inc(*v.mark("hs", d, t))
                    else:
                        V.tensor_tensor_scan(LH1[:, ::-1], LA_[:, ::-1], LXI[:, ::-1], 0.0, ALU.mult, ALU.add)\
                            .then_inc(*v.mark("h1", d, t))
                        dve.wait_ge(*v.last())
                        V.tensor_tensor(LHS[:, t, :], LHS[:, t, :], LH1, ALU.add).then_inc(*v.mark("hs", d, t))
                elif what == "lru_fin":
                    v, a = counter("vec_lru"), counter("act_lru")
                    dve.wait_ge(*a.at("gelu"))
                    dve.wait_ge(*v.last())
                    V.tensor_tensor(LHS, LHS, LG_, ALU.mult).then_inc(*v.mark("y32"))
                    dve.wait_ge(*a.at("yhi"))
                    V.tensor_tensor(Y[0][1], LHS, Y[0][0], ALU.subtract).then_inc(*counter("vec_fin").mark("y", 1))
                elif what == "gla_pre":
                    d = step[1]
                    v, a, q = counter("vec_gla"), counter("act_gla"), counter("pe_gla")
                    dve.wait_ge(*q.at("z", d))
                    if d:
                        dve.wait_ge(*q.at("o", 0, TT - 1))
                    V.tensor_scalar(TA, PS[:, 2:4, :].rearrange("p a b -> p (a b)"), cols[:, C_LRB + d:C_LRB + d + 1], -1.0,
                                    ALU.add, ALU.mult).then_inc(*v.mark("z", d))
                    dve.wait_ge(*a.at("ln", d))
                    dve.wait_ge(*v.last())
                    V.scalar_tensor_tensor(TA, TA, 0.0, TB, ALU.max, ALU.add).then_inc(*v.mark("sp", d))
                    dve.wait_ge(*v.last())
                    for c in range(TT):
                        cs = slice(c * P, c * P + P)
                        if d == 0:
                            i_ = V.tensor_tensor_scan(TB[:, cs], ones, TA[:, cs], 0.0, ALU.mult, ALU.add)
                        else:
                            i_ = V.tensor_tensor_scan(TB[:, cs][:, ::-1], ones, TA[:, cs][:, ::-1], 0.0, ALU.mult, ALU.add)
                        i_.then_inc(*v.mark("scan", d, c))
                    dve.wait_ge(*v.last())
                    sums = TB.rearrange("p (c n) -> p c n", c=TT)
                    mid, end = (63, 127) if d == 0 else (64, 0)
                    V.tensor_copy(g_mid, sums[:, :, mid]).then_inc(*v.mark("mid", d))
                    V.tensor_copy(g_end, sums[:, :, end]).then_inc(*v.mark("end", d))
                    dve.wait_ge(*v.at("mid", d))
                    V.tensor_tensor(TA.rearrange("p (c n) -> p c n", c=TT), sums, bc(g_mid.unsqueeze(2), P, TT, P), ALU.subtract)\
                        .then_inc(*v.mark("td", d))
                    dve.wait_ge(*a.at("e2", d))
                    V.tensor_tensor(TC, TC, GQK[:, 1, :], ALU.mult).then_inc(*v.mark("kt", d))
                    dve.wait_ge(*a.at("e1", d))
                    if d == 0:
                        dve.wait_ge(*counter("pool_gla").at("qbd0"))
                    V.scalar_tensor_tensor(QT_, GQK[:, 0, :], 32 ** -0.5, TB, ALU.mult, ALU.mult).then_inc(*v.mark("qt", d))
                    for h in range(NH):
                        hp = slice(32 * h, 32 * h + 32)
                        V.scalar_tensor_tensor(QBD[hp, h, :], GQK[hp, 0, :], 32 ** -0.5, TB[hp, :], ALU.mult, ALU.mult)\
                            .then_inc(*v.mark(*(("qbd", d) if h == NH - 1 else ("qbdh", d, h))))
                    V.tensor_copy(g_eem, TB.rearrange("p (c n) -> p c n", c=TT)[:, :, end]).then_inc(*v.mark("eem", d))
                elif what == "gla_chunk":
                    d, i = step[1:]
                    c = i if d == 0 else TT - 1 - i
                    nxt = i + 1 if d == 0 else TT - 2 - i
                    v, a, q = counter("vec_gla"), counter("act_gla"), counter("pe_gla")
                    if i == 0:
                        V.memset(GSM[:, c, :], 0.0).then_inc(*v.mark("state", d, 0))
                        dve.wait_ge(*v.last())
                        V.memset(GS, 0.0).then_inc(*v.mark("s0", d))
                    if i < TT - 1:
                        dve.wait_ge(*q.at("u", d, i))
                        dve.wait_ge(*v.last())
                        V.scalar_tensor_tensor(GSM[:, nxt, :], PS[:, 6 + i % 2, 0:256], g_eem[:, c:c + 1], gla_bd, ALU.mult, ALU.mult)\
                            .then_inc(*v.mark("u", d, i))
                        dve.wait_ge(*v.last())
                        V.scalar_tensor_tensor(GS, GS, g_ee[:, c:c + 1], GSM[:, nxt, :], ALU.mult, ALU.add).then_inc(*v.mark("s", d, i))
                        dve.wait_ge(*v.last())
                        V.tensor_scalar(GSM[:, nxt, :], GS, g_em[:, nxt:nxt + 1], None, ALU.mult).then_inc(*v.mark("state", d, i + 1))
                    dve.wait_ge(*q.at("s", d, i))
                    if i >= 2:
                        dve.wait_ge(*q.at("o", d, i - 2))
                    V.scalar_tensor_tensor(GST[i % 2].rearrange("p (h n) -> p h n", h=NH),
                                           PS[:, 2 + i % 2, :].rearrange("p (h n) -> p h n", h=NH), 3e38,
                                           over(inc_b if d else inc_f), ALU.min, ALU.mult).then_inc(*v.mark("st", d, i))
                    if d == 1:
                        dve.wait_ge(*q.at("o", d, i))
                        dve.wait_ge(*a.at("o", 0, TT - 1))
                        V.tensor_tensor(GO[:, c, :], PS[:, 4 + i % 2, 0:256], GO[:, c, :], ALU.add).then_inc(*v.mark("o", d, i))
                elif what == "fin":
                    br = step[1]
                    f = FIN[br]
                    v, a = counter("vec_fin"), counter("act_fin")
                    o3, t3 = (x.rearrange("p c (h n) -> p (c h) n", h=NH) for x in (f["o"], f["tmp"]))
                    dve.wait_ge(*a.at("sq", br))
                    V.tensor_reduce(fin_ss, t3, AX.X, ALU.add).then_inc(*v.mark("ss", br))
                    dve.wait_ge(*a.at("r", br))
                    V.tensor_tensor(o3, o3, bc(fin_r.unsqueeze(2), P, 32, 64), ALU.mult).then_inc(*v.mark("n", br))
                    dve.wait_ge(*v.last())
                    gain = rows[:, f["row"]:f["row"] + 64]
                    if f["scale"] != 1.0:
                        V.scalar_tensor_tensor(o3, o3, f["scale"], bc(gain.unsqueeze(1), P, 32, 64), ALU.mult, ALU.mult)\
                            .then_inc(*v.mark("g" if f["gate"] is not None else "done", br))
                    else:
                        V.tensor_tensor(o3, o3, bc(gain.unsqueeze(1), P, 32, 64), ALU.mult).then_inc(*v.mark("g", br))
                    if f["gate"] is not None:
                        dve.wait_ge(*a.at("silu", br))
                        dve.wait_ge(*v.last())
                        V.tensor_tensor(f["o"], f["o"], f["gate"], ALU.mult).then_inc(*v.mark("done", br))
                elif what == "fin_tr":
                    br = step[1]
                    v, a = counter("vec_fin"), counter("act_fin")
                    slot = FIN[br]["y"]
                    idx = {"gla": 0, "diff": 2, "gdn": 3}[br]
                    for ft in range(2):
                        dve.wait_ge(*a.at("yhi", br, ft))
                        V.tensor_tensor(Y[slot][1][:, ft, :], PS[:, 2 + 2 * ft:4 + 2 * ft, :].rearrange("p a b -> p (a b)"),
                                        Y[slot][0][:, ft, :], ALU.subtract).then_inc(*v.mark("y" if ft else "y0", idx))
                elif what == "diff_pre":
                    v, a = counter("vec_diff"), counter("act_diff")
                    dl = rows[:, R_DL:R_DL + 128].rearrange("p (s k n) -> p s k n", s=2, k=2)
                    dots = d_dot.rearrange("p (s n) -> p s n", s=2)
                    V.tensor_tensor(dots, dl[:, :, 0, :], dl[:, :, 1, :], ALU.mult).then_inc(*v.mark("prod"))
                    dve.wait_ge(*v.last())
                    V.tensor_reduce(d_lam[:, 0:2], dots, AX.X, ALU.add).then_inc(*v.mark("dots"))
                    dve.wait_ge(*a.at("lam"))
                    V.tensor_tensor(d_lam[:, 2:3], d_lam[:, 1:2], d_lam[:, 0:1], ALU.subtract).then_inc(*v.mark("lam0"))
                    dve.wait_ge(*v.last())
                    V.tensor_scalar(d_lam[:, 3:4], d_lam[:, 2:3], -0.2, None, ALU.add).then_inc(*v.mark("lam"))
                elif what == "diff_qk":
                    u = step[1]
                    h, qt = divmod(u, TT)
                    v, a, q = counter("vec_diff"), counter("act_diff"), counter("pe_diff")
                    if qt == 0:
                        dve.wait_ge(*a.at("w"))
                        if u:
                            dve.wait_ge(*v.at("max", u - 1, 1))
                        V.tensor_scalar(DWH, DW, -(2.0 ** (-8.0 * (h + 1) / NH)) * 32 ** 0.5, None, ALU.mult).then_inc(*v.mark("wh", h))
                        dve.wait_ge(*v.last())
                    for m in range(2):
                        dve.wait_ge(*q.at("s", u, m))
                        if u >= 2 and m == 0:
                            dve.wait_ge(*q.at("tr", u - 2, 1))
                            dve.wait_ge(*v.at("comb", u - 2))
                        V.tensor_tensor_reduce(out=DS[u % 2][:, m, :], in0=PS[:, 2 + 2 * m:4 + 2 * m, :].rearrange("p a b -> p (a b)"),
                                               in1=DWH[:, 896 - P * qt:896 - P * qt + T], scale=1.0, scalar=-3e38,
                                               op0=ALU.add, op1=ALU.max, accum_out=d_mx[u % 2][:, m:m + 1])\
                            .then_inc(*v.mark("max", u, m))
                    dve.wait_ge(*v.last())
                    V.tensor_scalar(d_mx[u % 2], d_mx[u % 2], -32 ** -0.5, None, ALU.mult).then_inc(*v.mark("nm", u))
                elif what == "diff_pv":
                    u = step[1]
                    v, a, q = counter("vec_diff"), counter("act_diff"), counter("pe_diff")
                    dve.wait_ge(*a.at("p", u, 1))
                    if u >= 2:
                        dve.wait_ge(*a.at("o", u - 2))
                    V.reciprocal(d_rl[u % 2], d_l[u % 2]).then_inc(*v.mark("rl", u))
                    dve.wait_ge(*v.last())
                    V.tensor_tensor(d_c[u % 2], d_l[u % 2][:, 0:1], d_rl[u % 2][:, 1:2], ALU.mult).then_inc(*v.mark("c0", u))
                    dve.wait_ge(*v.last())
                    V.tensor_tensor(d_c[u % 2], d_c[u % 2], d_lam[:, 3:4], ALU.mult).then_inc(*v.mark("c", u))
                    dve.wait_ge(*v.last())
                    V.scalar_tensor_tensor(DS[u % 2][:, 0, :], DS[u % 2][:, 1, :], d_c[u % 2], DS[u % 2][:, 0, :], ALU.mult, ALU.add)\
                        .then_inc(*v.mark("comb", u))
                    dve.wait_ge(*q.at("tr", u, 1))
                    if u >= 2:
                        dve.wait_ge(*q.at("o", u - 2))
                    V.tensor_copy(DAT[u % 2][:, 4:8, :], PS[:, 6, :].rearrange("p (k n) -> p k n", k=4)).then_inc(*v.mark("at", u, 1))
                elif what == "gdn_conv":
                    s = step[1]
                    v, a = counter("vec_gdnp"), counter("act_gdnp")
                    dst = {"nq": NQ, "nk": NK, "nv": NVF}[s]
                    k = {"nq": 0, "nk": 2, "nv": 4}[s]
                    dve.wait_ge(*counter("act_evac").at(g_of[s, 1, 1]))
                    if s == "nq":
                        dve.wait_ge(*counter("pool_gdnp").at("pad"))
                    if s == "nv":
                        dve.wait_ge(*v.at("norm", "nk"))
                    for t in range(2):
                        w = cols[:, C_GCW + 4 * (k + t):C_GCW + 4 * (k + t) + 4]
                        V.tensor_scalar(dst[:, t, :], RAW[:, t, 0:T], w[:, 0:1], None, ALU.mult).then_inc(*v.mark("c0", s, t))
                        for j in range(1, 4):
                            dve.wait_ge(*v.last())
                            V.scalar_tensor_tensor(dst[:, t, :], RAW[:, t, j:j + T], w[:, j:j + 1], dst[:, t, :], ALU.mult, ALU.add)\
                                .then_inc(*v.mark(*(("conv", s, t) if j == 3 else ("cj", s, t, j))))
                    if s != "nv":
                        dve.wait_ge(*a.at("rn", s))
                        V.tensor_tensor(dst, dst, NSQ, ALU.mult).then_inc(*v.mark("norm", s))
                elif what == "gdn_scal":
                    v, a = counter("vec_gdnp"), counter("act_gdnp")
                    ba = NBA_.rearrange("p (c k d h) -> p k d c h", c=TT, k=2, d=2)
                    t3 = [x.rearrange("p (d c h) -> p d c h", d=2, c=TT) for x in n_t]
                    dtb = rows[:, R_DTB:R_DTB + 8].rearrange("p (d h) -> p d h", d=2)
                    al = n_al.rearrange("p (d h) -> p d h", d=2)
                    dve.wait_ge(*counter("act_evac").at(g_of["nba", 0]))
                    for d in range(2):
                        V.tensor_tensor(t3[0][:, d], ba[:, 1, d], bc(dtb[:, d].unsqueeze(1), P, TT, NH), ALU.add).then_inc(*v.mark("a", d))
                    dve.wait_ge(*v.last())
                    V.tensor_scalar(n_t[2], n_t[0], -1.0, None, ALU.mult).then_inc(*v.mark("neg"))
                    dve.wait_ge(*v.last())
                    V.tensor_tensor(n_t[1], n_t[0], n_t[2], ALU.min).then_inc(*v.mark("nabs"))
                    dve.wait_ge(*a.at("e"))
                    log1p(n_t[1], n_t[2], n_t[3], n_la, v, "log1p")
                    V.scalar_tensor_tensor(n_t[0], n_t[0], 0.0, n_la, ALU.max, ALU.add).then_inc(*v.mark("sp"))
                    dve.wait_ge(*v.last())
                    dve.wait_ge(*a.at("al"))
                    for d in range(2):
                        V.scalar_tensor_tensor(LAd[:, d], t3[0][:, d], -1.0, bc(al[:, d].unsqueeze(1), P, TT, NH), ALU.mult, ALU.mult)\
                            .then_inc(*v.mark(*(("la",) if d else ("la0",))))
                    dve.wait_ge(*a.at("eg"))
                    for par in range(2):
                        hp = slice(64 * par, 64 * par + 64)
                        V.tensor_copy(n_cd[hp, :].rearrange("p (a t) -> p a t", t=2),
                                      n_eg[hp, 128:192].rearrange("p (a t u) -> p a t u", t=2, u=2)[:, :, :, par])\
                            .then_inc(*v.mark("cd", par))
                elif what == "gdn":
                    i, part = step[1:]
                    v, a, q, po = (counter(f"{e}_gdn") for e in ("vec", "act", "pe", "pool"))
                    for d in range(2):
                        c = i if d == 0 else TT - 1 - i
                        B0, B1, B2 = (PS[:, 2 + 3 * d + b, :].rearrange("p (h n) -> p h n", h=NH) for b in range(3))
                        nm = lambda lv, dd: over(nmask[:, 7 * dd + lv, :])
                        if part == 0:
                            dve.wait_ge(*q.at("kk", i, d))
                            dve.wait_ge(*po.at("dts", i, d))
                            V.tensor_tensor(NLT[d], B1[:, :, :], NLT[d], ALU.mult).then_inc(*v.mark("lt", i, d))
                            dve.wait_ge(*q.at("qk", i, d))
                            V.tensor_tensor(NQT[d], B2[:, :, :], NQT[d], ALU.mult).then_inc(*v.mark("qt", i, d))
                        elif part == 1:
                            dve.wait_ge(*q.at("l0", i, d))
                            V.tensor_tensor(NX[d], B0[:, :, :], nm(0, d), ALU.mult).then_inc(*v.mark("x0m", i, d))
                            dve.wait_ge(*v.last())
                            V.tensor_tensor(NX[d], NX[d], over(ident), ALU.add).then_inc(*v.mark("x", i, d, 0))
                            dve.wait_ge(*a.at("qd", i, d))
                            V.tensor_tensor(NQD[d], NQD[d], NQ[:, :, c * P:c * P + P], ALU.mult).then_inc(*v.mark("qd", i, d))
                        elif part < 8:
                            lv = part - 1
                            dve.wait_ge(*q.at("y", i, d, lv))
                            V.tensor_tensor(NY[d], B0[:, :, :], nm(lv, d), ALU.mult).then_inc(*v.mark("yn", i, d, lv))
                    for d in range(2):
                        c = i if d == 0 else TT - 1 - i
                        B0, B1, B2 = (PS[:, 2 + 3 * d + b, :].rearrange("p (h n) -> p h n", h=NH) for b in range(3))
                        if 2 <= part < 8:
                            lv = part - 1
                            dve.wait_ge(*q.at("zy", i, d, lv))
                            if lv < 6:
                                V.tensor_tensor(NX[d], B1[:, :, :], NX[d], ALU.add).then_inc(*v.mark("x", i, d, lv))
                            V.tensor_tensor(NZ_[d], B2[:, :, :], NZ_[d], ALU.add).then_inc(*v.mark("z", i, d, lv))
                        elif part == 8:
                            dve.wait_ge(*q.at("v", i, d))
                            V.tensor_tensor(NVN[d].rearrange("p t (u n) -> p (t u) n", u=2),
                                            PS[:, 3 + 3 * d, 0:256].rearrange("p (h n) -> p h n", h=NH), heads(BETA[:, d, c, :]),
                                            ALU.mult).then_inc(*v.mark("vn", i, d))
                    if part == 8:
                        for d in range(2):
                            c = i if d == 0 else TT - 1 - i
                            dve.wait_ge(*q.at("o", i, d))
                            V.tensor_tensor(NKE[d], PS[:, 4 + 3 * d, 0:256].rearrange("p (t n) -> p t n", t=2), over(bd64, 2), ALU.mult)\
                                .then_inc(*v.mark("um", i, d))
                            dve.wait_ge(*v.last())
                            for t in range(2):
                                V.scalar_tensor_tensor(NS[d][:, t, :], NS[d][:, t, :], CD[:, d, c, t:t + 1], NKE[d][:, t, :], ALU.mult, ALU.add)\
                                    .then_inc(*v.mark(*(("state", i, d) if t else ("state0", i, d))))
                            if i >= 4:
                                V.tensor_tensor(NO[:, c, :], PS[:, 2 + 3 * d, 0:256], NO[:, c, :], ALU.add).then_inc(*v.mark("o", i, d))
                elif what == "merged_pair":
                    v, a = counter("vec_pair"), counter("act_pair")
                    for k in range(KT):
                        dve.wait_ge(*a.at("merged", k))
                        V.tensor_tensor(MP[1][:, k, :], merged[:, k, :], MP[0][:, k, :], ALU.subtract).then_inc(*v.mark("merged", k))
                elif what == "xattn":
                    g = step[1]
                    h, half = divmod(g, 2)
                    v, a, q = (counter(f"{e}_xattn") for e in ("vec", "act", "pe"))
                    for j in range(2):
                        dve.wait_ge(*q.at("s", g, j))
                        if g >= 2 and j == 0:
                            dve.wait_ge(*a.at("p", g - 2, 3))
                        V.tensor_reduce(x_mx[g % 2][:, 2 * j:2 * j + 2], PS[:, 2 + j, :].rearrange("p (a b) -> p a b", a=2), AX.X, ALU.max)\
                            .then_inc(*v.mark("mx0", g, j))
                        dve.wait_ge(*v.last())
                        V.tensor_scalar(x_mx[g % 2][:, 2 * j:2 * j + 2], x_mx[g % 2][:, 2 * j:2 * j + 2], -1 / 16, None, ALU.mult)\
                            .then_inc(*v.mark("mx", g, j))
                    for j in range(2):
                        dve.wait_ge(*a.at("p", g, 2 * j + 1))
                        V.reciprocal(x_l[g % 2][:, 2 * j:2 * j + 2], x_l[g % 2][:, 2 * j:2 * j + 2]).then_inc(*v.mark("rl", g, j))
                        dve.wait_ge(*v.last())
                        V.tensor_tensor(XP[g % 2][:, 2 * j:2 * j + 2, :], XP[g % 2][:, 2 * j:2 * j + 2, :],
                                        bc(x_l[g % 2][:, 2 * j:2 * j + 2].unsqueeze(2), P, 2, 256), ALU.mult).then_inc(*v.mark("pn", g, j))
                    for m in range(2):
                        dve.wait_ge(*a.at("pt", g, m))
                        V.tensor_tensor(XPT[g % 2][1][:, m, :], PS[:, 4 + m, :], XPT[g % 2][0][:, m, :], ALU.subtract)\
                            .then_inc(*v.mark("pt", g, m))
                    for j in range(2):
                        dve.wait_ge(*a.at("o", g, j))
                        hs = slice(half * 512, half * 512 + 512)
                        V.tensor_tensor(XO[1][:, 2 * h + j, hs], PS[:, 6 + j, :], XO[0][:, 2 * h + j, hs], ALU.subtract)\
                            .then_inc(*v.mark(*(("o", g) if j else ("o0", g))))


            v, a, q = counter("vec_route"), counter("act_route"), counter("pe_route")
            e4 = r_g4.rearrange("p (t g) -> p t g", g=NG)
            w4 = r_w4.rearrange("p (t g) -> p t g", g=NG)
            NEG = 1e30

            def then(instruction, *key):
                instruction.then_inc(*v.mark(*key))
                dve.wait_ge(*v.last())

            def first(dst, diff, w, n, key):
                then(V.tensor_scalar(w, diff, 0.0, None, ALU.is_ge), key, "is_max")
                then(V.tensor_tensor(w, w, bc(K_DESC[:, 32 - n:32].unsqueeze(1), P, TT, n), ALU.mult), key, "weighted")
                then(V.tensor_reduce(r_wm, w, AX.X, ALU.max), key, "first")
                then(V.tensor_tensor(dst, w, bc(r_wm.unsqueeze(2), P, TT, n), ALU.is_equal), key, "one")

            dve.wait_ge(*counter("pool_route").at("iota"))
            then(V.tensor_copy(K_F, K_INT), "constants")
            dve.wait_ge(*q.at("logits", TT - 1))
            then(V.tensor_tensor(r_l, PS[:, 6, 0:TT * 36].rearrange("p (t n) -> p t n", n=36),
                                 bc(rows[:, R_BG:R_BG + 36].unsqueeze(1), P, TT, 36), ALU.add), "logits")
            then(V.tensor_reduce(r_gm, r_l[:, :, 0:NG], AX.X, ALU.max), "group_max")
            then(V.tensor_tensor(e4, r_l[:, :, 0:NG], bc(r_gm.unsqueeze(2), P, TT, NG), ALU.subtract), "group_diff0")
            then(V.tensor_scalar(w4, e4, 0.0, None, ALU.is_ge), "group_diff")
            then(V.tensor_tensor(w4, w4, bc(K_DESC[:, 32 - NG:32].unsqueeze(1), P, TT, NG), ALU.mult), "group_weighted")
            then(V.tensor_reduce(r_wm, w4, AX.X, ALU.max), "group_first")
            then(V.tensor_tensor(w4, w4, bc(r_wm.unsqueeze(2), P, TT, NG), ALU.is_equal), "group_one")
            then(V.tensor_scalar(w4, w4, -1.0, NEG, ALU.add, ALU.mult), "group_mask")
            for g in range(NG):
                then(V.tensor_tensor(r_e[:, :, g * GE:g * GE + GE], r_l[:, :, NG + g * GE:NG + g * GE + GE],
                                     bc(w4[:, :, g:g + 1], P, TT, GE), ALU.add), "masked", g)
            then(V.tensor_reduce(r_m1, r_e, AX.X, ALU.max), "max1")
            then(V.tensor_tensor(r_w, r_e, bc(r_m1.unsqueeze(2), P, TT, NE), ALU.subtract), "diff1")
            first(r_o1, r_w, r_w, NE, "top1")
            then(V.scalar_tensor_tensor(r_e, r_o1, -3 * NEG, r_e, ALU.mult, ALU.add), "without1")
            then(V.tensor_reduce(r_m2, r_e, AX.X, ALU.max), "max2")
            then(V.tensor_tensor(r_x, r_m2, r_m1, ALU.subtract), "top_diff")
            then(V.tensor_tensor(r_w, r_e, bc(r_m2.unsqueeze(2), P, TT, NE), ALU.subtract), "diff2")
            first(r_o2, r_w, r_w, NE, "top2")
            then(V.tensor_tensor(r_a, r_o1, r_o2, ALU.add), "both")
            then(V.tensor_scalar(r_ap[:, 0, :], r_a[:, 0, :], 0.0, None, ALU.mult), "prefix", 0)
            for t in range(1, TT + 1):
                dst = r_ap[:, t, :] if t < TT else r_at
                then(V.tensor_tensor(dst, r_ap[:, t - 1, :], r_a[:, t - 1, :], ALU.add), "prefix", t)
            dve.wait_ge(*a.at("top_exp"))
            then(V.tensor_reduce(r_gs, e4, AX.X, ALU.add), "group_sum")
            then(V.tensor_scalar(r_gm, r_ex, 1.0, None, ALU.add), "pair_sum")
            then(V.tensor_tensor(r_gs, r_gs, r_gm, ALU.mult), "sums")
            then(V.reciprocal(GATE[:, 0, :], r_gs), "gate0")
            then(V.tensor_tensor(GATE[:, 1, :], GATE[:, 0, :], r_ex, ALU.mult), "gate1")
            dve.wait_ge(*q.at("count"))
            then(V.tensor_copy(r_cnt, PS[:, 6, 0:NE]), "count")
            then(V.tensor_scalar(r_nov, r_cnt, float(P), None, ALU.is_gt), "beyond", 1)
            for m in range(2, T // P):
                then(V.scalar_tensor_tensor(r_nov, r_cnt, float(m * P), r_nov, ALU.is_gt, ALU.add), "beyond", m)
            then(V.tensor_tensor_scan(r_inc, ones[:, 0:NE], r_nov, 0.0, ALU.mult, ALU.add), "beyond_sum")
            then(V.tensor_tensor(r_sb, r_inc, r_nov, ALU.subtract), "beyond_first")
            then(V.tensor_scalar(r_sb, r_sb, float(P), float(P * (NE - 1)), ALU.mult, ALU.add), "beyond_slot")
            then(V.scalar_tensor_tensor(r_sb, K_E, -float(P), r_sb, ALU.mult, ALU.add), "beyond_shift")
            dve.wait_ge(*q.at("rank"))
            pos = PS[:, 7, 0:TT * NE].rearrange("p (t e) -> p t e", e=NE)
            then(V.tensor_scalar(r_mk, pos, float(P), None, ALU.is_ge), "rank_beyond")
            then(V.tensor_tensor(r_mk, r_mk, bc(r_sb.unsqueeze(1), P, TT, NE), ALU.mult), "rank_shift")
            then(V.tensor_tensor(r_pos, pos, r_mk, ALU.add), "rank_shifted")
            then(V.scalar_tensor_tensor(r_pos, bc(K_E.unsqueeze(1), P, TT, NE), float(P), r_pos, ALU.mult, ALU.add), "slots")
            for k, one in enumerate((r_o1, r_o2)):
                then(V.tensor_tensor(one, one, r_pos, ALU.mult), "slot_of", k)
                then(V.tensor_reduce(SLOT[:, k, :], one, AX.X, ALU.add), "slot", k)
            then(V.tensor_copy(SLOTU, SLOT.rearrange("p k t -> p (k t)")), "slots_int")
            then(V.tensor_tensor(r_cmp, bc(K_J.unsqueeze(2), P, 16, NE), bc(r_inc.unsqueeze(1), P, 16, NE), ALU.is_ge), "ends")
            then(V.tensor_reduce(r_ov[:, 0:16], r_cmp, AX.X, ALU.add), "owners")
            then(V.tensor_copy(r_ov[:, 16:17], r_inc[:, NE - 1:NE]), "number")
            then(V.tensor_copy(OVI, r_ov), "beyond_int")
            dve.wait_ge(*q.at("table"))
            then(V.tensor_copy(IDX, PS[:, 6, 64:64 + NBLK]), "gates")

            def g_mul(e):
                dve.wait_ge(act_sl, e + 1)
                dve.wait_ge(pe_a3, e + 1)
                after(dve, pe_gt, e)
                V.tensor_tensor(GU, PS[:, 3, :], SL, ALU.mult).then_inc(vec_g, 1)

            def x_copy(e, s):
                dve.wait_ge(pe_xt, 2 * e + 2)
                V.tensor_copy(XT[s][:, 4:8, :], PS[:, 1, :].rearrange("p (k n) -> p k n", k=4)).then_inc(vec_xt, 1)

            def y_copy(e, s, n):
                dve.wait_ge(pe_y, 2 * e + 2)
                after(dve, y_out[s], 16 * n)
                V.tensor_copy(YB[s][:, 1, :], PS[:, 6, :]).then_inc(vec_y, 1)

            def period(e, s, n):
                g_mul(e)
                if not (isinstance(e, int) and e == NE - 1):
                    x_copy(e + 1, 1 - s)
                if not (isinstance(e, int) and e == 0):
                    y_copy(e - 1, 1 - s, n - 1 + s)

            def block_beyond(e, j):
                x_copy(e, 0)
                g_mul(e)
                y_copy(e, 0, j + NE // 2)

            experts(dve, lambda: x_copy(0, 0), period, lambda: y_copy(NE - 1, 1, NE // 2 - 1))
            beyond(dve, block_beyond)
            v, a = counter("vec_final"), counter("act_final")

            def result(tt):
                dve.wait_ge(*a.at("r", tt))
                V.scalar_tensor_tensor(XH_OUT[tt], X[:, tt, :], f_r[:, tt:tt + 1], gain_row, ALU.mult, ALU.mult)\
                    .then_inc(*v.mark("out", tt))

            dve.wait_ge(gain_in, 16 * (len(GAINS) + 1))
            for tt in range(TT):
                dve.wait_ge(y_in[tt], 32)
                for k in range(2):
                    V.scalar_tensor_tensor(X[:, tt, :], YG[k][:, tt, :], GATE[:, k, tt:tt + 1], X[:, tt, :], ALU.mult, ALU.add)\
                        .then_inc(*v.mark(*(("sum", tt) if k else ("sum0", tt))))
                    if k == 0:
                        dve.wait_ge(*v.last())
                if tt:
                    result(tt - 1)
            result(TT - 1)

        @block.gpsimd
        def _(pool):
            G = nc.gpsimd
            c = counter("pool_const")

            def select(dst, src, pattern, base, ch, op, fill, key):
                G.affine_select(out=dst, in_=src, compare_op=op, fill=fill, base=base, pattern=pattern, channel_multiplier=ch)\
                    .then_inc(*c.mark(*key))

            G.memset(ident, 0.0).then_inc(*c.mark("ident0"))
            G.memset(ones, 1.0).then_inc(*c.mark("ones"))
            G.memset(eps_col, EPS).then_inc(*c.mark("eps"))
            G.memset(lneighth, math.log(0.125)).then_inc(*c.mark("cols"))
            ZERO_ROW = f32(YP_OFF, D)
            G.memset(ZERO_ROW, 0.0).then_inc(*c.mark("zero_row"))
            pool.wait_ge(*c.last())
            select(ident, ident, [[-1, P]], 0, 1, ALU.not_equal, 1.0, ("ident",))
            select(inc_f, ones, [[1, P]], 0, -1, ALU.is_ge, 0.0, ("inc_f",))
            select(inc_b, ones, [[-1, P]], 0, 1, ALU.is_ge, 0.0, ("inc_b",))
            select(st_f, ones, [[1, P]], 0, -1, ALU.is_gt, 0.0, ("st_f",))
            select(st_b, ones, [[-1, P]], 0, 1, ALU.is_gt, 0.0, ("st_b",))
            G.memset(bd64, 0.0).then_inc(*c.mark("bd0"))
            G.memset(gla_bd, 0.0).then_inc(*c.mark("gbd0"))
            G.memset(nmask, 0.0).then_inc(*c.mark("nm0"))
            G.memset(LXP[:, :, 0:2], 0.0).then_inc(*c.mark("pad0"))
            G.memset(LXP[:, :, 2 + T:4 + T], 0.0).then_inc(*c.mark("lxpad"))
            pool.wait_ge(*c.last())
            for s in range(2):
                G.memset(bd64[64 * s:64 * s + 64, 64 * s:64 * s + 64], 1.0).then_inc(*c.mark("bd", s))
                pool.wait_ge(*c.last())
            for h in range(NH):
                G.memset(gla_bd[32 * h:32 * h + 32, 64 * h:64 * h + 64], 1.0).then_inc(*c.mark("gbd", h))
                pool.wait_ge(*c.last())
            for d in range(2):
                for lv in range(7):
                    B = 2 ** lv
                    part = nmask[:, 7 * d + lv, :].rearrange("p (n s b) -> p n s b", s=2, b=B)[:, :, d, :]
                    G.memset(part, -1.0).then_inc(*c.mark("nm", d, lv, 0))
                    pool.wait_ge(*c.last())
                    n = P // (2 * B)
                    select(part, part, [[-2 * B, n], [0, B]], 0 if d else -B, 1, ALU.is_ge, 0.0, ("nm", d, lv, 1))
                    pool.wait_ge(*c.last())
                    select(part, part, [[2 * B, n], [0, B]], B - 1 if d else 2 * B - 1, -1, ALU.is_ge, 0.0, ("nm", d, lv, 2))
            for step in schedule:
                what = step[0]
                if what == "evac":
                    i, g = step[1:]
                    n = gid[i, g]
                    kind = kind_of[n]
                    if kind[0] == "up" and kind[1] != 1:
                        dst = merged[:, kind[2], kind[3] * 512:kind[3] * 512 + 512]
                        pool.wait_ge(*counter("vec_evac").at(n))
                        G.tensor_tensor(dst, dst, SG[2 + (gate_no[n] - 1) % 2], ALU.add).then_inc(*counter("pool_merge").mark(n))
                elif what == "lru_dir":
                    d, t = step[1:]
                    po = counter("pool_lru")
                    if d + t == 0:
                        pool.wait_ge(*c.at("zero_row"))
                        G.dma_start(YROWS[NE * P:, :].rearrange("(b p) d -> p b d", p=P),
                                    bc(ZERO_ROW.unsqueeze(1), P, NOV, D)).then_inc(spare_rows, 16)
                    pool.wait_ge(*counter("act_lru").at("i", d, t))
                    pool.wait_ge(*counter("vec_lru").at("u", t))
                    G.tensor_tensor(LI_, LI_, LU[:, t, :], ALU.mult).then_inc(*po.mark("iu", d, t))
                elif what == "gla_pre":
                    if step[1] == 0:
                        pool.wait_ge(*counter("vec_fin").at("y", 1))
                        pool.wait_ge(*counter("act_lru").at("yhi"))
                        G.memset(QBD, 0.0).then_inc(*counter("pool_gla").mark("qbd0"))
                elif what == "diff_pre":
                    po = counter("pool_diff")
                    pool.wait_ge(*counter("pe_fin").at("tr", "gla", 1))
                    pool.wait_ge(*counter("vec_fin").at("y", 0))
                    G.iota(DWH.bitcast(I32), pattern=[[-1, 1920]], base=896, channel_multiplier=1).then_inc(*po.mark("iota"))
                    for s in range(8):
                        G.memset(DQZ[s], 0.0).then_inc(*po.mark("z", s))
                    pool.wait_ge(*po.last())
                elif what == "diff_qk":
                    u = step[1]
                    h, qt = divmod(u, TT)
                    po = counter("pool_diff")
                    if u == 0:
                        pool.wait_ge(*counter("act_evac").at(g_of["dq", 1, 1]))
                    if u >= 2:
                        pool.wait_ge(*counter("pe_diff").at("s", u - 2, 1))
                    if counter("pool_merge").n:
                        pool.wait_ge(*counter("pool_merge").last())
                    for m in range(2):
                        hp = slice(64 * (h % 2) + 32 * m, 64 * (h % 2) + 32 * m + 32)
                        G.tensor_copy(DQZ[4 * (u % 2) + 2 * (h % 2) + m][hp, :], DQT[hp, h // 2, qt * P:qt * P + P])\
                            .then_inc(*po.mark(*(("q", u) if m else ("q0", u))))
                        pool.wait_ge(*po.last())
                elif what == "mm" and kind_of[gid[step[1], step[2]]] == ("nq", 0, 0):
                    po = counter("pool_gdnp")
                    pool.wait_ge(*counter("vec_fin").at("y", 2))
                    pool.wait_ge(*counter("pe_fin").at("tr", "diff", 1))
                    G.memset(RAW[:, :, 0:2], 0.0).then_inc(*po.mark("pad0"))
                    G.memset(RAW[:, :, 2 + T:4 + T], 0.0).then_inc(*po.mark("pad"))
                    for d in range(2):
                        G.memset(NS[d], 0.0).then_inc(*po.mark(*(("s0",) if d else ("s00",))))
                        G.memset(NKB[d], 0.0).then_inc(*po.mark("kb0", d))
                    pool.wait_ge(*po.last())
                elif what == "gdn":
                    i, part = step[1:]
                    po, v, q, a = (counter(f"{e}_gdn") for e in ("pool", "vec", "pe", "act"))
                    for d in range(2):
                        c_ = i if d == 0 else TT - 1 - i
                        cs = slice(c_ * P, c_ * P + P)
                        inc, st = (inc_b, st_b) if d else (inc_f, st_f)
                        if part == 0:
                            if i == 0 and d == 0:
                                pool.wait_ge(*counter("vec_gdnp").at("cd", 1))
                                pool.wait_ge(*counter("act_gdnp").at("tm", "nv", 3))
                            if i:
                                pool.wait_ge(*v.at("z", i - 1, d, 5))
                                pool.wait_ge(*q.at("o", i - 1, d))
                                pool.wait_ge(*v.at("state", i - 1, d))
                            G.tensor_tensor(NX[d], over(inc), bc(LAd[:, d, c_, :].unsqueeze(2), P, NH, P), ALU.mult)\
                                .then_inc(*po.mark("tla", i, d))
                            G.tensor_copy(NWK[d].rearrange("p t (u n) -> p (t u) n", u=2), heads(LAd[:, d, c_, :]))\
                                .then_inc(*po.mark("lab", i, d))
                            for t in range(2):
                                for u in range(2):
                                    pool.wait_ge(*po.last())
                                    if t + u == 0 and counter("pool_merge").n:
                                        pool.wait_ge(*counter("pool_merge").last())
                                    hp = slice(64 * u, 64 * u + 64)
                                    G.tensor_copy(NKB[d][hp, 2 * t + u, :], NK[hp, t, cs]).then_inc(
                                        *po.mark(*(("in", i, d) if t + u == 2 else ("kb", i, d, t, u))))
                                    pool.wait_ge(*po.last())
                            k4 = NKT[:, c_, :].rearrange("p (h n) -> p h n", h=NH)
                            G.tensor_tensor(NKE[d].rearrange("p t (u n) -> p (t u) n", u=2), k4, heads(EG[:, 0, d, c_, :]), ALU.mult)\
                                .then_inc(*po.mark("ke", i, d))
                            G.tensor_tensor(NKD[d].rearrange("p t (u n) -> p (t u) n", u=2), k4, heads(EG[:, 1, d, c_, :]), ALU.mult)\
                                .then_inc(*po.mark("kd", i, d))
                    for d in range(2):
                        c_ = i if d == 0 else TT - 1 - i
                        inc, st = (inc_b, st_b) if d else (inc_f, st_f)
                        if part == 0:
                            pool.wait_ge(*a.at("dt", i, d))
                            G.tensor_tensor(NLT[d], NY[d], over(st), ALU.mult).then_inc(*po.mark("dt0", i, d))
                            pool.wait_ge(*po.last())
                            G.tensor_tensor(NLT[d], NLT[d], bc(BETA[:, d, c_, :].unsqueeze(2), P, NH, P), ALU.mult)\
                                .then_inc(*po.mark("dt1", i, d))
                            G.tensor_tensor(NQT[d], NY[d], over(inc), ALU.mult).then_inc(*po.mark("dts", i, d))
                        elif part == 1:
                            pool.wait_ge(*v.at("lt", i, d))
                            G.tensor_tensor(NZ_[d], NLT[d], over(nmask[:, 7 * (1 - d), :]), ALU.mult).then_inc(*po.mark("z0", i, d))
                            pool.wait_ge(*po.last())
                            G.tensor_tensor(NZ_[d], NZ_[d], over(ident), ALU.add).then_inc(*po.mark("z", i, d))
                elif what == "norm_stats" and step[1] == "x2":
                    po = counter("pool_route")
                    pool.wait_ge(*counter("pool_merge").at(g_of["up", 3, KT - 1, 1]))
                    pool.wait_ge(*pe_mm.at(LAST_MM))
                    for o_, n, b_, ch in ((0, 32, 32, 0), (32, 32, 0, 0), (64, 16, 0, 0)):
                        G.iota(K_INT[:, o_:o_ + n], pattern=[[-1 if b_ else 1, n]], base=b_, channel_multiplier=ch)\
                            .then_inc(*po.mark("iota", o_))
                    G.iota(K_INT[:, 80:88], pattern=[[P, TT]], base=0, channel_multiplier=1).then_inc(*po.mark("iota"))
                    G.memset(ZROW, 0.0).then_inc(*po.mark("zeros"))
            v = counter("vec_route")
            pool.wait_ge(*v.at("slots_int"))
            pool.wait_ge(zero_out, 16)
            for j in range(2 * TT):
                G.indirect_dma_start(TABLE, bass.IndirectOffsetOnAxis(SLOTU[:, j:j + 1], 0), K_TOK[:, j % TT:j % TT + 1], None)\
                    .then_inc(scattered, 16)
            for s in range(2):
                pool.wait_ge(xhat_out[s], 16 * TT // 2)
            pool.wait_ge(*v.at("gates"))
            for e in range(NE):
                after(pool, pe_xt, 2 * (e - 1))
                G.indirect_dma_start(XR[e % 2], None, XH_D, bass.IndirectOffsetOnAxis(IDX[:, e:e + 1], 0)).then_inc(rows_in[e % 2], 16)

            pool.wait_ge(y_out[1], 16 * NE // 2)
            pool.wait_ge(y_out[0], 16 * NE // 2)
            number = pool.value_load(OVI[0:1, 16:17], min_val=0, max_val=NOV)
            for j in range(NOV):
                with pool.If(number > j):
                    G.indirect_dma_start(XR[0], None, XH_D, bass.IndirectOffsetOnAxis(IDX[:, NE + j:NE + j + 1], 0)).then_inc(rows_in[0], 16)
                    pool.wait_ge(y_out[0], 16 * NE // 2 + 16 * (j + 1))
            for tt in range(TT):
                for k in range(2):
                    G.indirect_dma_start(YG[k][:, tt, :], None, YROWS, bass.IndirectOffsetOnAxis(SLOTU[:, k * TT + tt:k * TT + tt + 1], 0))\
                        .then_inc(y_in[tt], 16)
    return {n: k.found for n, k in counters.items()}


def pack_small(inputs, np):
    cols = np.zeros((P, NCOLS), np.float32)
    cols[:, C_MERGEB:C_MERGEB + 32] = inputs["merge_b"][0].reshape(4 * KT, P).T
    cols[:, C_LRB:C_LRB + 2] = inputs["gla_lr_bias"][0].T
    cols[:, C_LCW:C_LCW + 8] = inputs["lru_conv_w"][0].reshape(4, 2, P).transpose(2, 1, 0).reshape(P, 8)
    cols[:, C_LCB:C_LCB + 2] = inputs["lru_conv_b"][0].reshape(2, P).T
    cols[:, C_LBA:C_LBA + 4] = inputs["lru_b_a"][0].reshape(4, P).T
    cols[:, C_LBX:C_LBX + 4] = inputs["lru_b_x"][0].reshape(4, P).T
    cols[:, C_LAM:C_LAM + 4] = inputs["lru_lambda"][0].reshape(4, P).T
    cols[:, C_GCW:C_GCW + 24] = inputs["gdn_conv_w"][0].reshape(4, 6, P).transpose(2, 1, 0).reshape(P, 24)
    rows = np.concatenate([
        inputs["gla_norm"][0], inputs["diff_norm"][0], inputs["gdn_norm"][0], inputs["gdn_a_log"][0].ravel(),
        inputs["gdn_dt_bias"][0].ravel(), inputs["diff_lq1"][0], inputs["diff_lk1"][0], inputs["diff_lq2"][0],
        inputs["diff_lk2"][0], inputs["moe_b_group"][0], inputs["moe_b_expert"][0]])
    lru_w = np.zeros((P, 8, P), np.float32)
    for d in range(2):
        for gate, name in enumerate(("lru_w_a", "lru_w_x")):
            for b in range(4):
                s = slice(64 * (b % 2), 64 * (b % 2) + 64)
                lru_w[s, 4 * d + 2 * gate + b // 2, s] = inputs[name][0, d, b]
    lr_up = np.zeros((32, 256), np.float32)
    for d in range(2):
        lr_up[16 * d:16 * d + 16, P * d:P * d + P] = inputs["gla_lr_up"][0, d]
    router_w = np.concatenate([inputs["moe_w_group"][0], inputs["moe_w_expert"][0]], axis=1)
    gains = np.stack([inputs["mix_norm"][0], inputs["mem_norm"][0], inputs["xattn_norm"][0], inputs["moe_norm"][0], inputs["final_norm"]])
    return {"cols": cols, "rows": rows, "lru_w": lru_w, "lr_up": lr_up, "gains": gains, "router_w": router_w}


def kernel(**inputs):
    import numpy as np
    import concourse.bacc as _bacc
    from concourse.bass_utils import run_bass_kernel_spmd as _run

    inputs = {n: np.asarray(v) for n, v in inputs.items()}
    arrays = pack_small(inputs, np)
    for n in ("x", "mem", "w_in", "merge_w", "branch_up", "mix_out", "xattn_wkv", "xattn_wq", "xattn_wo"):
        arrays[n] = inputs[n][0]
    for n in ("w1", "w3", "w2"):
        arrays[n] = inputs["moe_" + n][0]
    arrays = {f"in_{n}_dram": np.ascontiguousarray(v) for n, v in arrays.items()}

    def program(known):
        nc = _bacc.Bacc("TRN2", target_bir_lowering=False, num_devices=1)
        A = {n[3:-5]: nc.dram_tensor(n, v.shape, mybir.dt.from_np(v.dtype), kind="ExternalInput").ap()
             for n, v in arrays.items()}
        out = nc.dram_tensor("out_0_dram", (1, T, D), F32, kind="ExternalOutput").ap()
        A["xhat"] = nc.dram_tensor("xhat", (T, D), F32, kind="Internal").ap()
        A["table"] = nc.dram_tensor("table", (NBLK * P, 1), F32, kind="Internal").ap()
        A["yrows"] = nc.dram_tensor("yrows", (NBLK * P, D), F32, kind="Internal").ap()
        return nc, build(nc, A, out[0], known)

    known = program(None)[1]
    nc, _ = program(known)
    return _run(nc, [arrays], core_ids=[0]).results[0]["out_0_dram"]
```

```python
import math
from contextlib import ExitStack

import concourse.bass as bass
from concourse import mybir

P = 128
T = 1024
D = 1024
KT = D // P
TT = T // P
NH = 4
WS = 256.0
GSCALE = 1 / 16
NLAND = 4
NE = 32
NG = 4
GE = NE // NG
DE = D // 2
KE = DE // P
NOV = (2 * T - 1) // P
NBLK = NE + NOV
BATCHES = ((0, 3), (3, 6), (6, 8))

F32 = mybir.dt.float32
F16 = mybir.dt.float16
I32 = mybir.dt.int32
U32 = mybir.dt.uint32
ALU = mybir.AluOpType
ACT = mybir.ActivationFunctionType
AX = mybir.AxisListType
EPS = 1e-6

GQ, GK, GV, GOG, GLR = 0, 128, 256, 512, 768
LX, LG = 800, 1056
DQ, DK, DV = 1312, 1568, 1824
NQKV, NZ, NBA = 2080, 2848, 3104

C_MERGEB = 0
C_LRB = 32
C_LCW = 34
C_LCB = 42
C_LBA = 44
C_LBX = 48
C_LAM = 52
C_GCW = 56
NCOLS = 80
R_GLAN, R_DIFFN, R_GDNN = 0, 64, 128
R_ALOG, R_DTB = 192, 200
R_DL = 208
R_BG, R_BE = 336, 340
NROWS = 372


class Counter:

    def __init__(self, sem, name, known):
        self.sem, self.name, self.n, self.known, self.found = sem, name, 0, known, {}

    def mark(self, *key):
        self.n += 1
        assert key not in self.found, (self.name, key)
        self.found[key] = self.n
        return self.sem, 1

    def at(self, *key):
        if self.known is None:
            return self.sem, 1
        return self.sem, self.known[self.name][key]

    def last(self):
        return self.sem, self.n


def plan_panels(A):
    panels = []

    def kview(w):
        return w.rearrange("(k p) n -> p k n", p=P)

    def add(name, parts, groups):
        nk = max(k0 + s.shape[1] for s, k0, c0 in parts)
        panels.append(dict(name=name, parts=parts, nk=nk, groups=groups))

    w_in = kview(A["w_in"])

    def fm(name, c, n=2):
        return [(name, jt, half) for jt in range(n) for half in range(2)]

    def tm(name):
        return [(name, tp) for tp in range(TT // 2)]

    def proj(name, col, groups):
        add(name, [(w_in[:, :, col:col + 256], 0, 0)], groups)

    def merge(i):
        mw = kview(A["merge_w"][i])
        up = kview(A["branch_up"][i])
        for q in range(4):
            add(f"merge{i}{q}", [(mw[:, :, q * 256:q * 256 + 256], 0, 0), (up[:, :, q * 256:q * 256 + 256], KT, 0)],
                [(kind, i, 2 * q + jt, half) for jt in range(2) for half in range(2) for kind in ("gate", "up")])

    proj("lx", LX, [("lx", jt, half) for half in range(2) for jt in range(2)])
    proj("lg", LG, fm("lg", LG))
    add("glr_nba", [(w_in[:, :, GLR:GLR + 32], 0, 0), (w_in[:, :, NBA:NBA + 16], 0, 32)],
        [("glr", 0, 0), ("glr", 0, 1), ("nba", 0)])
    proj("gqk", GQ, fm("gqk", GQ))
    proj("gv", GV, tm("gv"))
    merge(1)
    proj("gog", GOG, tm("gog"))
    proj("dq", DQ, fm("dq", DQ))
    proj("dk", DK, fm("dk", DK))
    proj("dv", DV, tm("dv"))
    merge(0)
    proj("nq", NQKV, fm("nq", 0))
    proj("nk", NQKV + 256, fm("nk", 0))
    proj("nv", NQKV + 512, fm("nv", 0))
    merge(2)
    proj("nz", NZ, tm("nz"))
    merge(3)
    for q in range(4):
        add(f"mix{q}", [(kview(A["mix_out"])[:, :, q * 256:q * 256 + 256], 0, 0)], [("mix", q, tp) for tp in range(4)])
    for q in range(4):
        add(f"wk{q}", [(kview(A["xattn_wkv"])[:, :, q * 256:q * 256 + 256], 0, 0)], [("wk", q)])
    for q in range(4):
        add(f"wv{q}", [(kview(A["xattn_wkv"])[:, :, D + q * 256:D + q * 256 + 256], 0, 0)], [("wv", q)])
    for q in range(4):
        add(f"wq{q}", [(kview(A["xattn_wq"])[:, :, q * 256:q * 256 + 256], 0, 0)],
            [("wq", 2 * q + jt, half) for jt in range(2) for half in range(2)])
    for q in range(4):
        add(f"wo{q}", [(kview(A["xattn_wo"])[:, :, q * 256:q * 256 + 256], 0, 0)], [("wo", q, tp) for tp in range(4)])
    return panels


def plan_schedule(panels):
    order = []
    at = [0]
    index = {p["name"]: i for i, p in enumerate(panels)}

    def parts_of(kind):
        return 1 if kind[0] == "up" else 4

    def conv_all(i):
        order.extend(("conv", i, j) for j in range(panels[i]["nk"] // 2))

    def dense(*names, between=()):
        parts = []
        for n in names:
            i = index[n]
            assert i == at[0], (n, panels[at[0]]["name"])
            at[0] += 1
            groups = panels[i]["groups"]
            total = sum(parts_of(k) for k in groups)
            chunks = panels[i + 1]["nk"] // 2 if i + 1 < len(panels) else 0
            made = p = 0
            for g, kind in enumerate(groups):
                for part in range(parts_of(kind)):
                    steps = []
                    while made < chunks and made * total * 3 <= p * chunks * 4:
                        steps.append(("conv", i + 1, made))
                        made += 1
                    steps.append(("mm", i, g, part))
                    p += 1
                    if part == parts_of(kind) - 1:
                        steps.append(("evac", i, g))
                    if kind == ("gate", 3, kind[-2], 0) and kind[-2] and part == 2:
                        steps.append(("merged_pair", kind[-2] - 1))
                    parts.append(steps)
            parts[-1].extend(("conv", i + 1, j) for j in range(made, chunks))
        for step in between:
            if step is not None:
                order.append(step)
            elif parts:
                order.extend(parts.pop(0))
        for steps in parts:
            order.extend(steps)

    def norm(which, n):
        order.append(("norm_stats", which, n))
        for tt in range(n):
            order.append(("norm_tile", which, tt))

    merge = lambda i: [f"merge{i}{q}" for q in range(4)]
    norm("x", TT // 2)
    conv_all(0)
    rest = [x for tt in range(TT // 2, TT) for x in (("norm_tile", "x", tt), None, None)]
    dense("lx", "lg", between=[("norm_stats", "x", TT)] + rest + [None] * 9 + [("lru_pre",)])
    lru = [("lru_dir", d, t) for d in range(2) for t in range(2)] + [("lru_fin",)]
    lru = [x for step in lru for x in [step] + [None] * 8]
    dense("glr_nba", "gqk", "gv", between=lru)
    gla = []
    for d in range(2):
        for name in ("pre", "sp", "scan", "exp", "mul", "kt"):
            gla += [("gla_" + name, d)] + [None] * (3 if name != "kt" else 0)
        gla += [("gla_s", d, 0)]
        for i in range(TT):
            gla += [None] + [("gla_s", d, i + 1)] * (i + 1 < TT) + [None, ("gla_o", d, i)]
    dense(*merge(1), between=gla)
    dense("gog", "dq", "dk", "dv", between=[("fin", "gla")] + [None] * 16 + [("fin_gate", "gla")] + [None] * 6 + [("fin_tr", "gla")])
    diff = [("diff_pre",), ("diff_z", 0), ("diff_z", 1), ("diff_qk", 0), ("diff_exp", 0), ("diff_comb", 0)]
    for u in range(NH * TT):
        more = u + 1 < NH * TT
        diff += [("diff_qk", u + 1)] * more + [("diff_z", u + 2)] * (u + 2 < NH * TT) + [("diff_tr", u, 0), None] + [("diff_exp", u + 1)] * more
        diff += [("diff_tr", u, 1), None] + [("diff_comb", u + 1)] * more + [("diff_pv", u)] + [None] * (u % 2)
    dense(*merge(0), between=diff)
    gdn = [("fin", "diff")] + [None] * 10 + [("fin_tr", "diff")] + [None] * 6
    gdn += [("gdn_conv", "nq"), ("gdn_scal",)] + [None] * 5 + [("gdn_silu", "nq")] + [None] * 3 + [("gdn_ss", "nq")] + [None] * 4
    gdn += [("gdn_norm", "nq"), ("gdn_gam",)] + [None] * 4
    gdn += [("gdn_conv", "nk")] + [None] * 5 + [("gdn_silu", "nk")] + [None] * 3 + [("gdn_ss", "nk")] + [None] * 4
    gdn += [("gdn_norm", "nk")] + [None] * 2 + [("gdn_tm", "nk")] + [None] * 2
    gdn += [("gdn_conv", "nv")] + [None] * 5 + [("gdn_silu", "nv")] + [None] * 3 + [("gdn_tm", "nv"), ("gdn_kb", 0)]
    for i in range(TT):
        for part in range(9):
            gdn += [("gdn", i, part)] + [None] * (1, 2, 1, 1, 1, 1, 1, 1, 0)[part]
            if part == 3 and i + 1 < TT:
                gdn += [("gdn_kb", i + 1)]
    dense("nq", "nk", "nv", *merge(2), between=gdn)
    dense("nz", between=[("fin", "gdn")])
    order.extend([("fin_gate", "gdn"), ("fin_tr", "gdn")])
    order.append(("x_again",))
    dense(*merge(3))
    order.append(("merged_pair", KT - 1))
    late = [None] * 3 + [("norm_stats", "mem", 2)] + [None] * 5 + [("norm_tile", "mem", 0)] + [None] * 4 + [("norm_tile", "mem", 1)]
    late += [None] * (64 - late.count(None)) + [("norm_stats", "x1", TT)] + [None] * 6
    for tt in range(TT):
        late += [("norm_tile", "x1", tt)] + [None] * 3
    late += [None] * (64 + 32 + 18 - late.count(None))
    last = 2 * NH - 1
    for g in range(last + 1):
        late += [("xattn_s", g), None, None, ("xattn_n", g), None] + [("xattn_o", g - 1)] * (g > 0) + [None, ("xattn_t", g), None, None, None]
    late += [("xattn_o", last)]
    dense(*[f"mix{q}" for q in range(4)], *[f"wk{q}" for q in range(4)], *[f"wv{q}" for q in range(4)],
          *[f"wq{q}" for q in range(4)], between=late)
    order.append(("experts_first",))
    first = [None] * 8
    for m in range(2):
        for half in range(2):
            first += [("first_pair", m, half)] + [None] * 12
    dense(*[f"wo{q}" for q in range(4)], between=first)
    order.append(("norm_stats", "x2", TT))
    for tt in range(TT):
        order.append(("norm_tile", "x2", tt))
        if tt:
            order.append(("router", tt - 1))
    order.append(("router", TT - 1))
    return order


def build(nc, A, out, known):
    panels = plan_panels(A)
    schedule = plan_schedule(panels)
    counters = {}

    gid, chunk0, nchunk = {}, {}, 0
    for i, p in enumerate(panels):
        chunk0[i] = nchunk
        nchunk += p["nk"] // 2
        for g in range(len(p["groups"])):
            gid[i, g] = len(gid)
    last_group = {i: gid[i, len(p["groups"]) - 1] for i, p in enumerate(panels)}
    kind_of = [k for p in panels for k in p["groups"]]

    with ExitStack() as ctx:
        def sem(name):
            return ctx.enter_context(nc.semaphore(name))

        def counter(name):
            if name not in counters:
                counters[name] = Counter(sem(name), name, known)
            return counters[name]

        SB = ctx.enter_context(nc.sbuf_tensor("arena", [P, 52992], F32))
        PS = ctx.enter_context(nc.psum_tensor("psum", [P, 8, 512], F32))

        def f32(off, *shape):
            n = 1
            for s in shape:
                n *= s
            v = SB[:, off:off + n]
            if len(shape) == 2:
                v = v.rearrange("p (a b) -> p a b", b=shape[1])
            if len(shape) == 3:
                v = v.rearrange("p (a b c) -> p a b c", b=shape[1], c=shape[2])
            return v

        def f16(off, *shape):
            n = 1
            for s in shape:
                n *= s
            v = SB[:, off:off + n // 2].bitcast(F16)
            if len(shape) == 2:
                v = v.rearrange("p (a b) -> p a b", b=shape[1])
            if len(shape) == 3:
                v = v.rearrange("p (a b c) -> p a b c", b=shape[1], c=shape[2])
            return v

        at = [0]

        def take(n):
            at[0] += n
            return at[0] - n

        ident, inc_f, inc_b, st_f, st_b, ones, bd64 = (f32(take(P), P) for _ in range(7))
        gla_bd = f32(take(256), 256)
        nmask = f16(take(7 * P), 14, P)
        cols = f32(take(NCOLS), NCOLS)
        rows = f32(take(NROWS), NROWS)
        small = take(3840 - at[0])
        H = (f16(take(4096), KT, T), f16(take(4096), KT, T))
        H_OFF = at[0] - 8192
        MG_OFF = take(8192)
        merged = f32(MG_OFF, KT, T)
        YP_OFF = take(4096)
        Y = [(f16(YP_OFF + 2048 * s, 2, T), f16(YP_OFF + 2048 * s + 1024, 2, T)) for s in range(2)]
        LAND = [f32(take(512), 2, 256) for _ in range(NLAND)]
        W = [(f16(take(1280), 10, 256), f16(take(1280), 10, 256)) for _ in range(2)]
        SG_OFF = take(2048)
        SG = [f32(SG_OFF + 512 * s, 512) for s in range(4)]
        gain_row = f32(SG_OFF, D)
        BR = take(0)
        BR_N = 52992 - BR
        X = f32(BR + 8192, TT, D)
        MP = (f16(BR, KT, T), f16(BR + 4096, KT, T))
        XH = [f32(BR + 16384 + 1024 * s, D) for s in range(2)]
        SQ = f32(BR + 18432, D)
        sc0 = small

        def scol(n):
            nonlocal sc0
            sc0 += n
            assert sc0 <= 3840
            return f32(sc0 - n, n)

        norm_ss = scol(8)
        norm_r = scol(8)
        norm_sq = scol(4 * TT).rearrange("p (t q) -> p t q", q=4)
        eps_col = scol(1)
        lneighth = scol(1)
        fin_ss = scol(32)
        fin_r = scol(32)
        MEMT = (f16(MG_OFF, KT, 256), f16(MG_OFF + 1024, KT, 256))
        MEM = f32(MG_OFF + 2048, 2, D)
        XK = (f16(MG_OFF + 4096, KT, 256), f16(MG_OFF + 5120, KT, 256))
        XV = (f16(MG_OFF + 6144, 2, D), f16(MG_OFF + 7168, 2, D))
        H2 = H
        XQ = MP
        XO = XQ
        XP = [f32(YP_OFF + 1024 * s, 4, 256) for s in range(2)]
        XPT = [(f16(YP_OFF + 2048 + 1024 * s, 2, 512), f16(YP_OFF + 2560 + 1024 * s, 2, 512)) for s in range(2)]
        o = BR
        LXP = SB[:, o:o + 2056].rearrange("p (a b) -> p a b", b=1028)
        LU = f32(o + 2056, 2, T)
        LG_ = f32(o + 4104, 2, T)
        LHS = f32(o + 6152, 2, T)
        LR_, LI_, LA_, LTH, LM, LXI, LH1 = (f32(o + 8200 + 1024 * j, T) for j in range(7))
        LW = f32(MG_OFF, 8, P)
        GQK = f32(BR, 2, T)
        TA, TB, TC = (f32(BR + 2048 + 1024 * j, T) for j in range(3))
        GS = f32(BR + 2048, 256)
        GST = [f32(BR + 5120 + 512 * s, 512) for s in range(2)]
        GO = f32(BR + 6144, TT, 256)
        QBD = f32(BR + 8192, NH, T)
        GOGT = f32(BR + 8192, TT, 256)
        GTMP = f32(BR + 8192 + 2048, TT, 256)
        QT_ = f32(BR + 12288, T)
        KTM = f32(BR + 13312, TT, P)
        GSM = f32(BR + 14336, TT, 256)
        GLRT = f32(BR + 16384, T)
        GVT = f32(BR + 17408, TT, 256)
        LRUP = scol(256)
        g_em, g_ee, g_eem, g_mid, g_end = (scol(TT) for _ in range(5))
        DQT = (f16(BR, 2, T), f16(BR + 1024, 2, T))
        DKT = (f16(BR + 2048, 2, T), f16(BR + 3072, 2, T))
        DVT = f32(BR + 4096, TT, 256)
        DO = f32(BR + 6144, TT, 256)
        DW = f32(BR + 8192, 1920)
        DWH = f32(BR + 10112, 1920)
        DS = [f32(BR + 12032 + 2048 * s, 2, T) for s in range(2)]
        DAT = [f32(BR + 16128 + 1024 * s, TT, P) for s in range(2)]
        DQZ = [tuple(f16(BR + 18176 + 128 * s + 64 * q, P) for q in range(2)) for s in range(8)]
        DQT_BOTH = f16(BR, 2, 2, T)
        DQZ_BOTH = [f16(BR + 18176 + 128 * s, 2, P) for s in range(8)]
        DTMP = f32(BR + 16128, TT, 256)
        d_lam = scol(4)
        d_mx = [scol(2) for _ in range(2)]
        d_l = [scol(2) for _ in range(2)]
        d_rl = [scol(2) for _ in range(2)]
        d_c = [scol(1) for _ in range(2)]
        NQ = f32(BR, 2, T)
        NK = f32(BR + 2048, 2, T)
        NKT = f32(BR + 4096, TT, 256)
        NVT = f32(BR + 6144, TT, 256)
        NO = f32(BR + 8192, TT, 256)
        NS = [f32(BR + 10240 + 256 * d, 2, P) for d in range(2)]
        NKB = [f32(BR + 10752 + 512 * d, NH, P) for d in range(2)]
        UN = BR + 11776
        NLT = [f32(UN + 3840 * d, NH, P) for d in range(2)]
        NQT = [f32(UN + 3840 * d + 512, NH, P) for d in range(2)]
        NX = [f32(UN + 3840 * d + 1024, NH, P) for d in range(2)]
        NZ_ = [f32(UN + 3840 * d + 1536, NH, P) for d in range(2)]
        NY = [f32(UN + 3840 * d + 2048, NH, P) for d in range(2)]
        NKE = [f32(UN + 3840 * d + 2560, 2, P) for d in range(2)]
        NKD = [f32(UN + 3840 * d + 2816, 2, P) for d in range(2)]
        NWK = [f32(UN + 3840 * d + 3072, 2, P) for d in range(2)]
        NQD = [f32(UN + 3840 * d + 3328, 2, P) for d in range(2)]
        NVN = [f32(UN + 3840 * d + 3584, 2, P) for d in range(2)]
        RAW = [SB[:, o:o + 2056].rearrange("p (a b) -> p a b", b=1028) for o in (UN, BR + 8184)]
        RAW_OF = {"nq": RAW[0], "nk": RAW[1], "nv": RAW[0]}
        NVF = f32(UN + 2056, 2, T)
        NSQ = f32(UN + 4104, 2, T)
        NZT = f32(UN, TT, 256)
        NTMP = f32(UN + 2048, TT, 256)
        assert UN + 7680 <= 52992, UN
        NBA_ = scol(128)
        n_beta = scol(64)
        n_la = scol(64)
        n_t = [scol(64) for _ in range(4)]
        n_eg = scol(192)
        n_cd = scol(32)
        n_al = scol(8)
        BETA = n_beta.rearrange("p (d c h) -> p d c h", d=2, c=TT)
        LAd = n_la.rearrange("p (d c h) -> p d c h", d=2, c=TT)
        EG = n_eg.rearrange("p (k d c h) -> p k d c h", k=3, d=2, c=TT)
        CD = n_cd.rearrange("p (d c t) -> p d c t", d=2, c=TT)
        FIN = {
            "gla": dict(o=GO, gate=GOGT, tmp=GTMP, row=R_GLAN, scale=1.0, y=1),
            "diff": dict(o=DO, gate=None, tmp=DTMP, row=R_DIFFN, scale=0.8, y=0),
            "gdn": dict(o=NO, gate=NZT, tmp=NTMP, row=R_GDNN, scale=1.0, y=1),
        }
        l_t, l_e, l_z, l_q, l_s, l_pc, l_nc = (scol(4) for _ in range(7))
        x_mx = [scol(4) for _ in range(2)]
        x_l = [scol(4) for _ in range(2)]
        d_dot = scol(64)
        YSLOT = {1: 0, 0: 1, 2: 0, 3: 1}

        XLAND = [f32(H_OFF, KT, DE), f32(H_OFF + 4096, KT, DE), f32(H_OFF + 8192, KE, D)]
        XW = [tuple(f16(H_OFF + 12288 + 4096 * m + 2048 * s, *((KT, DE) if m < 2 else (KE, D))) for s in range(2)) for m in range(3)]
        XR = [f32(H_OFF + 24576 + 1024 * s, D) for s in range(2)]
        GU = f32(H_OFF + 26624, DE)
        GUT = tuple(f16(H_OFF + 27136 + 256 * s, KE, P) for s in range(2))
        assert H_OFF + 27648 <= SG_OFF
        o = SG_OFF + 1024
        WR = f32(o, KT, 36)
        K_INT = f32(o + 288, 88).bitcast(I32)
        K_F = f32(o + 376, 88)
        K_DESC, K_E, K_J, K_TOK = K_F[:, 0:32], K_F[:, 32:64], K_F[:, 64:80], K_F[:, 80:88]
        GATE = f32(o + 464, 2, TT)
        SLOT = f32(o + 480, 2, TT)
        SLOTU = f32(o + 496, 2 * TT).bitcast(U32)
        IDX = f32(o + 512, NBLK).bitcast(U32)
        OVI = f32(o + 561, 17).bitcast(I32)
        f_ss, f_r = f32(o + 580, TT), f32(o + 588, TT)
        K2_INT = f32(o + 600, NBLK + 1 + P).bitcast(I32)
        K2_F = f32(o + 776, NBLK + 1 + P)
        K_BLK, K_ROW = K2_F[:, 0:NBLK + 1], K2_F[:, NBLK + 1:NBLK + 1 + P]
        H3 = f32(BR, KT, T)
        XT = [tuple(f16(BR + 1024 * s + 512 * q, KT, P) for q in range(2)) for s in range(2)]
        YB = [f32(BR + 2048 + 1024 * s, 2, 512) for s in range(2)]
        SL = f32(BR + 4096, DE)
        o = BR + 4608
        r_l = f32(o, TT, 36)
        r_e, r_w, r_o1, r_o2, r_a, r_ap, r_pos, r_mk = (f32(o + 288 + 256 * j, TT, NE) for j in range(8))
        t_ge = f32(o + 288, 2 * TT, NBLK + 1)
        t_blk = f16(o + 288 + 768, 2 * TT, NBLK)
        T_ROW = f16(BR, 2 * TT, P)
        r_cmp = f32(o + 2336, 16, NE)
        o += 2848
        r_at, r_cnt, r_nov, r_inc, r_sb, r_g4, r_w4 = (f32(o + 32 * j, NE) for j in range(7))
        r_gm, r_gs, r_m1, r_m2, r_x, r_ex, r_wm = (f32(o + 224 + 8 * j, TT) for j in range(7))
        r_ov = f32(o + 280, 17)
        t_sum, t_row = f32(o + 297, 2 * TT), f32(o + 313, 2 * TT)
        YG = [f32(H_OFF + 8192 * k, TT, D) for k in range(2)]
        XH_OUT = [YG[0][:, tt, :] for tt in range(TT)]

        WSRC = tuple(A[n].rearrange("e (p k) n -> p e k n", p=P) for n in ("w1", "w3", "w2"))
        XH_D, YROWS = A["xhat"], A["yrows"]

        def row_of(which, tt):
            return (XH + XR)[tt % 4] if which == "x2" else XH[tt % 2]

        def bc(ap, *shape):
            return ap.broadcast_to(list(shape))

        def heads(ap):
            return bc(ap.unsqueeze(2), P, NH, 64)

        def over(ap, n=NH):
            return bc(ap.unsqueeze(1), P, n, P)

        def products(kind, panel):
            w = W[panel % 2]
            name = kind[0]

            def wt(c0, c1, k0=0):
                return [lambda k, q=q: w[q][:, k0 + k, c0:c1] for q in range(2)]

            def act(pair, c0, c1):
                return [lambda k, q=q: pair[q][:, k, c0:c1] for q in range(2)]

            if name in ("gv", "gog", "dv", "nz", "mix", "wo"):
                src = {"mix": MP, "wo": XO}.get(name, H)
                tp = kind[-1]
                return [((0, P), (256 * s, 256 * s + 256), act(src, (2 * tp + s) * P, (2 * tp + s + 1) * P),
                         wt(0, 256), KT) for s in range(2)]
            if name == "nba":
                return [((0, P), (16 * t, 16 * t + 16), act(H, t * P, t * P + P), wt(32, 48), KT) for t in range(TT)]
            if name == "glr":
                return [((0, 32), (0, 512), wt(0, 32), act(H, kind[2] * 512, kind[2] * 512 + 512), KT)]
            if name == "gate":
                j = kind[2] % 2
                return [((0, P), (0, 512), wt(j * P, j * P + P), act(H, kind[3] * 512, kind[3] * 512 + 512), KT)]
            if name == "up":
                j = kind[2] % 2
                return [((0, P), (0, 512), wt(j * P, j * P + P, KT),
                         act(Y[YSLOT[kind[1]]], kind[3] * 512, kind[3] * 512 + 512), 2)]
            if name == "wk":
                return [((0, P), (256 * j, 256 * j + 256), wt(j * P, j * P + P), act(MEMT, 0, 256), KT) for j in range(2)]
            if name == "wv":
                return [((0, P), (256 * m, 256 * m + 256), act(MEMT, m * P, m * P + P), wt(0, 256), KT) for m in range(2)]
            src = H2 if name == "wq" else H
            j = kind[1] % 2
            return [((0, P), (0, 512), wt(j * P, j * P + P), act(src, kind[2] * 512, kind[2] * 512 + 512), KT)]

        land = [sem(f"land{s}") for s in range(NLAND)]
        pe_mm = counter("pe_mm")
        act_hi = counter("act_w_hi")
        vec_lo = counter("vec_w_lo")

        def emptied(g):
            kind = kind_of[g]
            if kind[0] in ("up", "mix", "wo", "wk", "wv", "wq", "dq", "dk"):
                return counter("vec_evac").at(g)
            return counter("act_evac").at(g)

        block = ctx.enter_context(nc.Block())
        g_of = {k: n for n, k in enumerate(kind_of)}
        gate_no = {n: sum(k[0] == "gate" for k in kind_of[:n]) for n in range(len(kind_of))}
        par_in = sem("params_in")
        N_PAR = 4
        x_in = [sem(f"x_in{tt}") for tt in range(TT)]
        x_again = sem("x_again")
        gain_in = sem("gain_in")
        GAINS = ["x", "mem", "x1", "x2"]

        xhat_out = [sem(f"xhat_out{s}") for s in range(4)]
        wr_in = sem("router_w_in")
        LAST_MM = len(kind_of) - 1

        w_in = [[sem(f"w{n}_in{half}") for half in range(2)] for n in (1, 3, 2)]
        w_hi = [sem(f"w{n}_hi") for n in (1, 3, 2)]
        w_lo = [sem(f"w{n}_lo") for n in (1, 3, 2)]
        rows_in = [sem(f"rows_in{s}") for s in range(2)]
        y_out = [sem(f"y_out{s}") for s in range(2)]
        pe_xt, pe_a1, pe_a3, pe_gt, pe_y = (sem(f"expert_pe_{n}") for n in ("xt", "a1", "a3", "gt", "y"))
        pe_used = (pe_a1, pe_a3, pe_y)
        act_sl, act_xt, act_gt, act_y = (sem(f"expert_act_{n}") for n in ("silu", "xt", "gt", "y"))
        vec_g, vec_xt, vec_gt = (sem(f"expert_vec_{n}") for n in ("g", "xt", "gt"))
        y_in = [sem(f"y_in{tt}") for tt in range(TT)]
        out_done = sem("out_done")
        spare_rows = sem("spare_rows")

        def after(eng, semaphore, value):
            if not (isinstance(value, int) and value <= 0):
                eng.wait_ge(semaphore, value)

        def experts(eng, prologue, period, epilogue):
            prologue()
            period(0, 0, 0)
            period(1, 1, 0)
            with eng.Fori(1, NE // 2 - 1) as n:
                period(2 * n, 0, n)
                period(2 * n + 1, 1, n)
            period(NE - 2, 0, NE // 2 - 1)
            period(NE - 1, 1, NE // 2 - 1)
            epilogue()

        def known_to_be(e, last):
            return isinstance(e, int) and e == last

        def half_of(w, half):
            n = w.shape[1] // 2
            return w[:, half * n:half * n + n, :]

        def make_hi(e, m, half):
            act = nc.scalar
            act.wait_ge(w_in[m][half], 16 * e + 16)
            if half == 0:
                after(act, pe_used[m], (1, 1, 2)[m] * e)
            nc.scalar.activation(half_of(XW[m][0], half), half_of(XLAND[m], half), ACT.Copy, scale=WS).then_inc(w_hi[m], 1)

        def make_lo(e, m, half):
            nc.vector.wait_ge(w_hi[m], 2 * e + half + 1)
            nc.vector.scalar_tensor_tensor(half_of(XW[m][1], half), half_of(XLAND[m], half), WS, half_of(XW[m][0], half),
                                           ALU.mult, ALU.subtract).then_inc(w_lo[m], 1)

        def beyond(eng, body):
            number = eng.value_load(OVI[0:1, 16:17], min_val=0, max_val=NOV)
            with eng.Fori(0, NOV) as j:
                with eng.If(number > j):
                    body(j + NE, j)
            return number

        @block.tensor
        def _(pe):
            for step in schedule:
                what = step[0]
                if what == "mm":
                    i, g, part = step[1:]
                    n = gid[i, g]
                    if n >= 2 and part == 0:
                        pe.wait_ge(*emptied(n - 2))
                    bank = PS[:, n % 2, :]
                    kind = kind_of[n]
                    if part == 0 and kind[0] == "up":
                        pe.wait_ge(*counter("vec_fin").at("y", kind[1]))
                    if part == 0 and kind[0] == "mix" and g == 0:
                        pe.wait_ge(*counter("vec_pair").at("merged", KT - 1))
                    if part == 0 and kind[0] in ("wk", "wv") and g == 0:
                        pe.wait_ge(*counter("vec_norm").at("mem", "lo", 1))
                    if part == 0 and kind[0] == "wq" and g == 0:
                        pe.wait_ge(*counter("vec_norm").at("x1", "lo", TT - 1))
                    if part == 0 and kind[0] == "wo" and g == 0:
                        pe.wait_ge(*counter("vec_xattn").at("o", 2 * NH - 1))
                    if n in (0, 2) and part == 0:
                        pe.wait_ge(*counter("vec_norm").at("x", "lo", TT // 2 - 1 if n == 0 else TT - 1))
                    items = [(ip, k) + p for ip, p in enumerate(products(kind, i)) for k in range(p[4])]
                    of = len(items) if kind[0] == "up" else len(items) // 4
                    for ip, k, prt, (c0, c1), lhs, rhs, nk in items[part * of:part * of + of]:
                        if g == 0 and ip == 0 and k % 2 == 0:
                            for c in range(k // 2, panels[i]["nk"] // 2) if k + 2 >= nk else [k // 2]:
                                pe.wait_ge(*vec_lo.at(chunk0[i] + c))
                        for a, b in ((0, 0), (0, 1), (1, 0)):
                            mm = nc.tensor.matmul(bank[prt[0]:prt[1], c0:c1], lhs[a](k), rhs[b](k),
                                                  start=(k == 0 and a + b == 0), stop=(k == nk - 1 and a == 1))
                    if part == (0 if kind[0] == "up" else 3):
                        mm.then_inc(*pe_mm.mark(n))
                elif what == "norm_tile":
                    which, tt = step[1:]
                    v, a, q = counter("vec_norm"), counter("act_norm"), counter("pe_norm")
                    pe.wait_ge(*v.at(which, "xh", tt))
                    if tt >= 2 and which == "x2":
                        pe.wait_ge(*a.at(which, "hi", tt - 2, 1))
                    elif tt >= 2:
                        pe.wait_ge(*v.at(which, "lo", tt - 2))
                    elif which == "mem":
                        pe.wait_ge(*counter("vec_fin").at("y", 3))
                    elif which in ("x1", "x2"):
                        pe.wait_ge(*v.at("mem", "lo", 1))
                    elif tt == 0:
                        pe.wait_ge(*counter("pool_const").at("ident"))
                    for k in range(KT):
                        tr = nc.tensor.transpose(PS[:, 2 + 2 * (tt % 2) + k // 4, (k % 4) * P:(k % 4) * P + P],
                                                 row_of(which, tt)[:, k * P:k * P + P], ident)
                    tr.then_inc(*q.mark(which, "tr", tt))
                elif what == "lru_dir":
                    d, t = step[1:]
                    q, a = counter("pe_lru"), counter("act_lru")
                    if d + t == 0:
                        pe.wait_ge(*counter("vec_lru").at("u", 1))
                        pe.wait_ge(par_in, 16 * N_PAR)
                        pe.wait_ge(*counter("vec_norm").at("x", "lo", TT - 1))
                    else:
                        dp, tp = divmod(2 * d + t - 1, 2)
                        pe.wait_ge(*a.at("i", dp, tp))
                    for gate in range(2):
                        for half in range(2):
                            mm = nc.tensor.matmul(PS[:, 2 + 2 * gate + half, :], LW[:, 4 * d + 2 * gate + t, :],
                                                  LU[:, t, half * 512:half * 512 + 512], start=True, stop=True)
                        mm.then_inc(*q.mark("gate", d, t, gate))
                elif what == "gla_pre":
                    d = step[1]
                    q, a, v = counter("pe_gla"), counter("act_gla"), counter("vec_gla")
                    pe.wait_ge(*counter("act_evac").at(g_of["glr", 0, 1]))
                    if d == 0:
                        pe.wait_ge(*counter("act_lru").at("i", 1, 1))
                    else:
                        pe.wait_ge(*v.at("st", 0, TT - 1))
                    for half in range(2):
                        mm = nc.tensor.matmul(PS[:, 2 + half, :], LRUP[0:32, d * P:d * P + P],
                                              GLRT[0:32, half * 512:half * 512 + 512], start=True, stop=True)
                    mm.then_inc(*q.mark("z", d))
                elif what == "gla_kt":
                    d = step[1]
                    q, a, v = counter("pe_gla"), counter("act_gla"), counter("vec_gla")
                    pe.wait_ge(*v.at("kt", d))
                    if d == 1:
                        pe.wait_ge(*v.at("u", 0, TT - 2))
                    for c in range(TT):
                        mm = nc.tensor.transpose(PS[:, 6 + c // 4, (c % 4) * P:(c % 4) * P + P], TC[:, c * P:c * P + P], ident)
                        if c % 4 == 3:
                            mm.then_inc(*q.mark("ktt", d, c // 4))
                elif what == "gla_s":
                    d, i = step[1:]
                    c = i if d == 0 else TT - 1 - i
                    q, a, v = counter("pe_gla"), counter("act_gla"), counter("vec_gla")
                    cs = slice(c * P, c * P + P)
                    if i == 0:
                        pe.wait_ge(*v.at("qbd", d))
                        pe.wait_ge(*a.at("ktm", d, 1))
                        pe.wait_ge(*counter("act_evac").at(g_of["gv", 3]))
                    if i >= 2:
                        pe.wait_ge(*v.at("st", d, i - 2))
                    elif d == 1:
                        pe.wait_ge(*v.at("st", 0, TT - 2 + i))
                    pe.wait_ge(*v.at("z", d))
                    nc.tensor.matmul(PS[:, 2 + i % 2, :], TC[:, cs], QBD[:, :, cs], start=True, stop=True)\
                        .then_inc(*q.mark("s", d, i))
                    if i < TT - 1:
                        if i >= 2:
                            pe.wait_ge(*v.at("u", d, i - 2))
                        nc.tensor.matmul(PS[:, 6 + i % 2, 0:256], KTM[:, c, :], GVT[:, c, :], start=True, stop=True)\
                            .then_inc(*q.mark("u", d, i))
                elif what == "gla_o":
                    d, i = step[1:]
                    c = i if d == 0 else TT - 1 - i
                    q, a, v = counter("pe_gla"), counter("act_gla"), counter("vec_gla")
                    cs = slice(c * P, c * P + P)
                    bank = PS[:, 4 + i % 2, 0:256]
                    n = TT * d + i
                    if n >= 2:
                        dp, ip = divmod(n - 2, TT)
                        pe.wait_ge(*(a if dp == 0 else v).at("o", dp, ip))
                    pe.wait_ge(*v.at("state", d, i))
                    nc.tensor.matmul(bank, QT_[:, cs], GSM[:, c, :], start=True, stop=False)
                    pe.wait_ge(*v.at("st", d, i))
                    for h in range(NH):
                        mm = nc.tensor.matmul(bank[:, h * 64:h * 64 + 64], GST[i % 2][:, h * P:h * P + P],
                                              GVT[:, c, h * 64:h * 64 + 64], start=False, stop=h == NH - 1)
                    mm.then_inc(*q.mark("o", d, i))
                elif what == "fin_tr":
                    br = step[1]
                    q, v, a = counter("pe_fin"), counter("vec_fin"), counter("act_fin")
                    pe.wait_ge(*v.at("done", br))
                    for ft in range(2):
                        for c in range(TT):
                            tr = nc.tensor.transpose(PS[:, 2 + 2 * ft + c // 4, (c % 4) * P:(c % 4) * P + P],
                                                     FIN[br]["o"][:, c, ft * P:ft * P + P], ident)
                        tr.then_inc(*q.mark("tr", br, ft))
                elif what == "diff_qk":
                    u = step[1]
                    h, qt = divmod(u, TT)
                    q, v, po = counter("pe_diff"), counter("vec_diff"), counter("pool_diff")
                    if u == 0:
                        pe.wait_ge(*counter("act_evac").at(g_of["dv", 3]))
                        pe.wait_ge(*counter("vec_evac").at(g_of["dk", 1, 1]))
                        pe.wait_ge(*counter("vec_fin").at("y", 0))
                    pe.wait_ge(*po.at("q", u))
                    for m in range(2):
                        if u:
                            pe.wait_ge(*v.at("max", u - 1, m))
                        for half in range(2):
                            for x, y in ((0, 0), (0, 1), (1, 0)):
                                mm = nc.tensor.matmul(PS[:, 2 + 2 * m + half, :], DQZ[4 * (u % 2) + 2 * (h % 2) + m][x],
                                                      DKT[y][:, h // 2, half * 512:half * 512 + 512], start=x + y == 0, stop=x == 1)
                        mm.then_inc(*q.mark("s", u, m))
                elif what == "diff_tr":
                    u, r = step[1:]
                    q, v, a = counter("pe_diff"), counter("vec_diff"), counter("act_diff")
                    if r:
                        pe.wait_ge(*a.at("at", u, 0))
                    else:
                        pe.wait_ge(*v.at("comb", u))
                        if u:
                            pe.wait_ge(*v.at("at", u - 1, 1))
                    for k in range(4):
                        tr = nc.tensor.transpose(PS[:, 6, k * P:k * P + P], DS[u % 2][:, 0, (4 * r + k) * P:(4 * r + k + 1) * P], ident)
                    tr.then_inc(*q.mark("tr", u, r))
                elif what == "diff_pv":
                    u = step[1]
                    h, qt = divmod(u, TT)
                    q, v, a = counter("pe_diff"), counter("vec_diff"), counter("act_diff")
                    if u:
                        pe.wait_ge(*a.at("o", u - 1))
                    pe.wait_ge(*v.at("at", u, 1))
                    for k in range(TT):
                        mm = nc.tensor.matmul(PS[:, 7, 0:64], DAT[u % 2][:, k, :], DVT[:, k, h * 64:h * 64 + 64],
                                              start=k == 0, stop=k == TT - 1)
                    mm.then_inc(*q.mark("o", u))
                elif what == "gdn_ss":
                    s = step[1]
                    q, v, a = counter("pe_gdn"), counter("vec_gdnp"), counter("act_gdnp")
                    if s != "nv":
                        pe.wait_ge(*counter("vec_fin").at("y", 2))
                        pe.wait_ge(*a.at("sq", s))
                        if s == "nk":
                            pe.wait_ge(*a.at("ln", "nq", 3))
                        for j in range(4):
                            nc.tensor.matmul(PS[:, 2 + j, :], bd64, NSQ[:, j // 2, (j % 2) * 512:(j % 2) * 512 + 512],
                                             start=True, stop=True).then_inc(*q.mark("ss", s, j))
                elif what == "gdn_tm":
                    s = step[1]
                    q, v, a = counter("pe_gdn"), counter("vec_gdnp"), counter("act_gdnp")
                    dst = {"nq": NQ, "nk": NK, "nv": NVF}[s]
                    if s != "nq":
                        pe.wait_ge(*(v.at("norm", "nk") if s == "nk" else a.at("silu", "nv")))
                        for j in range(4):
                            pe.wait_ge(*(a.at("ln", "nk", j) if s == "nk" else a.at("tm", "nk", j)))
                            for cc in range(2):
                                for t in range(2):
                                    c = 2 * j + cc
                                    tr = nc.tensor.transpose(PS[:, 2 + j, cc * 256 + t * P:cc * 256 + t * P + P],
                                                             dst[:, t, c * P:c * P + P], ident)
                            tr.then_inc(*q.mark("tm", s, j))
                elif what == "gdn_gam":
                    q, v, a = counter("pe_gdn"), counter("vec_gdnp"), counter("act_gdnp")
                    pe.wait_ge(*v.at("la"))
                    for k, mats in enumerate(((inc_f, inc_b), (st_b, st_f), (ones, ones))):
                        for d in range(2):
                            mm = nc.tensor.matmul(PS[:, 6, 64 * k + 32 * d:64 * k + 32 * d + 32], mats[d],
                                                  n_la[:, 32 * d:32 * d + 32], start=True, stop=True)
                    mm.then_inc(*q.mark("gam"))
                elif what == "gdn":
                    i, part = step[1:]
                    q, v, a, po = (counter(f"{e}_gdn") for e in ("pe", "vec", "act", "pool"))
                    for d in range(2):
                        c = i if d == 0 else TT - 1 - i
                        cs = slice(c * P, c * P + P)
                        B0, B1, B2 = (PS[:, 2 + 3 * d + b, :].rearrange("p (h n) -> p h n", h=NH) for b in range(3))
                        inc = inc_b if d else inc_f
                        if part == 0:
                            if i == 0 and d == 0:
                                pe.wait_ge(*counter("act_gdnp").at("tm", "nv", 3))
                                pe.wait_ge(*counter("act_gdnp").at("eg"))
                            pe.wait_ge(*po.at("tla", i, d))
                            if i:
                                pe.wait_ge(*v.at("state", i - 1, d))
                                pe.wait_ge(*(a if i - 1 < 4 else v).at("o", i - 1, d))
                            nc.tensor.matmul(B0[:, :, :], st_f if d else st_b, NX[d], start=True, stop=True)\
                                .then_inc(*q.mark("seg", i, d))
                            pe.wait_ge(*po.at("kb", i, d, 1, 1))
                            for h in range(NH):
                                mm = nc.tensor.matmul(B1[:, h, :], NKB[d][:, h, :], NK[:, h // 2, cs], start=True, stop=True)
                            mm.then_inc(*q.mark("kk", i, d))
                            for h in range(NH):
                                mm = nc.tensor.matmul(B2[:, h, :], NKB[d][:, h, :], NQ[:, h // 2, cs], start=True, stop=True)
                            mm.then_inc(*q.mark("qk", i, d))
                        elif part == 1:
                            pe.wait_ge(*v.at("lt", i, d))
                            pe.wait_ge(*po.at("lab", i, d))
                            for h in range(NH):
                                tr = nc.tensor.transpose(B0[:, h, :], NLT[d][:, h, :], ident)
                            tr.then_inc(*q.mark("l0", i, d))
                            for t in range(2):
                                mm = nc.tensor.matmul(B1[:, t, :], NWK[d][:, t, :], inc, start=True, stop=True)
                            mm.then_inc(*q.mark("gbc", i, d))
                            pe.wait_ge(*v.at("qt", i, d))
                        elif part < 8:
                            lv = part - 1
                            if part == 2:
                                pe.wait_ge(*v.at("x", i, d, 0))
                                pe.wait_ge(*po.at("z", i, d))
                            else:
                                pe.wait_ge(*v.at("z", i, d, lv - 1))
                            for h in range(NH):
                                mm = nc.tensor.matmul(B0[:, h, :], NLT[d][:, h, :], NX[d][:, h, :], start=True, stop=True)
                            mm.then_inc(*q.mark("y", i, d, lv))
                        else:
                            pe.wait_ge(*v.at("z", i, d, 6))
                            pe.wait_ge(*po.at("kd", i, d))
                            for h in range(NH):
                                mm = nc.tensor.matmul(PS[64 * (h % 2):64 * (h % 2) + 64, 2 + 3 * d, (h // 2) * P:(h // 2) * P + P],
                                                      NKE[d][:, h // 2, (h % 2) * 64:(h % 2) * 64 + 64], NZ_[d][:, h, :],
                                                      start=True, stop=True)
                            mm.then_inc(*q.mark("wk", i, d))
                    for d in range(2):
                        c = i if d == 0 else TT - 1 - i
                        B0, B1, B2 = (PS[:, 2 + 3 * d + b, :].rearrange("p (h n) -> p h n", h=NH) for b in range(3))
                        if 2 <= part < 8:
                            lv = part - 1
                            pe.wait_ge(*v.at("yn", i, d, lv))
                            if part == 2:
                                pe.wait_ge(*a.at("qd", i, d))
                            if lv < 6:
                                for h in range(NH):
                                    mm = nc.tensor.matmul(B1[:, h, :], NZ_[d][:, h, :], NY[d][:, h, :], start=True, stop=True)
                                mm.then_inc(*q.mark("xy", i, d, lv))
                            for h in range(NH):
                                mm = nc.tensor.matmul(B2[:, h, :], NY[d][:, h, :], NZ_[d][:, h, :], start=True, stop=True)
                            mm.then_inc(*q.mark("zy", i, d, lv))
                        elif part == 8:
                            for h in range(NH):
                                nc.tensor.matmul(PS[:, 3 + 3 * d, h * 64:h * 64 + 64], NZ_[d][:, h, :],
                                                 NVT[:, c, h * 64:h * 64 + 64], start=h == 0, stop=False)
                            pe.wait_ge(*a.at("wk", i, d))
                            if i:
                                pe.wait_ge(*v.at("state", i - 1, d))
                            else:
                                pe.wait_ge(*counter("pool_gdnp").at("s0"))
                            for t in range(2):
                                mm = nc.tensor.matmul(PS[:, 3 + 3 * d, t * P:t * P + P], NWK[d][:, t, :], NS[d][:, t, :],
                                                      start=False, stop=t == 1)
                            mm.then_inc(*q.mark("v", i, d))
                    if part == 8:
                        for d in range(2):
                            c = i if d == 0 else TT - 1 - i
                            pe.wait_ge(*v.at("vn", i, d))
                            for t in range(2):
                                mm = nc.tensor.matmul(PS[:, 4 + 3 * d, t * P:t * P + P], NKD[d][:, t, :], NVN[d][:, t, :],
                                                      start=True, stop=True)
                            mm.then_inc(*q.mark("u", i, d))
                            for t in range(2):
                                nc.tensor.matmul(PS[:, 2 + 3 * d, t * P:t * P + P], NQD[d][:, t, :], NS[d][:, t, :],
                                                 start=t == 0, stop=False)
                            for h in range(NH):
                                mm = nc.tensor.matmul(PS[:, 2 + 3 * d, h * 64:h * 64 + 64], NQT[d][:, h, :],
                                                      NVN[d].rearrange("p t n -> p (t n)")[:, h * 64:h * 64 + 64],
                                                      start=False, stop=h == NH - 1)
                            mm.then_inc(*q.mark("o", i, d))
                elif what == "xattn_s":
                    g = step[1]
                    h, half = divmod(g, 2)
                    q, v, a = (counter(f"{e}_xattn") for e in ("pe", "vec", "act"))
                    pe.wait_ge(*counter("vec_evac").at(g_of["wq", 2 * h + 1, half]))
                    if g == 0:
                        pe.wait_ge(*counter("vec_norm").at("x1", "lo", TT - 1))
                    for j in range(4):
                        tt = 4 * half + j
                        if g and j % 2 == 0:
                            for jj in range(2):
                                pe.wait_ge(*a.at("p", g - 1, j + jj))
                        for k in range(2):
                            for x, y in ((0, 0), (0, 1), (1, 0)):
                                mm = nc.tensor.matmul(PS[:, 2 + j // 2, (j % 2) * 256:(j % 2) * 256 + 256],
                                                      XQ[x][:, 2 * h + k, tt * P:tt * P + P], XK[y][:, 2 * h + k, :],
                                                      start=(k == 0 and x + y == 0), stop=(k == 1 and x == 1))
                        if j % 2:
                            mm.then_inc(*q.mark("s", g, j // 2))
                elif what == "xattn_t":
                    g = step[1]
                    q, v, a = (counter(f"{e}_xattn") for e in ("pe", "vec", "act"))
                    if g:
                        pe.wait_ge(*v.at("pt", g - 1, 1))
                    for j in range(4):
                        pe.wait_ge(*v.at("pn", g, j // 2))
                        for m in range(2):
                            tr = nc.tensor.transpose(PS[:, 4 + m, j * P:j * P + P], XP[g % 2][:, j, m * P:m * P + P], ident)
                    tr.then_inc(*q.mark("t", g))
                elif what == "xattn_o":
                    g = step[1]
                    h, half = divmod(g, 2)
                    q, v, a = (counter(f"{e}_xattn") for e in ("pe", "vec", "act"))
                    pe.wait_ge(*v.at("pt", g, 1))
                    if g:
                        pe.wait_ge(*v.at("o", g - 1))
                    for j in range(2):
                        for m in range(2):
                            for x, y in ((0, 0), (0, 1), (1, 0)):
                                mm = nc.tensor.matmul(PS[:, 6 + j, :], XV[x][:, m, (2 * h + j) * P:(2 * h + j + 1) * P],
                                                      XPT[g % 2][y][:, m, :], start=(m == 0 and x + y == 0),
                                                      stop=(m == 1 and x == 1))
                        mm.then_inc(*q.mark("o", g, j))
                elif what == "router":
                    tt = step[1]
                    if tt == 0:
                        pe.wait_ge(wr_in, 16)
                        pe.wait_ge(*counter("act_xattn").at("o", 2 * NH - 1, 1))
                        pe.wait_ge(*counter("vec_xattn").at("o", 2 * NH - 1))
                    for b in range(2):
                        pe.wait_ge(*counter("act_norm").at("x2", "hi", tt, b))
                    for k in range(KT):
                        mm = nc.tensor.matmul(PS[:, 6, 36 * tt:36 * tt + 36], H3[:, k, tt * P:tt * P + P], WR[:, k, :],
                                              start=k == 0, stop=k == KT - 1)
                    mm.then_inc(*counter("pe_route").mark("logits", tt))
            q, v = counter("pe_route"), counter("vec_route")
            pe.wait_ge(*v.at("prefix", TT))
            nc.tensor.matmul(PS[:, 7, 0:TT * NE], st_f, r_a.rearrange("p t e -> p (t e)"), start=True, stop=False)
            nc.tensor.matmul(PS[:, 7, 0:TT * NE], ones, r_ap.rearrange("p t e -> p (t e)"), start=False, stop=True)\
                .then_inc(*q.mark("rank"))
            nc.tensor.matmul(PS[:, 6, 0:NE], ones, r_at, start=True, stop=True).then_inc(*q.mark("count"))
            pe.wait_ge(*v.at("table"))
            for j in range(2 * TT):
                mm = nc.tensor.matmul(PS[:, 6, 64:64 + NBLK], T_ROW[:, j, :], t_blk[:, j, :], start=j == 0, stop=j == 2 * TT - 1)
            mm.then_inc(*q.mark("table"))

            def x_tr(e, s, n):
                pe.wait_ge(rows_in[s], 16 * n + 16)
                after(pe, act_xt, 2 * e)
                after(pe, vec_xt, 2 * e)
                xs = XR[s].rearrange("p (q k) -> p k q", k=KT)
                for k in range(KT):
                    tr = nc.tensor.transpose(PS[:, k // 4, (k % 4) * P:(k % 4) * P + P], xs[:, k, :], ident)
                    if k % 4 == 3:
                        tr.then_inc(pe_xt, 1)

            def product(bank, left, right, m, e, columns, done):
                n = right[0].shape[1]
                for k in range(n):
                    if k % (n // 2) == 0:
                        pe.wait_ge(w_lo[m], 2 * e + 1 + 2 * k // n)
                    for a, b in ((0, 0), (0, 1), (1, 0)):
                        mm = nc.tensor.matmul(PS[:, bank, :], left[a][:, k, :], right[b][:, k, columns],
                                              start=k + a + b == 0, stop=(k == n - 1 and a == 1))
                mm.then_inc(done, 1)

            def up(e, s, n):
                pe.wait_ge(act_xt, 2 * e + 2)
                pe.wait_ge(vec_xt, 2 * e + 2)
                after(pe, vec_g, e)
                product(2, XT[s], XW[0], 0, e, slice(0, DE), pe_a1)
                product(3, XT[s], XW[1], 1, e, slice(0, DE), pe_a3)

            def g_tr(e):
                pe.wait_ge(vec_g, e + 1)
                after(pe, vec_gt, e)
                gs = GU.rearrange("p (q k) -> p k q", k=KE)
                for k in range(KE):
                    tr = nc.tensor.transpose(PS[:, 4, k * P:k * P + P], gs[:, k, :], ident)
                tr.then_inc(pe_gt, 1)

            def down(e):
                pe.wait_ge(vec_gt, e + 1)
                after(pe, act_y, 2 * e)
                for half in range(2):
                    product(5 + half, GUT, XW[2], 2, e, slice(half * 512, half * 512 + 512), pe_y)

            def period(e, s, n):
                up(e, s, n)
                if not known_to_be(e, NE - 1):
                    x_tr(e + 1, 1 - s, n + s)
                if not known_to_be(e, 0):
                    down(e - 1)
                g_tr(e)

            def block_beyond(e, j):
                x_tr(e, 0, j + NE // 2)
                up(e, 0, j + NE // 2)
                g_tr(e)
                down(e)

            experts(pe, lambda: x_tr(0, 0, 0), period, lambda: down(NE - 1))
            pe.wait_ge(*v.at("gates"))
            beyond(pe, block_beyond)

        @block.sync
        def _(sp):
            for step in schedule:
                if step[0] == "conv":
                    i, j = step[1:]
                    c = chunk0[i] + j
                    k = 2 * j
                    if c >= NLAND:
                        sp.wait_ge(*vec_lo.at(c - NLAND))
                    for src, k0, c0 in panels[i]["parts"]:
                        if k0 <= k < k0 + src.shape[1]:
                            sp.dma_start(LAND[c % NLAND][:, :, c0:c0 + src.shape[2]], src[:, k - k0:k - k0 + 2, :])\
                                .then_inc(land[c % NLAND], 16)
                elif step[0] == "experts_first":
                    sp.wait_ge(*pe_mm.at(g_of["wq", 7, 1]))
                    sp.wait_ge(*counter("pool_merge").at(g_of["up", 3, KT - 1, 1]))
                    sp.dma_start(WR, A["router_w"].rearrange("(k p) n -> p k n", p=P)).then_inc(wr_in, 16)
                    for m in range(3):
                        for half in range(2):
                            sp.dma_start(half_of(XLAND[m], half), half_of(WSRC[m][:, 0], half)).then_inc(w_in[m][half], 16)
                elif step[0] == "norm_tile" and step[1] == "x2":
                    tt = step[2]
                    sp.wait_ge(*counter("vec_norm").at("x2", "xh", tt))
                    sp.dma_start(XH_D[tt * P:tt * P + P, :], row_of("x2", tt)).then_inc(xhat_out[tt % 4], 16)

            sp.wait_ge(*counter("vec_norm").at("x2", "xh", TT - 1))
            sp.dma_start(gain_row, A["gains"][4].partition_broadcast(P)).then_inc(gain_in, 16)

            def load(e, m, done):
                for half in range(2):
                    sp.wait_ge(w_lo[m], 2 * done - 1 + half)
                    sp.dma_start(half_of(XLAND[m], half).unsqueeze(1), WSRC[m][:, bass.ds(e, 1), half * (KT, KT, KE)[m] // 2:(half + 1) * (KT, KT, KE)[m] // 2])\
                        .then_inc(w_in[m][half], 16)

            def ahead(e, s, n):
                for m in range(2):
                    if not (isinstance(e, int) and e >= NE - 2):
                        load(e + 2, m, e + 2)
                if not (known_to_be(e, 0) or known_to_be(e, NE - 1)):
                    load(e + 1, 2, e + 1)

            def load_beyond(e, j):
                expert = sp.value_load(OVI[0:1, bass.ds(j, 1)], min_val=0, max_val=NE - 1)
                for m in range(3):
                    load(expert, m, e)

            experts(sp, lambda: [load(1, m, 1) for m in range(3)], ahead, lambda: None)
            sp.wait_ge(*counter("vec_route").at("gates"))
            beyond(sp, load_beyond)
            for tt in range(TT):
                sp.wait_ge(*counter("vec_final").at("out", tt))
                sp.dma_start(out[tt * P:tt * P + P, :], XH_OUT[tt]).then_inc(out_done, 16)
            sp.wait_ge(out_done, 16 * TT)

        landed, n_land = {}, [0] * NLAND
        for i, p in enumerate(panels):
            for k in range(0, p["nk"], 2):
                c = chunk0[i] + k // 2
                n_land[c % NLAND] += 16 * sum(k0 <= k < k0 + s.shape[1] for s, k0, c0 in p["parts"])
                landed[c] = n_land[c % NLAND]

        @block.scalar
        def _(act):
            S = nc.scalar
            for step in schedule:
                what = step[0]
                if what == "conv":
                    i, j = step[1:]
                    c = chunk0[i] + j
                    act.wait_ge(land[c % NLAND], landed[c])
                    if j == 0 and i >= 2:
                        act.wait_ge(*pe_mm.at(last_group[i - 2]))
                    wide = max(c0 + s.shape[2] for s, _, c0 in panels[i]["parts"])
                    S.activation(W[i % 2][0][:, 2 * j:2 * j + 2, 0:wide], LAND[c % NLAND][:, :, 0:wide],
                                 ACT.Copy, scale=WS).then_inc(*act_hi.mark(c))
                elif what == "evac":
                    i, g = step[1:]
                    n = gid[i, g]
                    kind = kind_of[n]
                    name = kind[0]
                    bank = PS[:, n % 2, :]
                    e = counter("act_evac")
                    if name != "wo":
                        act.wait_ge(*pe_mm.at(n))
                    if name == "gate":
                        if n >= 4 and kind_of[n - 4][0] == "gate":
                            act.wait_ge(*counter("vec_evac").at(n - 3))
                        if n == g_of["gate", 1, 0, 0]:
                            act.wait_ge(par_in, 16 * N_PAR)
                        S.activation(SG[gate_no[n] % 2], bank, ACT.Sigmoid, scale=1 / WS,
                                     bias=cols[:, C_MERGEB + 8 * kind[1] + kind[2]:C_MERGEB + 8 * kind[1] + kind[2] + 1])\
                            .then_inc(*e.mark(n))
                    elif name in ("wk", "wv", "wq"):
                        if name == "wk" and g == 0:
                            act.wait_ge(*counter("vec_pair").at("merged", KT - 1))
                        if n == g_of["wq", 0, 0]:
                            act.wait_ge(*pe_mm.at(g_of["mix", 3, 3]))
                        if name == "wq":
                            dst = XQ[0][:, kind[1], kind[2] * 512:kind[2] * 512 + 512]
                            src = bank
                        else:
                            src = bank.rearrange("p (a b) -> p a b", a=2)
                            q = kind[1]
                            dst = XK[0][:, 2 * q:2 * q + 2, :] if name == "wk" else XV[0][:, :, q * 256:q * 256 + 256]
                        S.activation(dst, src, ACT.Copy, scale=1 / WS).then_inc(*e.mark(n))
                    elif name == "wo":
                        c = counter("act_sq")
                        act.wait_ge(*counter("vec_evac").at(n))
                        for s in range(2):
                            if c.n:
                                act.wait_ge(*c.last())
                            tt = 2 * kind[2] + s
                            S.activation(SQ[:, 0:256], X[:, tt, kind[1] * 256:kind[1] * 256 + 256], ACT.Square,
                                         accum_out=norm_sq[:, tt, kind[1]:kind[1] + 1]).then_inc(*c.mark(kind[1], tt))
                    elif name not in ("up", "mix"):
                        if name in ("gv", "gog", "dv", "nz"):
                            dst = {"gv": GVT, "gog": GOGT, "dv": DVT, "nz": NZT}[name][:, 2 * kind[1]:2 * kind[1] + 2, :]
                            src = bank.rearrange("p (a b) -> p a b", a=2)
                        elif name == "nba":
                            dst, src = NBA_, bank[:, 0:P]
                        elif name == "glr":
                            dst, src = GLRT[0:32, kind[2] * 512:kind[2] * 512 + 512], bank[0:32, :]
                        elif name in ("lx", "nq", "nk", "nv"):
                            base = LXP if name == "lx" else RAW_OF[name]
                            dst, src = base[:, kind[1], 2 + kind[2] * 512:2 + kind[2] * 512 + 512], bank
                        else:
                            base = {"lg": LG_, "gqk": GQK, "dq": DQT[0], "dk": DKT[0]}[name]
                            dst, src = base[:, kind[1], kind[2] * 512:kind[2] * 512 + 512], bank
                        if name == "lx" and g == 2:
                            act.wait_ge(*counter("pe_norm").at("x", "tr", TT - 1))
                        if g == 0:
                            if name == "gqk":
                                act.wait_ge(*counter("vec_lru").at("u", 1))
                            elif name == "gog":
                                act.wait_ge(*counter("pe_gla").at("o", 1, TT - 1))
                            elif name in ("dq", "dk", "dv"):
                                act.wait_ge(*counter("pe_gla").at("o", 1, TT - 1))
                            elif name == "nq":
                                act.wait_ge(*counter("pe_diff").at("tr", NH * TT - 1, 1))
                            elif name == "nk":
                                act.wait_ge(*counter("pe_fin").at("tr", "diff", 1))
                                act.wait_ge(*counter("vec_fin").at("y", 2))
                            elif name == "nv":
                                act.wait_ge(*counter("vec_gdnp").at("conv", "nq", 1))
                            elif name == "nz":
                                act.wait_ge(*counter("pe_gdn").at("o", TT - 1, 1))
                                act.wait_ge(*counter("vec_gdn").at("state", TT - 1, 1))
                        S.activation(dst, src, ACT.Copy, scale=1 / WS).then_inc(*e.mark(n))
                elif what == "norm_stats":
                    which, n = step[1:]
                    a = counter("act_norm")
                    if which == "x":
                        src = X
                    if which == "x" and n < TT:
                        for tt in range(TT):
                            S.dma_start(X[:, tt, :], A["x"][tt * P:tt * P + P, :]).then_inc(x_in[tt], 16)
                            if tt == 0:
                                S.dma_start(gain_row, A["gains"][0].partition_broadcast(P)).then_inc(gain_in, 16)
                        S.dma_start(cols, A["cols"]).then_inc(par_in, 16)
                        S.dma_start(rows, A["rows"].partition_broadcast(P)).then_inc(par_in, 16)
                        S.dma_start(LW, A["lru_w"]).then_inc(par_in, 16)
                        S.dma_start(LRUP[0:32, :], A["lr_up"]).then_inc(par_in, 16)
                    elif which == "x":
                        pass
                    elif which == "mem":
                        act.wait_ge(*counter("vec_pair").at("merged", KT - 1))
                        act.wait_ge(*counter("pool_merge").at(g_of["up", 3, KT - 1, 1]))
                        act.wait_ge(*counter("vec_evac").at(g_of["up", 3, KT - 1, 1]))
                        S.dma_start(gain_row, A["gains"][1].partition_broadcast(P)).then_inc(gain_in, 16)
                        S.dma_start(MEM[:, 0, :], A["mem"][0:P, :]).then_inc(x_in[0], 16)
                        S.dma_start(MEM[:, 1, :], A["mem"][P:2 * P, :]).then_inc(x_in[1], 16)
                        src = MEM
                    else:
                        act.wait_ge(*counter("vec_norm").at(*(("mem", "xh", 1) if which == "x1" else ("x1", "xh", TT - 1))))
                        S.dma_start(gain_row, A["gains"][GAINS.index(which)].partition_broadcast(P)).then_inc(gain_in, 16)
                        src = X
                    t0 = TT // 2 if which == "x" and n == TT else 0
                    key = (which, n) if which == "x" else (which,)
                    for tt in range(t0, 0 if which == "x2" else n):
                        if which == "x":
                            act.wait_ge(x_in[tt], 16)
                        elif which == "mem":
                            act.wait_ge(x_in[tt], 32)
                        elif tt == 0:
                            act.wait_ge(*counter("vec_evac").at(g_of["mix", 3, 3]))
                        if tt or which != "x":
                            act.wait_ge(*a.last())
                        S.activation(SQ, src[:, tt, :], ACT.Square, accum_out=norm_ss[:, tt:tt + 1]).then_inc(*a.mark(which, "sq", tt))
                    act.wait_ge(*(counter("vec_norm").at("x2", "ss") if which == "x2" else a.last()))
                    act.wait_ge(*counter("pool_const").at("cols"))
                    S.activation(norm_r[:, t0:n], norm_ss[:, t0:n], ACT.Ln, scale=1 / D, bias=eps_col).then_inc(*a.mark(*key, "ln"))
                    act.wait_ge(*a.last())
                    S.activation(norm_r[:, t0:n], norm_r[:, t0:n], ACT.Exp, scale=-0.5).then_inc(*a.mark(*key, "r"))
                elif what == "norm_tile":
                    which, tt = step[1:]
                    dst = {"x": H, "mem": MEMT, "x1": H2, "x2": (H3,)}[which]
                    a = counter("act_norm")
                    act.wait_ge(*counter("pe_norm").at(which, "tr", tt))
                    if which == "mem" and tt == 0:
                        act.wait_ge(*counter("vec_pair").at("merged", KT - 1))
                    for b in range(2):
                        S.activation(dst[0][:, 4 * b:4 * b + 4, tt * P:tt * P + P],
                                     PS[:, 2 + 2 * (tt % 2) + b, :].rearrange("p (k n) -> p k n", k=4), ACT.Copy)\
                            .then_inc(*a.mark(which, "hi", tt, b))
                elif what == "lru_pre":
                    a, v = counter("act_lru"), counter("vec_lru")
                    act.wait_ge(par_in, 16 * N_PAR)
                    act.wait_ge(*counter("vec_lru").at("nabs"))
                    S.activation(l_e, l_t, ACT.Exp).then_inc(*a.mark("e"))
                elif what == "lru_dir":
                    d, t = step[1:]
                    a, v, q = counter("act_lru"), counter("vec_lru"), counter("pe_lru")
                    k = 2 * d + t
                    act.wait_ge(*q.at("gate", d, t, 0))
                    if k:
                        dp, tp = divmod(k - 1, 2)
                        act.wait_ge(*v.at("hs", dp, tp))
                        act.wait_ge(*counter("pool_lru").at("iu", dp, tp))
                    S.activation(LR_, PS[:, 2:4, :].rearrange("p a b -> p (a b)"), ACT.Sigmoid,
                                 bias=cols[:, C_LBA + k:C_LBA + k + 1]).then_inc(*a.mark("r", d, t))
                    act.wait_ge(*q.at("gate", d, t, 1))
                    S.activation(LI_, PS[:, 4:6, :].rearrange("p a b -> p (a b)"), ACT.Sigmoid,
                                 bias=cols[:, C_LBX + k:C_LBX + k + 1]).then_inc(*a.mark("i", d, t))
                    act.wait_ge(*v.at("coef"))
                    act.wait_ge(*a.last())
                    S.activation(LA_, LR_, ACT.Exp, scale=l_nc[:, k:k + 1]).then_inc(*a.mark("a", d, t))
                    S.activation(LTH, LR_, ACT.Tanh, scale=l_pc[:, k:k + 1]).then_inc(*a.mark("th", d, t))
                    act.wait_ge(*v.at("m", d, t))
                    S.activation(LM, LM, ACT.Sqrt).then_inc(*a.mark("s", d, t))
                elif what == "lru_fin":
                    a, v = counter("act_lru"), counter("vec_lru")
                    act.wait_ge(*counter("act_evac").at(g_of["lg", 1, 1]))
                    S.activation(LG_[:, :, :], LG_[:, :, :], ACT.Gelu_apprx_tanh).then_inc(*a.mark("gelu"))
                    act.wait_ge(*v.at("y32"))
                    act.wait_ge(spare_rows, 16)
                    S.activation(Y[0][0], LHS, ACT.Copy).then_inc(*a.mark("yhi"))
                elif what == "gla_sp":
                    d = step[1]
                    a, v, q = counter("act_gla"), counter("vec_gla"), counter("pe_gla")
                    act.wait_ge(*v.at("z", d))
                    S.activation(TB, TA, ACT.Abs).then_inc(*a.mark("abs", d))
                    act.wait_ge(*a.last())
                    S.activation(TB, TB, ACT.Exp, scale=-1.0).then_inc(*a.mark("exp", d))
                    act.wait_ge(*a.last())
                    S.activation(TB, TB, ACT.Ln, bias=1.0).then_inc(*a.mark("ln", d))
                elif what == "gla_exp":
                    d = step[1]
                    a, v, q = counter("act_gla"), counter("vec_gla"), counter("pe_gla")
                    act.wait_ge(*v.at("td", d))
                    S.activation(g_em, g_mid, ACT.Exp, scale=-1 / 16).then_inc(*a.mark("em", d))
                    S.activation(g_ee, g_end, ACT.Exp, scale=-1 / 16).then_inc(*a.mark("ee", d))
                    S.activation(TC, TA, ACT.Exp, scale=1 / 16).then_inc(*a.mark("e2", d))
                    S.activation(TB, TA, ACT.Exp, scale=-1 / 16).then_inc(*a.mark("e1", d))
                elif what == "gla_kt":
                    d = step[1]
                    a, v, q = counter("act_gla"), counter("vec_gla"), counter("pe_gla")
                    for b in range(2):
                        act.wait_ge(*q.at("ktt", d, b))
                        if d and b == 0:
                            act.wait_ge(*q.at("u", 0, TT - 2))
                        S.activation(KTM[:, 4 * b:4 * b + 4, :], PS[:, 6 + b, :].rearrange("p (c n) -> p c n", c=4), ACT.Copy)\
                            .then_inc(*a.mark("ktm", d, b))
                elif what == "gla_o":
                    d, i = step[1:]
                    if d == 0:
                        act.wait_ge(*counter("pe_gla").at("o", d, i))
                        S.activation(GO[:, i, :], PS[:, 4 + i % 2, 0:256], ACT.Copy).then_inc(*counter("act_gla").mark("o", d, i))
                elif what == "fin":
                    br = step[1]
                    f = FIN[br]
                    a, v = counter("act_fin"), counter("vec_fin")
                    if br == "diff":
                        act.wait_ge(*counter("act_diff").at("o", NH * TT - 1))
                    if br == "gdn":
                        act.wait_ge(*counter("act_gdn").at("o", 3, 1))
                        act.wait_ge(*counter("vec_gdn").at("o", TT - 1, 1))
                        act.wait_ge(*counter("vec_gdn").at("state", TT - 1, 1))
                    if br == "gla":
                        act.wait_ge(*counter("vec_gla").at("o", 1, TT - 1))
                        act.wait_ge(*counter("pe_gla").at("o", 1, TT - 1))
                    S.activation(f["tmp"], f["o"], ACT.Square).then_inc(*a.mark("sq", br))
                    act.wait_ge(*v.at("ss", br))
                    S.activation(fin_r, fin_ss, ACT.Ln, scale=1 / 64, bias=eps_col).then_inc(*a.mark("ln", br))
                    act.wait_ge(*a.last())
                    S.activation(fin_r, fin_r, ACT.Exp, scale=-0.5).then_inc(*a.mark("r", br))
                elif what == "fin_gate":
                    br = step[1]
                    f = FIN[br]
                    a, v = counter("act_fin"), counter("vec_fin")
                    if f["gate"] is not None:
                        act.wait_ge(*counter("act_evac").at(g_of[{"gla": "gog", "gdn": "nz"}[br], 3]))
                        S.activation(f["gate"], f["gate"], ACT.Silu).then_inc(*a.mark("silu", br))
                elif what == "fin_tr":
                    br = step[1]
                    a = counter("act_fin")
                    slot = FIN[br]["y"]
                    if br != "gla":
                        act.wait_ge(*pe_mm.at(g_of["up", {"diff": 1, "gdn": 0}[br], KT - 1, 1]))
                    for ft in range(2):
                        act.wait_ge(*counter("pe_fin").at("tr", br, ft))
                        S.activation(Y[slot][0][:, ft, :], PS[:, 2 + 2 * ft:4 + 2 * ft, :].rearrange("p a b -> p (a b)"),
                                     ACT.Copy).then_inc(*a.mark("yhi", br, ft))
                elif what == "diff_pre":
                    a = counter("act_diff")
                    act.wait_ge(*counter("pool_diff").at("iota"))
                    S.activation(DW, DWH.bitcast(I32), ACT.Abs).then_inc(*a.mark("w"))
                    act.wait_ge(*counter("vec_diff").at("dots"))
                    S.activation(d_lam[:, 0:2], d_lam[:, 0:2], ACT.Exp).then_inc(*a.mark("lam"))
                elif what == "diff_exp":
                    u = step[1]
                    a, v = counter("act_diff"), counter("vec_diff")
                    if u >= 2:
                        act.wait_ge(*v.at("comb", u - 2))
                    for m in range(2):
                        act.wait_ge(*v.at("nm", u, m))
                        S.activation(DS[u % 2][:, m, :], DS[u % 2][:, m, :], ACT.Exp, scale=32 ** -0.5,
                                     bias=d_mx[u % 2][:, m:m + 1], accum_out=d_l[u % 2][:, m:m + 1])\
                            .then_inc(*a.mark("p", u, m))
                elif what == "diff_tr" and step[2] == 0:
                    u = step[1]
                    a, q = counter("act_diff"), counter("pe_diff")
                    act.wait_ge(*q.at("tr", u, 0))
                    if u >= 2:
                        act.wait_ge(*q.at("o", u - 2))
                    S.activation(DAT[u % 2][:, 0:4, :], PS[:, 6, :].rearrange("p (k n) -> p k n", k=4), ACT.Copy)\
                        .then_inc(*a.mark("at", u, 0))
                elif what == "diff_pv":
                    u = step[1]
                    h, qt = divmod(u, TT)
                    a, q = counter("act_diff"), counter("pe_diff")
                    act.wait_ge(*q.at("o", u))
                    S.activation(DO[:, qt, h * 64:h * 64 + 64], PS[:, 7, 0:64], ACT.Copy, scale=d_rl[u % 2][:, 0:1])\
                        .then_inc(*a.mark("o", u))
                elif what == "gdn_silu":
                    s = step[1]
                    a, v, q = counter("act_gdnp"), counter("vec_gdnp"), counter("pe_gdn")
                    dst = {"nq": NQ, "nk": NK, "nv": NVF}[s]
                    act.wait_ge(*v.at("conv", s, 1))
                    S.activation(dst, dst, ACT.Silu).then_inc(*a.mark("silu", s))
                    if s != "nv":
                        act.wait_ge(*a.last())
                        if s == "nk":
                            act.wait_ge(*v.at("norm", "nq"))
                        S.activation(NSQ, dst, ACT.Square).then_inc(*a.mark("sq", s))
                elif what == "gdn_ss":
                    s = step[1]
                    a, v, q = counter("act_gdnp"), counter("vec_gdnp"), counter("pe_gdn")
                    if s != "nv":
                        for j in range(4):
                            act.wait_ge(*q.at("ss", s, j))
                            if j == 0:
                                act.wait_ge(*q.at("ss", s, 3))
                            S.activation(NSQ[:, j // 2, (j % 2) * 512:(j % 2) * 512 + 512], PS[:, 2 + j, :], ACT.Ln,
                                         bias=eps_col).then_inc(*a.mark("ln", s, j))
                        act.wait_ge(*a.last())
                        S.activation(NSQ, NSQ, ACT.Exp, scale=-0.5, bias=lneighth if s == "nq" else 0.0).then_inc(*a.mark("rn", s))
                elif what == "gdn_tm":
                    s = step[1]
                    a, v, q = counter("act_gdnp"), counter("vec_gdnp"), counter("pe_gdn")
                    if s != "nq":
                        for j in range(4):
                            act.wait_ge(*q.at("tm", s, j))
                            S.activation((NKT if s == "nk" else NVT)[:, 2 * j:2 * j + 2, :],
                                         PS[:, 2 + j, :].rearrange("p (c n) -> p c n", c=2), ACT.Copy).then_inc(*a.mark("tm", s, j))
                elif what == "gdn_scal":
                    a, v = counter("act_gdnp"), counter("vec_gdnp")
                    ba = NBA_.rearrange("p (c k d h) -> p k d c h", c=TT, k=2, d=2)
                    act.wait_ge(*counter("act_evac").at(g_of["nba", 0]))
                    for d in range(2):
                        S.activation(BETA[:, d], ba[:, 0, d], ACT.Sigmoid).then_inc(*a.mark("beta", d))
                    act.wait_ge(*v.at("nabs"))
                    S.activation(n_t[1], n_t[1], ACT.Exp).then_inc(*a.mark("e"))
                    S.activation(n_al, rows[:, R_ALOG:R_ALOG + 8], ACT.Exp).then_inc(*a.mark("al"))
                elif what == "gdn_gam":
                    a, v = counter("act_gdnp"), counter("vec_gdnp")
                    act.wait_ge(*counter("pe_gdn").at("gam"))
                    S.activation(n_eg, PS[:, 6, 0:192], ACT.Exp).then_inc(*a.mark("eg"))
                elif what == "gdn":
                    i, part = step[1:]
                    a, v, q = (counter(f"{e}_gdn") for e in ("act", "vec", "pe"))
                    for d in range(2):
                        c = i if d == 0 else TT - 1 - i
                        if part == 0:
                            act.wait_ge(*q.at("seg", i, d))
                            S.activation(NY[d], PS[:, 2 + 3 * d, :].rearrange("p (h n) -> p h n", h=NH), ACT.Exp)\
                                .then_inc(*a.mark("dt", i, d))
                        elif part == 1:
                            act.wait_ge(*q.at("gbc", i, d))
                            S.activation(NQD[d], PS[:, 3 + 3 * d, 0:256].rearrange("p (t n) -> p t n", t=2), ACT.Exp)\
                                .then_inc(*a.mark("qd", i, d))
                        elif part == 8:
                            act.wait_ge(*q.at("wk", i, d))
                            S.activation(NWK[d], PS[:, 2 + 3 * d, 0:256].rearrange("p (t n) -> p t n", t=2), ACT.Copy, scale=-1.0)\
                                .then_inc(*a.mark("wk", i, d))
                    if part == 8 and i < 4:
                        for d in range(2):
                            c = i if d == 0 else TT - 1 - i
                            act.wait_ge(*q.at("o", i, d))
                            S.activation(NO[:, c, :], PS[:, 2 + 3 * d, 0:256], ACT.Copy).then_inc(*a.mark("o", i, d))
                elif what == "x_again":
                    act.wait_ge(*counter("pe_fin").at("tr", "gdn", 1))
                    act.wait_ge(*counter("vec_fin").at("y", 3))
                    for tt in range(TT):
                        S.dma_start(X[:, tt, :], A["x"][tt * P:tt * P + P, :]).then_inc(x_again, 16)
                elif what == "merged_pair":
                    a = counter("act_pair")
                    for k in [step[1]]:
                        act.wait_ge(*counter("pool_merge").at(g_of["up", 3, k, 1]))
                        S.activation(MP[0][:, k, :], merged[:, k, :], ACT.Copy).then_inc(*a.mark("merged", k))
                elif what == "first_pair":
                    if step[1:] == (0, 0):
                        act.wait_ge(*counter("pe_xattn").at("o", 2 * NH - 1, 1))
                    make_hi(0, *step[1:])
                elif what == "xattn_s":
                    g = step[1]
                    a, v, q = (counter(f"{e}_xattn") for e in ("act", "vec", "pe"))
                    for j in range(4):
                        act.wait_ge(*v.at("mx", g, j // 2))
                        if j == 0 and g >= 2:
                            act.wait_ge(*q.at("t", g - 2))
                        S.activation(XP[g % 2][:, j, :], PS[:, 2 + j // 2, (j % 2) * 256:(j % 2) * 256 + 256], ACT.Exp,
                                     scale=1 / 16, bias=x_mx[g % 2][:, j:j + 1], accum_out=x_l[g % 2][:, j:j + 1])\
                            .then_inc(*a.mark("p", g, j))
                elif what == "xattn_t":
                    g = step[1]
                    a, v, q = (counter(f"{e}_xattn") for e in ("act", "vec", "pe"))
                    for m in range(2):
                        act.wait_ge(*q.at("t", g))
                        if g >= 2 and m == 0:
                            act.wait_ge(*q.at("o", g - 2, 1))
                        S.activation(XPT[g % 2][0][:, m, :], PS[:, 4 + m, :], ACT.Copy).then_inc(*a.mark("pt", g, m))
                elif what == "xattn_o":
                    g = step[1]
                    a, v, q = (counter(f"{e}_xattn") for e in ("act", "vec", "pe"))
                    h, half = divmod(g, 2)
                    for j in range(2):
                        act.wait_ge(*q.at("o", g, j))
                        S.activation(XO[0][:, 2 * h + j, half * 512:half * 512 + 512], PS[:, 6 + j, :], ACT.Copy)\
                            .then_inc(*a.mark("o", g, j))


            a, v = counter("act_route"), counter("vec_route")
            act.wait_ge(*pe_mm.at(LAST_MM))
            for half in range(2):
                make_hi(0, 2, half)
            act.wait_ge(*v.at("group_diff"))
            S.activation(r_g4, r_g4, ACT.Exp).then_inc(*a.mark("group_exp"))
            act.wait_ge(*v.at("top_diff"))
            S.activation(r_ex, r_x, ACT.Exp).then_inc(*a.mark("top_exp"))

            def silu(e):
                act.wait_ge(pe_a1, e + 1)
                after(act, vec_g, e)
                S.activation(SL, PS[:, 2, :], ACT.Silu, scale=1 / WS).then_inc(act_sl, 1)

            def x_copy(e, s):
                for half in range(2):
                    act.wait_ge(pe_xt, 2 * e + 1 + half)
                    S.activation(XT[s][0][:, 4 * half:4 * half + 4, :], PS[:, half, :].rearrange("p (k n) -> p k n", k=4),
                                 ACT.Copy).then_inc(act_xt, 1)

            def y_copy(e, s, n):
                after(act, y_out[s], 16 * n)
                for half in range(2):
                    act.wait_ge(pe_y, 2 * e + 1 + half)
                    S.activation(YB[s][:, half, :], PS[:, 5 + half, :], ACT.Copy, scale=1 / (WS * GSCALE)).then_inc(act_y, 1)
                act.wait_ge(act_y, 2 * e + 2)
                S.dma_start(YROWS[bass.ds(e * P, P), :], YB[s].rearrange("p a b -> p (a b)")).then_inc(y_out[s], 16)

            def g_copy(e):
                act.wait_ge(pe_gt, e + 1)
                S.activation(GUT[0], PS[:, 4, :].rearrange("p (k n) -> p k n", k=KE), ACT.Copy).then_inc(act_gt, 1)

            def period(e, s, n):
                silu(e)
                more = not known_to_be(e, NE - 1)
                if more:
                    make_hi(e + 1, 0, 0)
                    make_hi(e + 1, 0, 1)
                    make_hi(e + 1, 1, 0)
                    x_copy(e + 1, 1 - s)
                    make_hi(e + 1, 1, 1)
                if not known_to_be(e, 0):
                    y_copy(e - 1, 1 - s, n - 1 + s)
                    make_hi(e, 2, 0)
                g_copy(e)
                if not known_to_be(e, 0):
                    make_hi(e, 2, 1)

            def block_beyond(e, j):
                for m in range(3):
                    make_hi(e, m, 0)
                    make_hi(e, m, 1)
                x_copy(e, 0)
                silu(e)
                g_copy(e)
                y_copy(e, 0, j + NE // 2)

            experts(act, lambda: x_copy(0, 0), period, lambda: y_copy(NE - 1, 1, NE // 2 - 1))
            act.wait_ge(*v.at("gates"))
            beyond(act, block_beyond)
            a, v = counter("act_final"), counter("vec_final")
            for t0, t1 in BATCHES:
                for tt in range(t0, t1):
                    act.wait_ge(*v.at("sum", tt))
                    S.activation(YG[1][:, tt, :], X[:, tt, :], ACT.Square, accum_out=f_ss[:, tt:tt + 1]).then_inc(*a.mark("sq", tt))
                act.wait_ge(*a.last())
                S.activation(f_r[:, t0:t1], f_ss[:, t0:t1], ACT.Ln, scale=1 / D, bias=eps_col).then_inc(*a.mark("ln", t0))
                act.wait_ge(*a.last())
                S.activation(f_r[:, t0:t1], f_r[:, t0:t1], ACT.Exp, scale=-0.5).then_inc(*a.mark("r", t0))

        @block.vector
        def _(dve):
            V = nc.vector

            def log1p(x, z, q, s, c, key, half=1.0):
                dve.wait_ge(*c.last())
                V.tensor_scalar(z, x, 2.0, None, ALU.add).then_inc(*c.mark(key, "d"))
                dve.wait_ge(*c.last())
                V.reciprocal(z, z).then_inc(*c.mark(key, "r"))
                dve.wait_ge(*c.last())
                V.tensor_tensor(z, z, x, ALU.mult).then_inc(*c.mark(key, "z"))
                dve.wait_ge(*c.last())
                V.tensor_tensor(q, z, z, ALU.mult).then_inc(*c.mark(key, "q"))
                dve.wait_ge(*c.last())
                V.tensor_scalar(s, q, 1 / 17, None, ALU.mult).then_inc(*c.mark(key, 17))
                for n in (15, 13, 11, 9, 7, 5, 3):
                    dve.wait_ge(*c.last())
                    V.scalar_tensor_tensor(s, s, 1 / n, q, ALU.add, ALU.mult).then_inc(*c.mark(key, n))
                dve.wait_ge(*c.last())
                V.scalar_tensor_tensor(s, s, 1.0, z, ALU.add, ALU.mult).then_inc(*c.mark(key, 1))
                dve.wait_ge(*c.last())
                V.tensor_scalar(s, s, 2.0 / half, None, ALU.mult).then_inc(*c.mark(key, "s"))
                dve.wait_ge(*c.last())

            for step in schedule:
                what = step[0]
                if what == "conv":
                    i, j = step[1:]
                    c = chunk0[i] + j
                    wide = max(c0 + s.shape[2] for s, _, c0 in panels[i]["parts"])
                    dve.wait_ge(*act_hi.at(c))
                    V.scalar_tensor_tensor(W[i % 2][1][:, 2 * j:2 * j + 2, 0:wide], LAND[c % NLAND][:, :, 0:wide], WS,
                                           W[i % 2][0][:, 2 * j:2 * j + 2, 0:wide], ALU.mult, ALU.subtract)\
                        .then_inc(*vec_lo.mark(c))
                elif what == "evac":
                    i, g = step[1:]
                    n = gid[i, g]
                    kind = kind_of[n]
                    name = kind[0]
                    bank = PS[:, n % 2, :]
                    e = counter("vec_evac")
                    if name == "up":
                        first = kind[1] == 1
                        dst = merged[:, kind[2], kind[3] * 512:kind[3] * 512 + 512]
                        o = gate_no[n] - 1
                        dve.wait_ge(*counter("act_evac").at(n - 1))
                        dve.wait_ge(*pe_mm.at(n))
                        if not first:
                            dst = SG[2 + o % 2]
                            if n >= 4 and kind_of[n - 4][0] == "up" and kind_of[n - 4][1] != 1:
                                dve.wait_ge(*counter("pool_merge").at(n - 4))
                            elif o >= 34 and n >= 4 and kind_of[n - 4][0] != "up":
                                prev = [m for m in range(n) if kind_of[m][0] == "up"][-2]
                                dve.wait_ge(*counter("pool_merge").at(prev))
                        V.scalar_tensor_tensor(dst, bank, 1 / WS, SG[o % 2], ALU.mult, ALU.mult).then_inc(*e.mark(n))
                    elif name in ("mix", "wo"):
                        dve.wait_ge(*pe_mm.at(n))
                        if n == g_of["mix", 0, 0]:
                            dve.wait_ge(x_again, 16 * TT)
                        xs = X[:, 2 * kind[2]:2 * kind[2] + 2, kind[1] * 256:kind[1] * 256 + 256]
                        V.scalar_tensor_tensor(xs, bank.rearrange("p (a b) -> p a b", a=2), 1 / WS, xs, ALU.mult, ALU.add)\
                            .then_inc(*e.mark(n))
                    elif name in ("wk", "wv", "wq", "dq", "dk"):
                        dve.wait_ge(*counter("act_evac").at(n))
                        if name in ("dq", "dk"):
                            hi, lo = ((DQT if name == "dq" else DKT)[s][:, kind[1], kind[2] * 512:kind[2] * 512 + 512] for s in range(2))
                            src = bank
                        elif name == "wq":
                            hi, lo = (XQ[s][:, kind[1], kind[2] * 512:kind[2] * 512 + 512] for s in range(2))
                            src = bank
                        else:
                            q = kind[1]
                            src = bank.rearrange("p (a b) -> p a b", a=2)
                            hi, lo = ((XK[s][:, 2 * q:2 * q + 2, :] if name == "wk" else XV[s][:, :, q * 256:q * 256 + 256])
                                      for s in range(2))
                        V.scalar_tensor_tensor(lo, src, 1 / WS, hi, ALU.mult, ALU.subtract).then_inc(*e.mark(n))
                elif what == "norm_stats" and step[1] == "x2":
                    dve.wait_ge(*counter("act_sq").at(3, TT - 1))
                    V.tensor_reduce(norm_ss, norm_sq, AX.X, ALU.add).then_inc(*counter("vec_norm").mark("x2", "ss"))
                elif what == "norm_tile":
                    which, tt = step[1:]
                    v, a = counter("vec_norm"), counter("act_norm")
                    src = MEM if which == "mem" else X
                    dst = {"x": H, "mem": MEMT, "x1": H2, "x2": None}[which]
                    if tt == 0:
                        dve.wait_ge(gain_in, 16 * (GAINS.index(which) + 1))
                        dve.wait_ge(*(a.at("x", TT // 2, "r") if which == "x" else a.at(which, "r")))
                    if which == "x" and tt == TT // 2:
                        dve.wait_ge(*a.at("x", TT, "r"))
                    if tt >= (4 if which == "x2" else 2):
                        dve.wait_ge(*counter("pe_norm").at(which, "tr", tt - (4 if which == "x2" else 2)))
                        if which == "x2":
                            dve.wait_ge(xhat_out[tt % 4], 16 * (tt // 4))
                    V.scalar_tensor_tensor(row_of(which, tt), src[:, tt, :], norm_r[:, tt:tt + 1], gain_row, ALU.mult, ALU.mult)\
                        .then_inc(*v.mark(which, "xh", tt))
                    for b in range(0 if which == "x2" else 2):
                        dve.wait_ge(*a.at(which, "hi", tt, b))
                        ts = slice(tt * P, tt * P + P)
                        V.tensor_tensor(dst[1][:, 4 * b:4 * b + 4, ts],
                                        PS[:, 2 + 2 * (tt % 2) + b, :].rearrange("p (k n) -> p k n", k=4),
                                        dst[0][:, 4 * b:4 * b + 4, ts], ALU.subtract)\
                            .then_inc(*v.mark(*((which, "lo", tt) if b else (which, "lo0", tt))))
                elif what == "lru_pre":
                    v = counter("vec_lru")
                    dve.wait_ge(par_in, 16 * N_PAR)
                    lam = cols[:, C_LAM:C_LAM + 4]
                    V.tensor_scalar(l_q, lam, -1.0, None, ALU.mult).then_inc(*v.mark("neg"))
                    dve.wait_ge(*v.last())
                    V.tensor_tensor(l_t, lam, l_q, ALU.min).then_inc(*v.mark("nabs"))
                    dve.wait_ge(*counter("act_lru").at("e"))
                    log1p(l_e, l_z, l_q, l_s, v, "log1p")
                    V.tensor_scalar(l_q, lam, -1.0, 0.0, ALU.mult, ALU.max).then_inc(*v.mark("relu"))
                    dve.wait_ge(*v.last())
                    V.tensor_tensor(l_s, l_s, l_q, ALU.add).then_inc(*v.mark("sp"))
                    dve.wait_ge(*v.last())
                    V.tensor_scalar(l_pc, l_s, 8.0, None, ALU.mult).then_inc(*v.mark("pc"))
                    V.tensor_scalar(l_nc, l_s, -8.0, None, ALU.mult).then_inc(*v.mark("coef"))
                    dve.wait_ge(*counter("act_evac").at(g_of["lx", 1, 1]))
                    dve.wait_ge(*counter("pool_const").at("lxpad"))
                    for t in range(2):
                        w = cols[:, C_LCW + 4 * t:C_LCW + 4 * t + 4]
                        V.tensor_scalar(LU[:, t, :], LXP[:, t, 0:T], w[:, 0:1], cols[:, C_LCB + t:C_LCB + t + 1], ALU.mult, ALU.add)\
                            .then_inc(*v.mark("u0", t))
                        for j in range(1, 4):
                            dve.wait_ge(*v.last())
                            V.scalar_tensor_tensor(LU[:, t, :], LXP[:, t, j:j + T], w[:, j:j + 1], LU[:, t, :], ALU.mult, ALU.add)\
                                .then_inc(*v.mark(*(("u", t) if j == 3 else ("uj", t, j))))
                elif what == "lru_dir":
                    d, t = step[1:]
                    v, a = counter("vec_lru"), counter("act_lru")
                    dve.wait_ge(*a.at("th", d, t))
                    V.tensor_tensor(LM, LA_, LA_, ALU.mult).then_inc(*v.mark("a2", d, t))
                    dve.wait_ge(*v.last())
                    V.scalar_tensor_tensor(LM, LM, 1.0, LTH, ALU.add, ALU.mult).then_inc(*v.mark("m", d, t))
                    dve.wait_ge(*a.at("s", d, t))
                    dve.wait_ge(*counter("pool_lru").at("iu", d, t))
                    V.tensor_tensor(LXI, LM, LI_, ALU.mult).then_inc(*v.mark("xin", d, t))
                    dve.wait_ge(*v.last())
                    if d == 0:
                        V.tensor_tensor_scan(LHS[:, t, :], LA_, LXI, 0.0, ALU.mult, ALU.add).then_inc(*v.mark("hs", d, t))
                    else:
                        V.tensor_tensor_scan(LH1[:, ::-1], LA_[:, ::-1], LXI[:, ::-1], 0.0, ALU.mult, ALU.add)\
                            .then_inc(*v.mark("h1", d, t))
                        dve.wait_ge(*v.last())
                        V.tensor_tensor(LHS[:, t, :], LHS[:, t, :], LH1, ALU.add).then_inc(*v.mark("hs", d, t))
                elif what == "lru_fin":
                    v, a = counter("vec_lru"), counter("act_lru")
                    dve.wait_ge(*a.at("gelu"))
                    dve.wait_ge(*v.last())
                    V.tensor_tensor(LHS, LHS, LG_, ALU.mult).then_inc(*v.mark("y32"))
                    dve.wait_ge(*a.at("yhi"))
                    V.tensor_tensor(Y[0][1], LHS, Y[0][0], ALU.subtract).then_inc(*counter("vec_fin").mark("y", 1))
                elif what == "gla_pre":
                    d = step[1]
                    v, a, q = counter("vec_gla"), counter("act_gla"), counter("pe_gla")
                    dve.wait_ge(*q.at("z", d))
                    if d:
                        dve.wait_ge(*q.at("o", 0, TT - 1))
                    V.tensor_scalar(TA, PS[:, 2:4, :].rearrange("p a b -> p (a b)"), cols[:, C_LRB + d:C_LRB + d + 1], -1.0,
                                    ALU.add, ALU.mult).then_inc(*v.mark("z", d))
                elif what == "gla_scan":
                    d = step[1]
                    v, a, q = counter("vec_gla"), counter("act_gla"), counter("pe_gla")
                    dve.wait_ge(*a.at("ln", d))
                    dve.wait_ge(*v.at("z", d))
                    V.scalar_tensor_tensor(TA, TA, 0.0, TB, ALU.max, ALU.add).then_inc(*v.mark("sp", d))
                    dve.wait_ge(*v.last())
                    for c in range(TT):
                        cs = slice(c * P, c * P + P)
                        if d == 0:
                            i_ = V.tensor_tensor_scan(TB[:, cs], ones, TA[:, cs], 0.0, ALU.mult, ALU.add)
                        else:
                            i_ = V.tensor_tensor_scan(TB[:, cs][:, ::-1], ones, TA[:, cs][:, ::-1], 0.0, ALU.mult, ALU.add)
                        i_.then_inc(*v.mark("scan", d, c))
                    dve.wait_ge(*v.last())
                    sums = TB.rearrange("p (c n) -> p c n", c=TT)
                    mid, end = (63, 127) if d == 0 else (64, 0)
                    V.tensor_copy(g_mid, sums[:, :, mid]).then_inc(*v.mark("mid", d))
                    V.tensor_copy(g_end, sums[:, :, end]).then_inc(*v.mark("end", d))
                    dve.wait_ge(*v.at("mid", d))
                    V.tensor_tensor(TA.rearrange("p (c n) -> p c n", c=TT), sums, bc(g_mid.unsqueeze(2), P, TT, P), ALU.subtract)\
                        .then_inc(*v.mark("td", d))
                elif what == "gla_mul":
                    d = step[1]
                    v, a, q = counter("vec_gla"), counter("act_gla"), counter("pe_gla")
                    dve.wait_ge(*a.at("e2", d))
                    V.tensor_tensor(TC, TC, GQK[:, 1, :], ALU.mult).then_inc(*v.mark("kt", d))
                    dve.wait_ge(*a.at("e1", d))
                    if d == 0:
                        dve.wait_ge(*counter("pool_gla").at("qbd0"))
                    V.scalar_tensor_tensor(QT_, GQK[:, 0, :], 32 ** -0.5, TB, ALU.mult, ALU.mult).then_inc(*v.mark("qt", d))
                    for h in range(NH):
                        hp = slice(32 * h, 32 * h + 32)
                        V.scalar_tensor_tensor(QBD[hp, h, :], GQK[hp, 0, :], 32 ** -0.5, TB[hp, :], ALU.mult, ALU.mult)\
                            .then_inc(*v.mark(*(("qbd", d) if h == NH - 1 else ("qbdh", d, h))))
                    V.tensor_copy(g_eem, TB.rearrange("p (c n) -> p c n", c=TT)[:, :, end]).then_inc(*v.mark("eem", d))
                elif what == "gla_s":
                    d, i = step[1:]
                    c = i if d == 0 else TT - 1 - i
                    nxt = i + 1 if d == 0 else TT - 2 - i
                    v, a, q = counter("vec_gla"), counter("act_gla"), counter("pe_gla")
                    if i == 0:
                        V.memset(GSM[:, c, :], 0.0).then_inc(*v.mark("state", d, 0))
                        dve.wait_ge(*v.last())
                        V.memset(GS, 0.0).then_inc(*v.mark("s0", d))
                    if i < TT - 1:
                        dve.wait_ge(*q.at("u", d, i))
                        dve.wait_ge(*(v.at("s", d, i - 1) if i else v.at("s0", d)))
                        V.scalar_tensor_tensor(GSM[:, nxt, :], PS[:, 6 + i % 2, 0:256], g_eem[:, c:c + 1], gla_bd, ALU.mult, ALU.mult)\
                            .then_inc(*v.mark("u", d, i))
                        dve.wait_ge(*v.last())
                        V.scalar_tensor_tensor(GS, GS, g_ee[:, c:c + 1], GSM[:, nxt, :], ALU.mult, ALU.add).then_inc(*v.mark("s", d, i))
                        dve.wait_ge(*v.last())
                        V.tensor_scalar(GSM[:, nxt, :], GS, g_em[:, nxt:nxt + 1], None, ALU.mult).then_inc(*v.mark("state", d, i + 1))
                    dve.wait_ge(*q.at("s", d, i))
                    if i >= 2:
                        dve.wait_ge(*q.at("o", d, i - 2))
                    V.scalar_tensor_tensor(GST[i % 2].rearrange("p (h n) -> p h n", h=NH),
                                           PS[:, 2 + i % 2, :].rearrange("p (h n) -> p h n", h=NH), 3e38,
                                           over(inc_b if d else inc_f), ALU.min, ALU.mult).then_inc(*v.mark("st", d, i))
                elif what == "gla_o":
                    d, i = step[1:]
                    c = i if d == 0 else TT - 1 - i
                    v, a, q = counter("vec_gla"), counter("act_gla"), counter("pe_gla")
                    if d == 1:
                        dve.wait_ge(*q.at("o", d, i))
                        dve.wait_ge(*a.at("o", 0, TT - 1))
                        V.tensor_tensor(GO[:, c, :], PS[:, 4 + i % 2, 0:256], GO[:, c, :], ALU.add).then_inc(*v.mark("o", d, i))
                elif what == "fin":
                    br = step[1]
                    f = FIN[br]
                    v, a = counter("vec_fin"), counter("act_fin")
                    o3, t3 = (x.rearrange("p c (h n) -> p (c h) n", h=NH) for x in (f["o"], f["tmp"]))
                    dve.wait_ge(*a.at("sq", br))
                    V.tensor_reduce(fin_ss, t3, AX.X, ALU.add).then_inc(*v.mark("ss", br))
                    dve.wait_ge(*a.at("r", br))
                    V.tensor_tensor(o3, o3, bc(fin_r.unsqueeze(2), P, 32, 64), ALU.mult).then_inc(*v.mark("n", br))
                    dve.wait_ge(*v.last())
                    gain = rows[:, f["row"]:f["row"] + 64]
                    if f["scale"] != 1.0:
                        V.scalar_tensor_tensor(o3, o3, f["scale"], bc(gain.unsqueeze(1), P, 32, 64), ALU.mult, ALU.mult)\
                            .then_inc(*v.mark("g" if f["gate"] is not None else "done", br))
                    else:
                        V.tensor_tensor(o3, o3, bc(gain.unsqueeze(1), P, 32, 64), ALU.mult).then_inc(*v.mark("g", br))
                elif what == "fin_gate":
                    br = step[1]
                    f = FIN[br]
                    v, a = counter("vec_fin"), counter("act_fin")
                    if f["gate"] is not None:
                        dve.wait_ge(*a.at("silu", br))
                        dve.wait_ge(*v.at("g", br))
                        V.tensor_tensor(f["o"], f["o"], f["gate"], ALU.mult).then_inc(*v.mark("done", br))
                elif what == "fin_tr":
                    br = step[1]
                    v, a = counter("vec_fin"), counter("act_fin")
                    slot = FIN[br]["y"]
                    idx = {"gla": 0, "diff": 2, "gdn": 3}[br]
                    for ft in range(2):
                        dve.wait_ge(*a.at("yhi", br, ft))
                        V.tensor_tensor(Y[slot][1][:, ft, :], PS[:, 2 + 2 * ft:4 + 2 * ft, :].rearrange("p a b -> p (a b)"),
                                        Y[slot][0][:, ft, :], ALU.subtract).then_inc(*v.mark("y" if ft else "y0", idx))
                elif what == "diff_pre":
                    v, a = counter("vec_diff"), counter("act_diff")
                    dl = rows[:, R_DL:R_DL + 128].rearrange("p (s k n) -> p s k n", s=2, k=2)
                    dots = d_dot.rearrange("p (s n) -> p s n", s=2)
                    V.tensor_tensor(dots, dl[:, :, 0, :], dl[:, :, 1, :], ALU.mult).then_inc(*v.mark("prod"))
                    dve.wait_ge(*v.last())
                    V.tensor_reduce(d_lam[:, 0:2], dots, AX.X, ALU.add).then_inc(*v.mark("dots"))
                    dve.wait_ge(*a.at("lam"))
                    V.tensor_tensor(d_lam[:, 2:3], d_lam[:, 1:2], d_lam[:, 0:1], ALU.subtract).then_inc(*v.mark("lam0"))
                    dve.wait_ge(*v.last())
                    V.tensor_scalar(d_lam[:, 3:4], d_lam[:, 2:3], -0.2, None, ALU.add).then_inc(*v.mark("lam"))
                elif what == "diff_qk":
                    u = step[1]
                    h, qt = divmod(u, TT)
                    v, a, q = counter("vec_diff"), counter("act_diff"), counter("pe_diff")
                    if qt == 0:
                        dve.wait_ge(*a.at("w"))
                        if u:
                            dve.wait_ge(*v.at("max", u - 1, 1))
                        V.tensor_scalar(DWH, DW, -(2.0 ** (-8.0 * (h + 1) / NH)) * 32 ** 0.5, None, ALU.mult).then_inc(*v.mark("wh", h))
                        dve.wait_ge(*v.last())
                    for m in range(2):
                        dve.wait_ge(*q.at("s", u, m))
                        if u >= 2 and m == 0:
                            dve.wait_ge(*q.at("tr", u - 2, 1))
                            dve.wait_ge(*v.at("comb", u - 2))
                        V.tensor_tensor_reduce(out=DS[u % 2][:, m, :], in0=PS[:, 2 + 2 * m:4 + 2 * m, :].rearrange("p a b -> p (a b)"),
                                               in1=DWH[:, 896 - P * qt:896 - P * qt + T], scale=1.0, scalar=-3e38,
                                               op0=ALU.add, op1=ALU.max, accum_out=d_mx[u % 2][:, m:m + 1])\
                            .then_inc(*v.mark("max", u, m))
                        dve.wait_ge(*v.last())
                        V.tensor_scalar(d_mx[u % 2][:, m:m + 1], d_mx[u % 2][:, m:m + 1], -32 ** -0.5, None, ALU.mult)\
                            .then_inc(*v.mark("nm", u, m))
                elif what == "diff_comb":
                    u = step[1]
                    v, a, q = counter("vec_diff"), counter("act_diff"), counter("pe_diff")
                    dve.wait_ge(*a.at("p", u, 1))
                    if u >= 2:
                        dve.wait_ge(*a.at("o", u - 2))
                    V.reciprocal(d_rl[u % 2], d_l[u % 2]).then_inc(*v.mark("rl", u))
                    dve.wait_ge(*v.last())
                    V.tensor_tensor(d_c[u % 2], d_l[u % 2][:, 0:1], d_rl[u % 2][:, 1:2], ALU.mult).then_inc(*v.mark("c0", u))
                    dve.wait_ge(*v.last())
                    V.tensor_tensor(d_c[u % 2], d_c[u % 2], d_lam[:, 3:4], ALU.mult).then_inc(*v.mark("c", u))
                    dve.wait_ge(*v.last())
                    V.scalar_tensor_tensor(DS[u % 2][:, 0, :], DS[u % 2][:, 1, :], d_c[u % 2], DS[u % 2][:, 0, :], ALU.mult, ALU.add)\
                        .then_inc(*v.mark("comb", u))
                elif what == "diff_tr" and step[2] == 1:
                    u = step[1]
                    v, q = counter("vec_diff"), counter("pe_diff")
                    dve.wait_ge(*q.at("tr", u, 1))
                    if u >= 2:
                        dve.wait_ge(*q.at("o", u - 2))
                    V.tensor_copy(DAT[u % 2][:, 4:8, :], PS[:, 6, :].rearrange("p (k n) -> p k n", k=4)).then_inc(*v.mark("at", u, 1))
                elif what == "gdn_conv":
                    s = step[1]
                    v, a = counter("vec_gdnp"), counter("act_gdnp")
                    dst = {"nq": NQ, "nk": NK, "nv": NVF}[s]
                    k = {"nq": 0, "nk": 2, "nv": 4}[s]
                    dve.wait_ge(*counter("act_evac").at(g_of[s, 1, 1]))
                    if s != "nv":
                        dve.wait_ge(*counter("pool_gdnp").at(*(("pad",) if s == "nq" else ("pad", 1))))
                    if s == "nv":
                        dve.wait_ge(*v.at("norm", "nk"))
                    for t in range(2):
                        w = cols[:, C_GCW + 4 * (k + t):C_GCW + 4 * (k + t) + 4]
                        V.tensor_scalar(dst[:, t, :], RAW_OF[s][:, t, 0:T], w[:, 0:1], None, ALU.mult).then_inc(*v.mark("c0", s, t))
                        for j in range(1, 4):
                            dve.wait_ge(*v.last())
                            V.scalar_tensor_tensor(dst[:, t, :], RAW_OF[s][:, t, j:j + T], w[:, j:j + 1], dst[:, t, :], ALU.mult, ALU.add)\
                                .then_inc(*v.mark(*(("conv", s, t) if j == 3 else ("cj", s, t, j))))
                elif what == "gdn_norm":
                    s = step[1]
                    v, a = counter("vec_gdnp"), counter("act_gdnp")
                    dst = {"nq": NQ, "nk": NK, "nv": NVF}[s]
                    if s != "nv":
                        dve.wait_ge(*a.at("rn", s))
                        V.tensor_tensor(dst, dst, NSQ, ALU.mult).then_inc(*v.mark("norm", s))
                elif what == "gdn_scal":
                    v, a = counter("vec_gdnp"), counter("act_gdnp")
                    ba = NBA_.rearrange("p (c k d h) -> p k d c h", c=TT, k=2, d=2)
                    t3 = [x.rearrange("p (d c h) -> p d c h", d=2, c=TT) for x in n_t]
                    dtb = rows[:, R_DTB:R_DTB + 8].rearrange("p (d h) -> p d h", d=2)
                    al = n_al.rearrange("p (d h) -> p d h", d=2)
                    dve.wait_ge(*counter("act_evac").at(g_of["nba", 0]))
                    for d in range(2):
                        V.tensor_tensor(t3[0][:, d], ba[:, 1, d], bc(dtb[:, d].unsqueeze(1), P, TT, NH), ALU.add).then_inc(*v.mark("a", d))
                    dve.wait_ge(*v.last())
                    V.tensor_scalar(n_t[2], n_t[0], -1.0, None, ALU.mult).then_inc(*v.mark("neg"))
                    dve.wait_ge(*v.last())
                    V.tensor_tensor(n_t[1], n_t[0], n_t[2], ALU.min).then_inc(*v.mark("nabs"))
                    dve.wait_ge(*a.at("e"))
                    log1p(n_t[1], n_t[2], n_t[3], n_la, v, "log1p")
                    V.scalar_tensor_tensor(n_t[0], n_t[0], 0.0, n_la, ALU.max, ALU.add).then_inc(*v.mark("sp"))
                    dve.wait_ge(*v.last())
                    dve.wait_ge(*a.at("al"))
                    for d in range(2):
                        V.scalar_tensor_tensor(LAd[:, d], t3[0][:, d], -1.0, bc(al[:, d].unsqueeze(1), P, TT, NH), ALU.mult, ALU.mult)\
                            .then_inc(*v.mark(*(("la",) if d else ("la0",))))
                elif what == "gdn_gam":
                    v, a = counter("vec_gdnp"), counter("act_gdnp")
                    dve.wait_ge(*a.at("eg"))
                    for par in range(2):
                        hp = slice(64 * par, 64 * par + 64)
                        V.tensor_copy(n_cd[hp, :].rearrange("p (a t) -> p a t", t=2),
                                      n_eg[hp, 128:192].rearrange("p (a t u) -> p a t u", t=2, u=2)[:, :, :, par])\
                            .then_inc(*v.mark("cd", par))
                elif what == "gdn":
                    i, part = step[1:]
                    v, a, q, po = (counter(f"{e}_gdn") for e in ("vec", "act", "pe", "pool"))
                    for d in range(2):
                        c = i if d == 0 else TT - 1 - i
                        B0, B1, B2 = (PS[:, 2 + 3 * d + b, :].rearrange("p (h n) -> p h n", h=NH) for b in range(3))
                        nm = lambda lv, dd: over(nmask[:, 7 * dd + lv, :])
                        if part == 0:
                            dve.wait_ge(*a.at("dt", i, d))
                            V.tensor_tensor(NLT[d], NY[d], over(st_b if d else st_f), ALU.mult).then_inc(*v.mark("dt0", i, d))
                            dve.wait_ge(*v.last())
                            V.tensor_tensor(NLT[d], NLT[d], bc(BETA[:, d, c, :].unsqueeze(2), P, NH, P), ALU.mult)\
                                .then_inc(*v.mark("dt1", i, d))
                            dve.wait_ge(*v.last())
                            dve.wait_ge(*q.at("kk", i, d))
                            V.tensor_tensor(NLT[d], B1[:, :, :], NLT[d], ALU.mult).then_inc(*v.mark("lt", i, d))
                            dve.wait_ge(*q.at("qk", i, d))
                            dve.wait_ge(*po.at("dts", i, d))
                            V.tensor_tensor(NQT[d], B2[:, :, :], NQT[d], ALU.mult).then_inc(*v.mark("qt", i, d))
                        elif part == 1:
                            dve.wait_ge(*q.at("l0", i, d))
                            V.tensor_tensor(NX[d], B0[:, :, :], nm(0, d), ALU.mult).then_inc(*v.mark("x0m", i, d))
                            dve.wait_ge(*v.last())
                            V.tensor_tensor(NX[d], NX[d], over(ident), ALU.add).then_inc(*v.mark("x", i, d, 0))
                            dve.wait_ge(*a.at("qd", i, d))
                            V.tensor_tensor(NQD[d], NQD[d], NQ[:, :, c * P:c * P + P], ALU.mult).then_inc(*v.mark("qd", i, d))
                        elif part < 8:
                            lv = part - 1
                            dve.wait_ge(*q.at("y", i, d, lv))
                            V.tensor_tensor(NY[d], B0[:, :, :], nm(lv, d), ALU.mult).then_inc(*v.mark("yn", i, d, lv))
                    for d in range(2):
                        c = i if d == 0 else TT - 1 - i
                        B0, B1, B2 = (PS[:, 2 + 3 * d + b, :].rearrange("p (h n) -> p h n", h=NH) for b in range(3))
                        if 2 <= part < 8:
                            lv = part - 1
                            dve.wait_ge(*q.at("zy", i, d, lv))
                            if lv < 6:
                                V.tensor_tensor(NX[d], B1[:, :, :], NX[d], ALU.add).then_inc(*v.mark("x", i, d, lv))
                            V.tensor_tensor(NZ_[d], B2[:, :, :], NZ_[d], ALU.add).then_inc(*v.mark("z", i, d, lv))
                        elif part == 8:
                            dve.wait_ge(*q.at("v", i, d))
                            V.tensor_tensor(NVN[d].rearrange("p t (u n) -> p (t u) n", u=2),
                                            PS[:, 3 + 3 * d, 0:256].rearrange("p (h n) -> p h n", h=NH), heads(BETA[:, d, c, :]),
                                            ALU.mult).then_inc(*v.mark("vn", i, d))
                    if part == 8:
                        for d in range(2):
                            c = i if d == 0 else TT - 1 - i
                            dve.wait_ge(*q.at("o", i, d))
                            V.tensor_tensor(NKE[d], PS[:, 4 + 3 * d, 0:256].rearrange("p (t n) -> p t n", t=2), over(bd64, 2), ALU.mult)\
                                .then_inc(*v.mark("um", i, d))
                            dve.wait_ge(*v.last())
                            for t in range(2):
                                V.scalar_tensor_tensor(NS[d][:, t, :], NS[d][:, t, :], CD[:, d, c, t:t + 1], NKE[d][:, t, :], ALU.mult, ALU.add)\
                                    .then_inc(*v.mark(*(("state", i, d) if t else ("state0", i, d))))
                            if i >= 4:
                                V.tensor_tensor(NO[:, c, :], PS[:, 2 + 3 * d, 0:256], NO[:, c, :], ALU.add).then_inc(*v.mark("o", i, d))
                elif what == "merged_pair":
                    v, a = counter("vec_pair"), counter("act_pair")
                    for k in [step[1]]:
                        dve.wait_ge(*a.at("merged", k))
                        V.tensor_tensor(MP[1][:, k, :], merged[:, k, :], MP[0][:, k, :], ALU.subtract).then_inc(*v.mark("merged", k))
                elif what == "first_pair":
                    make_lo(0, *step[1:])
                elif what == "xattn_s":
                    g = step[1]
                    v, a, q = (counter(f"{e}_xattn") for e in ("vec", "act", "pe"))
                    for j in range(2):
                        dve.wait_ge(*q.at("s", g, j))
                        if g >= 2 and j == 0:
                            dve.wait_ge(*a.at("p", g - 2, 3))
                        V.tensor_reduce(x_mx[g % 2][:, 2 * j:2 * j + 2], PS[:, 2 + j, :].rearrange("p (a b) -> p a b", a=2), AX.X, ALU.max)\
                            .then_inc(*v.mark("mx0", g, j))
                        dve.wait_ge(*v.last())
                        V.tensor_scalar(x_mx[g % 2][:, 2 * j:2 * j + 2], x_mx[g % 2][:, 2 * j:2 * j + 2], -1 / 16, None, ALU.mult)\
                            .then_inc(*v.mark("mx", g, j))
                elif what == "xattn_n":
                    g = step[1]
                    v, a, q = (counter(f"{e}_xattn") for e in ("vec", "act", "pe"))
                    for j in range(2):
                        dve.wait_ge(*a.at("p", g, 2 * j + 1))
                        V.reciprocal(x_l[g % 2][:, 2 * j:2 * j + 2], x_l[g % 2][:, 2 * j:2 * j + 2]).then_inc(*v.mark("rl", g, j))
                        dve.wait_ge(*v.last())
                        V.tensor_tensor(XP[g % 2][:, 2 * j:2 * j + 2, :], XP[g % 2][:, 2 * j:2 * j + 2, :],
                                        bc(x_l[g % 2][:, 2 * j:2 * j + 2].unsqueeze(2), P, 2, 256), ALU.mult).then_inc(*v.mark("pn", g, j))
                elif what == "xattn_t":
                    g = step[1]
                    v, a, q = (counter(f"{e}_xattn") for e in ("vec", "act", "pe"))
                    for m in range(2):
                        dve.wait_ge(*a.at("pt", g, m))
                        V.tensor_tensor(XPT[g % 2][1][:, m, :], PS[:, 4 + m, :], XPT[g % 2][0][:, m, :], ALU.subtract)\
                            .then_inc(*v.mark("pt", g, m))
                elif what == "xattn_o":
                    g = step[1]
                    h, half = divmod(g, 2)
                    v, a, q = (counter(f"{e}_xattn") for e in ("vec", "act", "pe"))
                    for j in range(2):
                        dve.wait_ge(*a.at("o", g, j))
                        hs = slice(half * 512, half * 512 + 512)
                        V.tensor_tensor(XO[1][:, 2 * h + j, hs], PS[:, 6 + j, :], XO[0][:, 2 * h + j, hs], ALU.subtract)\
                            .then_inc(*v.mark(*(("o", g) if j else ("o0", g))))


            v, a, q = counter("vec_route"), counter("act_route"), counter("pe_route")
            e4 = r_g4.rearrange("p (t g) -> p t g", g=NG)
            w4 = r_w4.rearrange("p (t g) -> p t g", g=NG)
            NEG = 1e30

            def then(instruction, *key):
                instruction.then_inc(*v.mark(*key))
                dve.wait_ge(*v.last())

            def first(dst, diff, w, n, key):
                then(V.tensor_scalar(w, diff, 0.0, None, ALU.is_ge), key, "is_max")
                then(V.tensor_tensor(w, w, bc(K_DESC[:, 32 - n:32].unsqueeze(1), P, TT, n), ALU.mult), key, "weighted")
                then(V.tensor_reduce(r_wm, w, AX.X, ALU.max), key, "first")
                then(V.tensor_tensor(dst, w, bc(r_wm.unsqueeze(2), P, TT, n), ALU.is_equal), key, "one")

            dve.wait_ge(*counter("pool_route").at("iota"))
            then(V.tensor_copy(K_F, K_INT), "constants")
            then(V.tensor_copy(K2_F, K2_INT), "constants2")
            dve.wait_ge(*q.at("logits", TT - 1))
            then(V.tensor_tensor(r_l, PS[:, 6, 0:TT * 36].rearrange("p (t n) -> p t n", n=36),
                                 bc(rows[:, R_BG:R_BG + 36].unsqueeze(1), P, TT, 36), ALU.add), "logits")
            then(V.tensor_reduce(r_gm, r_l[:, :, 0:NG], AX.X, ALU.max), "group_max")
            then(V.tensor_tensor(e4, r_l[:, :, 0:NG], bc(r_gm.unsqueeze(2), P, TT, NG), ALU.subtract), "group_diff0")
            then(V.tensor_scalar(w4, e4, 0.0, None, ALU.is_ge), "group_diff")
            then(V.tensor_tensor(w4, w4, bc(K_DESC[:, 32 - NG:32].unsqueeze(1), P, TT, NG), ALU.mult), "group_weighted")
            then(V.tensor_reduce(r_wm, w4, AX.X, ALU.max), "group_first")
            then(V.tensor_tensor(w4, w4, bc(r_wm.unsqueeze(2), P, TT, NG), ALU.is_equal), "group_one")
            then(V.tensor_scalar(w4, w4, -1.0, NEG, ALU.add, ALU.mult), "group_mask")
            for g in range(NG):
                then(V.tensor_tensor(r_e[:, :, g * GE:g * GE + GE], r_l[:, :, NG + g * GE:NG + g * GE + GE],
                                     bc(w4[:, :, g:g + 1], P, TT, GE), ALU.add), "masked", g)
            then(V.tensor_reduce(r_m1, r_e, AX.X, ALU.max), "max1")
            then(V.tensor_tensor(r_w, r_e, bc(r_m1.unsqueeze(2), P, TT, NE), ALU.subtract), "diff1")
            first(r_o1, r_w, r_w, NE, "top1")
            then(V.scalar_tensor_tensor(r_e, r_o1, -3 * NEG, r_e, ALU.mult, ALU.add), "without1")
            then(V.tensor_reduce(r_m2, r_e, AX.X, ALU.max), "max2")
            then(V.tensor_tensor(r_x, r_m2, r_m1, ALU.subtract), "top_diff")
            then(V.tensor_tensor(r_w, r_e, bc(r_m2.unsqueeze(2), P, TT, NE), ALU.subtract), "diff2")
            first(r_o2, r_w, r_w, NE, "top2")
            then(V.tensor_tensor(r_a, r_o1, r_o2, ALU.add), "both")
            then(V.tensor_scalar(r_ap[:, 0, :], r_a[:, 0, :], 0.0, None, ALU.mult), "prefix", 0)
            for t in range(1, TT + 1):
                dst = r_ap[:, t, :] if t < TT else r_at
                then(V.tensor_tensor(dst, r_ap[:, t - 1, :], r_a[:, t - 1, :], ALU.add), "prefix", t)
            dve.wait_ge(*q.at("count"))
            then(V.tensor_copy(r_cnt, PS[:, 6, 0:NE]), "count")
            then(V.tensor_scalar(r_nov, r_cnt, float(P), None, ALU.is_gt), "beyond", 1)
            for m in range(2, T // P):
                then(V.scalar_tensor_tensor(r_nov, r_cnt, float(m * P), r_nov, ALU.is_gt, ALU.add), "beyond", m)
            then(V.tensor_tensor_scan(r_inc, ones[:, 0:NE], r_nov, 0.0, ALU.mult, ALU.add), "beyond_sum")
            then(V.tensor_tensor(r_sb, r_inc, r_nov, ALU.subtract), "beyond_first")
            then(V.tensor_scalar(r_sb, r_sb, float(P), float(P * (NE - 1)), ALU.mult, ALU.add), "beyond_slot")
            then(V.scalar_tensor_tensor(r_sb, K_E, -float(P), r_sb, ALU.mult, ALU.add), "beyond_shift")
            dve.wait_ge(*q.at("rank"))
            pos = PS[:, 7, 0:TT * NE].rearrange("p (t e) -> p t e", e=NE)
            then(V.tensor_scalar(r_mk, pos, float(P), None, ALU.is_ge), "rank_beyond")
            then(V.tensor_tensor(r_mk, r_mk, bc(r_sb.unsqueeze(1), P, TT, NE), ALU.mult), "rank_shift")
            then(V.tensor_tensor(r_pos, pos, r_mk, ALU.add), "rank_shifted")
            then(V.scalar_tensor_tensor(r_pos, bc(K_E.unsqueeze(1), P, TT, NE), float(P), r_pos, ALU.mult, ALU.add), "slots")
            for k, one in enumerate((r_o1, r_o2)):
                then(V.tensor_tensor(one, one, r_pos, ALU.mult), "slot_of", k)
                then(V.tensor_reduce(SLOT[:, k, :], one, AX.X, ALU.add), "slot", k)
            slots = SLOT.rearrange("p k t -> p (k t)")
            then(V.tensor_tensor(t_ge, bc(slots.unsqueeze(2), P, 2 * TT, NBLK + 1), bc(K_BLK.unsqueeze(1), P, 2 * TT, NBLK + 1), ALU.is_ge),
                 "slot_ge")
            then(V.tensor_reduce(t_sum, t_ge[:, :, 0:NBLK], AX.X, ALU.add), "slot_block")
            then(V.scalar_tensor_tensor(t_row, t_sum, -float(P), slots, ALU.mult, ALU.add), "slot_row")
            then(V.tensor_tensor(T_ROW, bc(K_ROW.unsqueeze(1), P, 2 * TT, P), bc(t_row.unsqueeze(2), P, 2 * TT, P), ALU.is_equal),
                 "slot_row_one")
            then(V.tensor_tensor(t_blk, t_ge[:, :, 0:NBLK], t_ge[:, :, 1:NBLK + 1], ALU.subtract), "slot_block_one")
            for k in range(2):
                blk = t_blk[:, k * TT:k * TT + TT, :]
                then(V.tensor_tensor(blk, blk, bc(K_TOK.unsqueeze(2), P, TT, NBLK), ALU.mult), *(("table",) if k else ("table0",)))
            for half in range(2):
                make_lo(0, 2, half)
            dve.wait_ge(*q.at("table"))
            then(V.tensor_copy(IDX, PS[:, 6, 64:64 + NBLK]), "index")
            dve.wait_ge(*a.at("top_exp"))
            then(V.tensor_copy(SLOTU, SLOT.rearrange("p k t -> p (k t)")), "slots_int")
            then(V.tensor_reduce(r_gs, e4, AX.X, ALU.add), "group_sum")
            then(V.tensor_scalar(r_gm, r_ex, 1.0, None, ALU.add), "pair_sum")
            then(V.tensor_tensor(r_gs, r_gs, r_gm, ALU.mult), "sums")
            then(V.reciprocal(GATE[:, 0, :], r_gs), "gate0")
            then(V.tensor_tensor(GATE[:, 1, :], GATE[:, 0, :], r_ex, ALU.mult), "gate1")
            then(V.tensor_tensor(r_cmp, bc(K_J.unsqueeze(2), P, 16, NE), bc(r_inc.unsqueeze(1), P, 16, NE), ALU.is_ge), "ends")
            then(V.tensor_reduce(r_ov[:, 0:16], r_cmp, AX.X, ALU.add), "owners")
            then(V.tensor_copy(r_ov[:, 16:17], r_inc[:, NE - 1:NE]), "number")
            then(V.tensor_copy(OVI, r_ov), "gates")

            def g_mul(e):
                dve.wait_ge(act_sl, e + 1)
                dve.wait_ge(pe_a3, e + 1)
                after(dve, pe_gt, e)
                V.scalar_tensor_tensor(GU, PS[:, 3, :], GSCALE / WS, SL, ALU.mult, ALU.mult).then_inc(vec_g, 1)

            def x_copy(e, s):
                for half in range(2):
                    dve.wait_ge(act_xt, 2 * e + 1 + half)
                    ks = slice(4 * half, 4 * half + 4)
                    V.tensor_tensor(XT[s][1][:, ks, :], PS[:, half, :].rearrange("p (k n) -> p k n", k=4), XT[s][0][:, ks, :],
                                    ALU.subtract).then_inc(vec_xt, 1)

            def g_copy(e):
                dve.wait_ge(act_gt, e + 1)
                V.tensor_tensor(GUT[1], PS[:, 4, :].rearrange("p (k n) -> p k n", k=KE), GUT[0], ALU.subtract).then_inc(vec_gt, 1)

            def period(e, s, n):
                more = not known_to_be(e, NE - 1)
                if more:
                    make_lo(e + 1, 0, 0)
                    make_lo(e + 1, 0, 1)
                g_mul(e)
                if more:
                    make_lo(e + 1, 1, 0)
                    x_copy(e + 1, 1 - s)
                    make_lo(e + 1, 1, 1)
                if not known_to_be(e, 0):
                    make_lo(e, 2, 0)
                g_copy(e)
                if not known_to_be(e, 0):
                    make_lo(e, 2, 1)

            def block_beyond(e, j):
                for m in range(3):
                    make_lo(e, m, 0)
                    make_lo(e, m, 1)
                x_copy(e, 0)
                g_mul(e)
                g_copy(e)

            experts(dve, lambda: x_copy(0, 0), period, lambda: None)
            beyond(dve, block_beyond)
            v, a = counter("vec_final"), counter("act_final")

            def sums(t0, t1):
                for tt in range(t0, t1):
                    dve.wait_ge(y_in[tt], 32)
                    for k in range(2):
                        V.scalar_tensor_tensor(X[:, tt, :], YG[k][:, tt, :], GATE[:, k, tt:tt + 1], X[:, tt, :], ALU.mult, ALU.add)\
                            .then_inc(*v.mark(*(("sum", tt) if k else ("sum0", tt))))
                        if k == 0:
                            dve.wait_ge(*v.last())

            def results(t0, t1):
                dve.wait_ge(*a.at("r", t0))
                for tt in range(t0, t1):
                    V.scalar_tensor_tensor(XH_OUT[tt], X[:, tt, :], f_r[:, tt:tt + 1], gain_row, ALU.mult, ALU.mult)\
                        .then_inc(*v.mark("out", tt))

            dve.wait_ge(gain_in, 16 * (len(GAINS) + 1))
            sums(*BATCHES[0])
            for b in range(1, len(BATCHES)):
                sums(*BATCHES[b])
                results(*BATCHES[b - 1])
            results(*BATCHES[-1])

        @block.gpsimd
        def _(pool):
            G = nc.gpsimd
            c = counter("pool_const")

            def select(dst, src, pattern, base, ch, op, fill, key):
                G.affine_select(out=dst, in_=src, compare_op=op, fill=fill, base=base, pattern=pattern, channel_multiplier=ch)\
                    .then_inc(*c.mark(*key))

            G.memset(ident, 0.0).then_inc(*c.mark("ident0"))
            G.memset(ones, 1.0).then_inc(*c.mark("ones"))
            G.memset(eps_col, EPS).then_inc(*c.mark("eps"))
            G.memset(lneighth, math.log(0.125)).then_inc(*c.mark("cols"))
            ZERO_ROW = f32(YP_OFF, D)
            G.memset(ZERO_ROW, 0.0).then_inc(*c.mark("zero_row"))
            pool.wait_ge(*c.last())
            select(ident, ident, [[-1, P]], 0, 1, ALU.not_equal, 1.0, ("ident",))
            select(inc_f, ones, [[1, P]], 0, -1, ALU.is_ge, 0.0, ("inc_f",))
            select(inc_b, ones, [[-1, P]], 0, 1, ALU.is_ge, 0.0, ("inc_b",))
            select(st_f, ones, [[1, P]], 0, -1, ALU.is_gt, 0.0, ("st_f",))
            select(st_b, ones, [[-1, P]], 0, 1, ALU.is_gt, 0.0, ("st_b",))
            G.memset(bd64, 0.0).then_inc(*c.mark("bd0"))
            G.memset(gla_bd, 0.0).then_inc(*c.mark("gbd0"))
            G.memset(nmask, 0.0).then_inc(*c.mark("nm0"))
            G.memset(LXP[:, :, 0:2], 0.0).then_inc(*c.mark("pad0"))
            G.memset(LXP[:, :, 2 + T:4 + T], 0.0).then_inc(*c.mark("lxpad"))
            pool.wait_ge(*c.last())
            for s in range(2):
                G.memset(bd64[64 * s:64 * s + 64, 64 * s:64 * s + 64], 1.0).then_inc(*c.mark("bd", s))
                pool.wait_ge(*c.last())
            for h in range(NH):
                G.memset(gla_bd[32 * h:32 * h + 32, 64 * h:64 * h + 64], 1.0).then_inc(*c.mark("gbd", h))
                pool.wait_ge(*c.last())
            for d in range(2):
                for lv in range(7):
                    B = 2 ** lv
                    part = nmask[:, 7 * d + lv, :].rearrange("p (n s b) -> p n s b", s=2, b=B)[:, :, d, :]
                    G.memset(part, -1.0).then_inc(*c.mark("nm", d, lv, 0))
                    pool.wait_ge(*c.last())
                    n = P // (2 * B)
                    select(part, part, [[-2 * B, n], [0, B]], 0 if d else -B, 1, ALU.is_ge, 0.0, ("nm", d, lv, 1))
                    pool.wait_ge(*c.last())
                    select(part, part, [[2 * B, n], [0, B]], B - 1 if d else 2 * B - 1, -1, ALU.is_ge, 0.0, ("nm", d, lv, 2))
            for step in schedule:
                what = step[0]
                if what == "evac":
                    i, g = step[1:]
                    n = gid[i, g]
                    kind = kind_of[n]
                    if kind[0] == "up" and kind[1] != 1:
                        dst = merged[:, kind[2], kind[3] * 512:kind[3] * 512 + 512]
                        pool.wait_ge(*counter("vec_evac").at(n))
                        G.tensor_tensor(dst, dst, SG[2 + (gate_no[n] - 1) % 2], ALU.add).then_inc(*counter("pool_merge").mark(n))
                elif what == "lru_dir":
                    d, t = step[1:]
                    po = counter("pool_lru")
                    if d + t == 0:
                        pool.wait_ge(*c.at("zero_row"))
                        G.dma_start(YROWS[NE * P:, :].rearrange("(b p) d -> p b d", p=P),
                                    bc(ZERO_ROW.unsqueeze(1), P, NOV, D)).then_inc(spare_rows, 16)
                    pool.wait_ge(*counter("act_lru").at("i", d, t))
                    pool.wait_ge(*counter("vec_lru").at("u", t))
                    G.tensor_tensor(LI_, LI_, LU[:, t, :], ALU.mult).then_inc(*po.mark("iu", d, t))
                elif what == "gla_pre":
                    if step[1] == 0:
                        pool.wait_ge(*counter("vec_fin").at("y", 1))
                        pool.wait_ge(*counter("act_lru").at("yhi"))
                        G.memset(QBD, 0.0).then_inc(*counter("pool_gla").mark("qbd0"))
                elif what == "diff_pre":
                    po = counter("pool_diff")
                    pool.wait_ge(*counter("pe_fin").at("tr", "gla", 1))
                    pool.wait_ge(*counter("vec_fin").at("y", 0))
                    G.iota(DWH.bitcast(I32), pattern=[[-1, 1920]], base=896, channel_multiplier=1).then_inc(*po.mark("iota"))
                    for s in range(8):
                        for x in range(2):
                            G.memset(DQZ[s][x], 0.0).then_inc(*po.mark("z", s, x))
                    pool.wait_ge(*po.last())
                elif what == "diff_z":
                    u = step[1]
                    h, qt = divmod(u, TT)
                    po = counter("pool_diff")
                    if u == 0:
                        pool.wait_ge(*counter("vec_evac").at(g_of["dq", 1, 1]))
                    if u >= 2:
                        pool.wait_ge(*counter("pe_diff").at("s", u - 2, 1))
                    if counter("pool_merge").n:
                        pool.wait_ge(*counter("pool_merge").last())
                    for m in range(2):
                        hp = slice(64 * (h % 2) + 32 * m, 64 * (h % 2) + 32 * m + 32)
                        G.tensor_copy(DQZ_BOTH[4 * (u % 2) + 2 * (h % 2) + m][hp, :, :], DQT_BOTH[hp, :, h // 2, qt * P:qt * P + P])\
                            .then_inc(*po.mark(*(("q", u) if m else ("q0", u))))
                        pool.wait_ge(*po.last())
                elif what == "mm" and kind_of[gid[step[1], step[2]]] == ("nk", 0, 0) and step[3] == 0:
                    po = counter("pool_gdnp")
                    pool.wait_ge(*counter("pe_fin").at("tr", "diff", 1))
                    G.memset(RAW[1][:, :, 0:2], 0.0).then_inc(*po.mark("pad0", 1))
                    G.memset(RAW[1][:, :, 2 + T:4 + T], 0.0).then_inc(*po.mark("pad", 1))
                elif what == "mm" and kind_of[gid[step[1], step[2]]] == ("nq", 0, 0) and step[3] == 0:
                    po = counter("pool_gdnp")
                    pool.wait_ge(*counter("pe_diff").at("tr", NH * TT - 1, 1))
                    pool.wait_ge(*counter("vec_diff").at("max", NH * TT - 1, 1))
                    G.memset(RAW[0][:, :, 0:2], 0.0).then_inc(*po.mark("pad0"))
                    G.memset(RAW[0][:, :, 2 + T:4 + T], 0.0).then_inc(*po.mark("pad"))
                    for d in range(2):
                        G.memset(NS[d], 0.0).then_inc(*po.mark(*(("s0",) if d else ("s00",))))
                        G.memset(NKB[d], 0.0).then_inc(*po.mark("kb0", d))
                    pool.wait_ge(*po.last())
                elif what == "gdn_kb":
                    i = step[1]
                    po, q = counter("pool_gdn"), counter("pe_gdn")
                    for d in range(2):
                        c_ = i if d == 0 else TT - 1 - i
                        cs = slice(c_ * P, c_ * P + P)
                        if i == 0:
                            pool.wait_ge(*counter("act_gdnp").at("tm", "nv", 3))
                        else:
                            pool.wait_ge(*q.at("qk", i - 1, d))
                        for t in range(2):
                            for u in range(2):
                                if po.n:
                                    pool.wait_ge(*po.last())
                                if counter("pool_merge").n:
                                    pool.wait_ge(*counter("pool_merge").last())
                                hp = slice(64 * u, 64 * u + 64)
                                G.tensor_copy(NKB[d][hp, 2 * t + u, :], NK[hp, t, cs]).then_inc(*po.mark("kb", i, d, t, u))
                                pool.wait_ge(*po.last())
                elif what == "gdn":
                    i, part = step[1:]
                    po, v, q, a = (counter(f"{e}_gdn") for e in ("pool", "vec", "pe", "act"))
                    for d in range(2):
                        c_ = i if d == 0 else TT - 1 - i
                        cs = slice(c_ * P, c_ * P + P)
                        inc, st = (inc_b, st_b) if d else (inc_f, st_f)
                        if part == 0:
                            if i == 0 and d == 0:
                                pool.wait_ge(*counter("vec_gdnp").at("cd", 1))
                                pool.wait_ge(*counter("act_gdnp").at("tm", "nv", 3))
                            if i:
                                pool.wait_ge(*q.at("y", i - 1, d, 6))
                            G.tensor_tensor(NX[d], over(inc), bc(LAd[:, d, c_, :].unsqueeze(2), P, NH, P), ALU.mult)\
                                .then_inc(*po.mark("tla", i, d))
                    for d in range(2):
                        c_ = i if d == 0 else TT - 1 - i
                        inc = inc_b if d else inc_f
                        if part == 0:
                            if i:
                                pool.wait_ge(*q.at("v", i - 1, d))
                            G.tensor_copy(NWK[d].rearrange("p t (u n) -> p (t u) n", u=2), heads(LAd[:, d, c_, :]))\
                                .then_inc(*po.mark("lab", i, d))
                            pool.wait_ge(*a.at("dt", i, d))
                            if i:
                                pool.wait_ge(*q.at("o", i - 1, d))
                            G.tensor_tensor(NQT[d], NY[d], over(inc), ALU.mult).then_inc(*po.mark("dts", i, d))
                        elif part == 1:
                            pool.wait_ge(*v.at("lt", i, d))
                            G.tensor_tensor(NZ_[d], NLT[d], over(nmask[:, 7 * (1 - d), :]), ALU.mult).then_inc(*po.mark("z0", i, d))
                            pool.wait_ge(*po.last())
                            G.tensor_tensor(NZ_[d], NZ_[d], over(ident), ALU.add).then_inc(*po.mark("z", i, d))
                        elif part == 2:
                            if i:
                                pool.wait_ge(*v.at("state", i - 1, d))
                            k4 = NKT[:, c_, :].rearrange("p (h n) -> p h n", h=NH)
                            G.tensor_tensor(NKE[d].rearrange("p t (u n) -> p (t u) n", u=2), k4, heads(EG[:, 0, d, c_, :]), ALU.mult)\
                                .then_inc(*po.mark("ke", i, d))
                            G.tensor_tensor(NKD[d].rearrange("p t (u n) -> p (t u) n", u=2), k4, heads(EG[:, 1, d, c_, :]), ALU.mult)\
                                .then_inc(*po.mark("kd", i, d))
                elif what == "norm_stats" and step[1] == "x2":
                    po = counter("pool_route")
                    pool.wait_ge(*counter("pool_merge").at(g_of["up", 3, KT - 1, 1]))
                    pool.wait_ge(*pe_mm.at(LAST_MM))
                    for o_, n, b_, ch in ((0, 32, 32, 0), (32, 32, 0, 0), (64, 16, 0, 0)):
                        G.iota(K_INT[:, o_:o_ + n], pattern=[[-1 if b_ else 1, n]], base=b_, channel_multiplier=ch)\
                            .then_inc(*po.mark("iota", o_))
                    G.iota(K_INT[:, 80:88], pattern=[[P, TT]], base=0, channel_multiplier=1).then_inc(*po.mark("iota_tok"))
                    G.iota(K2_INT[:, 0:NBLK + 1], pattern=[[P, NBLK + 1]], base=0, channel_multiplier=0).then_inc(*po.mark("iota_blk"))
                    G.iota(K2_INT[:, NBLK + 1:NBLK + 1 + P], pattern=[[1, P]], base=-P, channel_multiplier=0).then_inc(*po.mark("iota"))
            v = counter("vec_route")
            for s in range(4):
                pool.wait_ge(xhat_out[s], 16 * TT // 4)
            pool.wait_ge(*v.at("index"))
            for e in range(NE):
                after(pool, pe_xt, 2 * (e - 1))
                G.indirect_dma_start(XR[e % 2], None, XH_D, bass.IndirectOffsetOnAxis(IDX[:, e:e + 1], 0)).then_inc(rows_in[e % 2], 16)

            pool.wait_ge(*v.at("gates"))
            number = pool.value_load(OVI[0:1, 16:17], min_val=0, max_val=NOV)
            pool.wait_ge(y_out[1], 16 * NE // 2)
            pool.wait_ge(y_out[0], 16 * NE // 2)
            with pool.If(number > 0):
                for j in range(NOV):
                    with pool.If(number > j):
                        G.indirect_dma_start(XR[0], None, XH_D, bass.IndirectOffsetOnAxis(IDX[:, NE + j:NE + j + 1], 0)).then_inc(rows_in[0], 16)
                        pool.wait_ge(y_out[0], 16 * NE // 2 + 16 * (j + 1))
            for tt in range(TT):
                for k in range(2):
                    G.indirect_dma_start(YG[k][:, tt, :], None, YROWS, bass.IndirectOffsetOnAxis(SLOTU[:, k * TT + tt:k * TT + tt + 1], 0))\
                        .then_inc(y_in[tt], 16)
    return {n: k.found for n, k in counters.items()}


def pack_small(inputs, np):
    cols = np.zeros((P, NCOLS), np.float32)
    cols[:, C_MERGEB:C_MERGEB + 32] = inputs["merge_b"][0].reshape(4 * KT, P).T
    cols[:, C_LRB:C_LRB + 2] = inputs["gla_lr_bias"][0].T
    cols[:, C_LCW:C_LCW + 8] = inputs["lru_conv_w"][0].reshape(4, 2, P).transpose(2, 1, 0).reshape(P, 8)
    cols[:, C_LCB:C_LCB + 2] = inputs["lru_conv_b"][0].reshape(2, P).T
    cols[:, C_LBA:C_LBA + 4] = inputs["lru_b_a"][0].reshape(4, P).T
    cols[:, C_LBX:C_LBX + 4] = inputs["lru_b_x"][0].reshape(4, P).T
    cols[:, C_LAM:C_LAM + 4] = inputs["lru_lambda"][0].reshape(4, P).T
    cols[:, C_GCW:C_GCW + 24] = inputs["gdn_conv_w"][0].reshape(4, 6, P).transpose(2, 1, 0).reshape(P, 24)
    rows = np.concatenate([
        inputs["gla_norm"][0], inputs["diff_norm"][0], inputs["gdn_norm"][0], inputs["gdn_a_log"][0].ravel(),
        inputs["gdn_dt_bias"][0].ravel(), inputs["diff_lq1"][0], inputs["diff_lk1"][0], inputs["diff_lq2"][0],
        inputs["diff_lk2"][0], inputs["moe_b_group"][0], inputs["moe_b_expert"][0]])
    lru_w = np.zeros((P, 8, P), np.float32)
    for d in range(2):
        for gate, name in enumerate(("lru_w_a", "lru_w_x")):
            for b in range(4):
                s = slice(64 * (b % 2), 64 * (b % 2) + 64)
                lru_w[s, 4 * d + 2 * gate + b // 2, s] = inputs[name][0, d, b]
    lr_up = np.zeros((32, 256), np.float32)
    for d in range(2):
        lr_up[16 * d:16 * d + 16, P * d:P * d + P] = inputs["gla_lr_up"][0, d]
    router_w = np.concatenate([inputs["moe_w_group"][0], inputs["moe_w_expert"][0]], axis=1)
    gains = np.stack([inputs["mix_norm"][0], inputs["mem_norm"][0], inputs["xattn_norm"][0], inputs["moe_norm"][0], inputs["final_norm"]])
    return {"cols": cols, "rows": rows, "lru_w": lru_w, "lr_up": lr_up, "gains": gains, "router_w": router_w}


def kernel(**inputs):
    import numpy as np
    import concourse.bacc as _bacc
    from concourse.bass_utils import run_bass_kernel_spmd as _run

    inputs = {n: np.asarray(v) for n, v in inputs.items()}
    arrays = pack_small(inputs, np)
    for n in ("x", "mem", "w_in", "merge_w", "branch_up", "mix_out", "xattn_wkv", "xattn_wq", "xattn_wo"):
        arrays[n] = inputs[n][0]
    for n in ("w1", "w3", "w2"):
        arrays[n] = inputs["moe_" + n][0]
    arrays = {f"in_{n}_dram": np.ascontiguousarray(v) for n, v in arrays.items()}

    def program(known):
        nc = _bacc.Bacc("TRN2", target_bir_lowering=False, num_devices=1)
        A = {n[3:-5]: nc.dram_tensor(n, v.shape, mybir.dt.from_np(v.dtype), kind="ExternalInput").ap()
             for n, v in arrays.items()}
        out = nc.dram_tensor("out_0_dram", (1, T, D), F32, kind="ExternalOutput").ap()
        A["xhat"] = nc.dram_tensor("xhat", (T, D), F32, kind="Internal").ap()
        A["yrows"] = nc.dram_tensor("yrows", (NBLK * P, D), F32, kind="Internal").ap()
        return nc, build(nc, A, out[0], known)

    known = program(None)[1]
    nc, _ = program(known)
    return _run(nc, [arrays], core_ids=[0]).results[0]["out_0_dram"]
```
